# Optimizing a Trainium2 kernel written in Bass

```python
import math
import jax, jax.numpy as jnp
from jax import lax
import numpy as np

D_MODEL = 1024
BATCH = 1
SEQ = 1024
DEPTH = 2

RG_WIDTH = D_MODEL // 2
RG_BLOCKS = 8
RG_BLOCK = RG_WIDTH // RG_BLOCKS
CONV_WIDTH = 4
RG_C = 8.0
GLA_HEADS = 4
GLA_VDIM = D_MODEL // 2
GLA_KDIM = GLA_VDIM // 2
GLA_HK = GLA_KDIM // GLA_HEADS
GLA_HV = GLA_VDIM // GLA_HEADS
GLA_LOWRANK = 16
GLA_GATE_TAU = 16.0
GLA_CHUNK = 64
EVEN_IN = 2 * RG_WIDTH + 2 * GLA_KDIM + 2 * GLA_VDIM + GLA_LOWRANK
MIX_WIDTH = RG_WIDTH + GLA_VDIM

FOX_HEADS = 16
FOX_HD = D_MODEL // FOX_HEADS
FOX_BLOCK = 128
ODD_IN = 4 * D_MODEL + FOX_HEADS

D_FF = 4 * D_MODEL
N_EVEN = (DEPTH + 1) // 2
N_ODD = DEPTH // 2
ALPHA = (2 * DEPTH) ** 0.25
BETA = (8 * DEPTH) ** -0.25
LN_EPS = 1e-5
RMS_EPS = 1e-6


def layer_norm(x, g, b):
    xf = x.astype(jnp.float32)
    mu = jnp.mean(xf, axis=-1, keepdims=True)
    var = jnp.mean(jnp.square(xf - mu), axis=-1, keepdims=True)
    return ((xf - mu) * lax.rsqrt(var + LN_EPS) * g.astype(jnp.float32)
            + b.astype(jnp.float32)).astype(x.dtype)

def rms_norm(x, g):
    xf = x.astype(jnp.float32)
    y = xf * lax.rsqrt(jnp.mean(xf * xf, axis=-1, keepdims=True) + RMS_EPS)
    return (y * g.astype(jnp.float32)).astype(x.dtype)

def ada_mod(c, w, b):
    m = (jax.nn.silu(c) @ w + b)[:, None, :]
    shift, scale, gate = jnp.split(m, 3, axis=-1)
    return shift, scale, 1.0 + gate

def causal_dwconv(x, w, b):
    k_len, ch = w.shape
    y = lax.conv_general_dilated(
        x, w[:, None, :].astype(x.dtype), window_strides=(1,),
        padding=[(k_len - 1, 0)], dimension_numbers=('NWC', 'WIO', 'NWC'),
        feature_group_count=ch)
    return y + b

def rg_lru(x, w_a, b_a, w_x, b_x, lam):
    bn, sn, _ = x.shape
    xf = x.astype(jnp.float32)
    xb = xf.reshape(bn, sn, RG_BLOCKS, RG_BLOCK)
    r = jax.nn.sigmoid(jnp.einsum('bsni,nij->bsnj', xb, w_a.astype(jnp.float32)).reshape(bn, sn, RG_WIDTH) + b_a)
    i = jax.nn.sigmoid(jnp.einsum('bsni,nij->bsnj', xb, w_x.astype(jnp.float32)).reshape(bn, sn, RG_WIDTH) + b_x)
    log_a = RG_C * r * jax.nn.log_sigmoid(lam.astype(jnp.float32))
    a = jnp.exp(log_a)
    u = jnp.sqrt(-jnp.expm1(2.0 * log_a)) * (i * xf)

    def combine(left, right):
        a1, h1 = left
        a2, h2 = right
        return a1 * a2, a2 * h1 + h2

    _, h = lax.associative_scan(combine, (a, u), axis=1)
    return h.astype(x.dtype)

def gla_chunked(q, k, v, log_alpha):
    bn, sn, nh, dk = q.shape
    dv = v.shape[-1]
    n_chunks = sn // GLA_CHUNK

    def blocks(t):
        return t.astype(jnp.float32).reshape(bn, n_chunks, GLA_CHUNK, nh, t.shape[-1]).transpose(1, 0, 3, 2, 4)

    qc = blocks(q) * (dk ** -0.5)
    kc = blocks(k)
    vc = blocks(v)
    bcum = jnp.cumsum(blocks(log_alpha), axis=3)
    b_last = bcum[:, :, :, -1:, :]
    q_dec = qc * jnp.exp(bcum)
    k_dec = kc * jnp.exp(-bcum)
    k_end = kc * jnp.exp(b_last - bcum)
    causal = jnp.tril(jnp.ones((GLA_CHUNK, GLA_CHUNK), dtype=bool))
    att = jnp.where(causal, jnp.einsum('nbhtd,nbhsd->nbhts', q_dec, k_dec), 0.0)
    o_intra = jnp.einsum('nbhts,nbhsv->nbhtv', att, vc)
    kv = jnp.einsum('nbhsd,nbhsv->nbhdv', k_end, vc)
    decay = jnp.exp(b_last[:, :, :, 0, :])

    def step(state, inp):
        dcy, kv_n = inp
        return dcy[..., None] * state + kv_n, state

    _, s_prev = lax.scan(step, jnp.zeros((bn, nh, dk, dv), jnp.float32), (decay, kv))
    o = o_intra + jnp.einsum('nbhtd,nbhdv->nbhtv', q_dec, s_prev)
    return o.transpose(1, 0, 3, 2, 4).reshape(bn, sn, nh, dv).astype(q.dtype)

def even_mixer(u, w_in, conv_w, conv_b, rg_wa, rg_ba, rg_wx, rg_bx, rg_lam,
               gla_w_up, gla_b_up, gla_norm_g, w_out):
    bn, sn, _ = u.shape
    proj = u @ w_in
    s1 = RG_WIDTH
    s2 = s1 + RG_WIDTH
    s3 = s2 + GLA_KDIM
    s4 = s3 + GLA_KDIM
    s5 = s4 + GLA_VDIM
    s6 = s5 + GLA_VDIM
    xr, yr, q, k, v, g, zl = jnp.split(proj, [s1, s2, s3, s4, s5, s6], axis=-1)
    h = rg_lru(causal_dwconv(xr, conv_w, conv_b), rg_wa, rg_ba, rg_wx, rg_bx, rg_lam)
    rg_out = h * jax.nn.gelu(yr)
    log_alpha = jax.nn.log_sigmoid((zl @ gla_w_up + gla_b_up).astype(jnp.float32)) / GLA_GATE_TAU
    o = gla_chunked(q.reshape(bn, sn, GLA_HEADS, GLA_HK),
                    k.reshape(bn, sn, GLA_HEADS, GLA_HK),
                    v.reshape(bn, sn, GLA_HEADS, GLA_HV),
                    log_alpha.reshape(bn, sn, GLA_HEADS, GLA_HK))
    o = rms_norm(o, gla_norm_g.reshape(GLA_HEADS, GLA_HV)) * jax.nn.silu(g).reshape(bn, sn, GLA_HEADS, GLA_HV)
    mix = jnp.concatenate([rg_out, o.reshape(bn, sn, GLA_VDIM)], axis=-1)
    return mix @ w_out

def fox_attention(u, w_in, b_f, q_norm_g, k_norm_g, w_out):
    bn, sn, _ = u.shape
    proj = u @ w_in
    q, k, v, g, fl = jnp.split(proj, [D_MODEL, 2 * D_MODEL, 3 * D_MODEL, 4 * D_MODEL], axis=-1)
    q = rms_norm(q.reshape(bn, sn, FOX_HEADS, FOX_HD), q_norm_g).transpose(0, 2, 1, 3) * (FOX_HD ** -0.5)
    k = rms_norm(k.reshape(bn, sn, FOX_HEADS, FOX_HD), k_norm_g).transpose(0, 2, 1, 3)
    v = v.reshape(bn, sn, FOX_HEADS, FOX_HD).transpose(0, 2, 1, 3)
    log_f = jax.nn.log_sigmoid((fl + b_f).astype(jnp.float32))
    f_cum = jnp.cumsum(log_f, axis=1).transpose(0, 2, 1)
    outs = []
    for blk in range(sn // FOX_BLOCK):
        t0 = blk * FOX_BLOCK
        t1 = t0 + FOX_BLOCK
        s = jnp.einsum('bhtd,bhsd->bhts', q[:, :, t0:t1], k[:, :, :t1]).astype(jnp.float32)
        s = s + f_cum[:, :, t0:t1, None] - f_cum[:, :, None, :t1]
        mask = (t0 + jnp.arange(FOX_BLOCK))[:, None] >= jnp.arange(t1)[None, :]
        p = jax.nn.softmax(jnp.where(mask, s, -jnp.inf), axis=-1)
        outs.append(jnp.einsum('bhts,bhsd->bhtd', p.astype(v.dtype), v[:, :, :t1]))
    o = jnp.concatenate(outs, axis=2).transpose(0, 2, 1, 3).reshape(bn, sn, D_MODEL)
    return (o * jax.nn.sigmoid(g)) @ w_out

def first_inputs(seed: int = 0) -> dict:
    key = jax.random.key(seed)
    ks = jax.random.split(key, 32)
    D = D_MODEL

    def nrm(i, shape, scale):
        return scale * jax.random.normal(ks[i], shape, jnp.float32)

    lam_a = jax.random.uniform(ks[13], (N_EVEN, RG_WIDTH), jnp.float32, 0.9, 0.999)
    lam_root = lam_a ** (1.0 / RG_C)
    ev_lam = jnp.log(lam_root) - jnp.log1p(-lam_root)
    return {
        "x": nrm(0, (BATCH, SEQ, D), 1.0),
        "c": nrm(1, (BATCH, D), 1.0),
        "ada_w": nrm(2, (DEPTH, 2, D, 3 * D), 0.1 * D ** -0.5),
        "ada_b": nrm(3, (DEPTH, 2, 3 * D), 0.02),
        "ln_g": 1.0 + nrm(4, (DEPTH, 2, D), 0.05),
        "ln_b": nrm(5, (DEPTH, 2, D), 0.02),
        "ev_w_in": nrm(6, (N_EVEN, D, EVEN_IN), D ** -0.5),
        "ev_conv_w": nrm(7, (N_EVEN, CONV_WIDTH, RG_WIDTH), CONV_WIDTH ** -0.5),
        "ev_conv_b": nrm(8, (N_EVEN, RG_WIDTH), 0.02),
        "ev_rg_wa": nrm(9, (N_EVEN, RG_BLOCKS, RG_BLOCK, RG_BLOCK), RG_BLOCK ** -0.5),
        "ev_rg_ba": nrm(10, (N_EVEN, RG_WIDTH), 0.02),
        "ev_rg_wx": nrm(11, (N_EVEN, RG_BLOCKS, RG_BLOCK, RG_BLOCK), RG_BLOCK ** -0.5),
        "ev_rg_bx": nrm(12, (N_EVEN, RG_WIDTH), 0.02),
        "ev_rg_lam": ev_lam,
        "ev_gla_w_up": nrm(14, (N_EVEN, GLA_LOWRANK, GLA_KDIM), GLA_LOWRANK ** -0.5),
        "ev_gla_b_up": nrm(15, (N_EVEN, GLA_KDIM), 0.02),
        "ev_gla_norm_g": 1.0 + nrm(16, (N_EVEN, GLA_VDIM), 0.05),
        "ev_w_out": nrm(17, (N_EVEN, MIX_WIDTH, D), BETA * MIX_WIDTH ** -0.5),
        "od_w_in": nrm(18, (N_ODD, D, ODD_IN), D ** -0.5),
        "od_b_f": 3.0 + 3.0 * jax.random.uniform(ks[19], (N_ODD, FOX_HEADS), jnp.float32),
        "od_q_norm_g": 1.0 + nrm(20, (N_ODD, FOX_HD), 0.05),
        "od_k_norm_g": 1.0 + nrm(21, (N_ODD, FOX_HD), 0.05),
        "od_w_out": nrm(22, (N_ODD, D, D), BETA * D ** -0.5),
        "mlp_w1": nrm(23, (DEPTH, D, D_FF), D ** -0.5),
        "mlp_b1": nrm(24, (DEPTH, D_FF), 0.02),
        "mlp_w2": nrm(25, (DEPTH, D_FF, D), BETA * D_FF ** -0.5),
        "mlp_b2": nrm(26, (DEPTH, D), 0.02),
    }

def first_block(x, c, ada_w, ada_b, ln_g, ln_b,
              ev_w_in, ev_conv_w, ev_conv_b, ev_rg_wa, ev_rg_ba, ev_rg_wx, ev_rg_bx, ev_rg_lam,
              ev_gla_w_up, ev_gla_b_up, ev_gla_norm_g, ev_w_out,
              od_w_in, od_b_f, od_q_norm_g, od_k_norm_g, od_w_out,
              mlp_w1, mlp_b1, mlp_w2, mlp_b2):
    for layer in range(DEPTH):
        shift, scale, gate = ada_mod(c, ada_w[layer, 0], ada_b[layer, 0])
        u = x * (1.0 + scale) + shift
        if layer % 2 == 0:
            e = layer // 2
            y = even_mixer(u, ev_w_in[e], ev_conv_w[e], ev_conv_b[e], ev_rg_wa[e], ev_rg_ba[e],
                           ev_rg_wx[e], ev_rg_bx[e], ev_rg_lam[e], ev_gla_w_up[e], ev_gla_b_up[e],
                           ev_gla_norm_g[e], ev_w_out[e])
        else:
            o = layer // 2
            y = fox_attention(u, od_w_in[o], od_b_f[o], od_q_norm_g[o], od_k_norm_g[o], od_w_out[o])
        x = layer_norm(ALPHA * x + gate * y, ln_g[layer, 0], ln_b[layer, 0])
        shift, scale, gate = ada_mod(c, ada_w[layer, 1], ada_b[layer, 1])
        u = x * (1.0 + scale) + shift
        y = jnp.square(jax.nn.relu(u @ mlp_w1[layer] + mlp_b1[layer])) @ mlp_w2[layer] + mlp_b2[layer]
        x = layer_norm(ALPHA * x + gate * y, ln_g[layer, 1], ln_b[layer, 1])
    return x


DEPTH_2 = 1

D_MIX = D_MODEL
D_A = D_MIX // 2
D_B = D_MIX - D_A
HEADS_A = 4
HEAD_DIM_A = D_A // HEADS_A
HEADS_B = 8
CHUNK = 128
CONV_B_WIDTH = 31
D_FF_2 = 2816
CONV_F_WIDTH = 3
D_IN = 2 * D_A + 2 * D_B
DEEPNORM_ALPHA = (2.0 * DEPTH_2) ** 0.25
DEEPNORM_BETA = (8.0 * DEPTH_2) ** -0.25


def _layernorm(x, g, b):
    xf = x.astype(jnp.float32)
    mu = jnp.mean(xf, axis=-1, keepdims=True)
    var = jnp.mean(jnp.square(xf - mu), axis=-1, keepdims=True)
    y = (xf - mu) * lax.rsqrt(var + LN_EPS)
    return (y * g.astype(jnp.float32) + b.astype(jnp.float32)).astype(x.dtype)

def _causal_depthwise_conv(x, w, b):
    k = w.shape[0]
    y = lax.conv_general_dilated(
        x, w[:, None, :].astype(x.dtype), window_strides=(1,),
        padding=[(k - 1, 0)], dimension_numbers=("NWC", "WIO", "NWC"),
        feature_group_count=x.shape[-1])
    return y + b

def second_inputs(seed: int = 0) -> dict:
    key = jax.random.key(seed)
    ks = jax.random.split(key, 24)
    f32 = jnp.float32
    nrm = lambda k, shape, s: jax.random.normal(k, shape, f32) * s
    gain = lambda k, shape: 1.0 + nrm(k, shape, 0.02)
    return {
        "x": jax.random.normal(ks[0], (BATCH, SEQ, D_MODEL), f32),
        "w_in": nrm(ks[1], (D_MODEL, D_IN), D_MODEL ** -0.5),
        "b_in": nrm(ks[2], (D_IN,), 0.02),
        "ln_a_g": gain(ks[3], (HEADS_A, HEAD_DIM_A)),
        "ln_a_b": nrm(ks[4], (HEADS_A, HEAD_DIM_A), 0.02),
        "w_spatial": nrm(ks[5], (HEADS_A, CHUNK, CHUNK), CHUNK ** -0.5),
        "b_spatial": gain(ks[6], (HEADS_A, CHUNK)),
        "conv_b_w": nrm(ks[7], (CONV_B_WIDTH, D_B), CONV_B_WIDTH ** -0.5),
        "conv_b_b": nrm(ks[8], (D_B,), 0.02),
        "ln_b_g": gain(ks[9], (D_B,)),
        "ln_b_b": nrm(ks[10], (D_B,), 0.02),
        "w_out": nrm(ks[11], (D_MIX, D_MODEL), D_MIX ** -0.5 * DEEPNORM_BETA),
        "b_out": nrm(ks[12], (D_MODEL,), 0.02),
        "ln1_g": gain(ks[13], (D_MODEL,)),
        "ln1_b": nrm(ks[14], (D_MODEL,), 0.02),
        "w_up": nrm(ks[15], (D_MODEL, 2 * D_FF_2), D_MODEL ** -0.5),
        "conv_f_w": nrm(ks[16], (CONV_F_WIDTH, 2 * D_FF_2), CONV_F_WIDTH ** -0.5),
        "conv_f_b": nrm(ks[17], (2 * D_FF_2,), 0.02),
        "w_down": nrm(ks[18], (D_FF_2, D_MODEL), D_FF_2 ** -0.5 * DEEPNORM_BETA),
        "ln2_g": gain(ks[19], (D_MODEL,)),
        "ln2_b": nrm(ks[20], (D_MODEL,), 0.02),
    }

def _token_mixing(x, w_in, b_in, ln_a_g, ln_a_b, w_spatial, b_spatial,
                  conv_b_w, conv_b_b, ln_b_g, ln_b_b, w_out, b_out):
    bsz, seq, _ = x.shape
    n_chunks = seq // CHUNK
    h = x @ w_in + b_in
    za, zb = h[..., :2 * D_A], h[..., 2 * D_A:]

    za = jax.nn.gelu(za, approximate=False)
    u, v = za[..., :D_A], za[..., D_A:]
    v = _layernorm(v.reshape(bsz, seq, HEADS_A, HEAD_DIM_A), ln_a_g, ln_a_b)
    v = v.reshape(bsz, n_chunks, CHUNK, HEADS_A, HEAD_DIM_A)
    causal = jnp.tril(jnp.ones((CHUNK, CHUNK), dtype=w_spatial.dtype))
    ws = w_spatial * causal
    sv = jnp.einsum("hts,bcshd->bcthd", ws, v) + b_spatial.T[None, None, :, :, None]
    y_a = u * sv.reshape(bsz, seq, D_A)

    a_b, g_b = zb[..., :D_B], zb[..., D_B:]
    yb = a_b * jax.nn.sigmoid(g_b)
    yb = _causal_depthwise_conv(yb, conv_b_w, conv_b_b)
    y_b = jax.nn.silu(_layernorm(yb, ln_b_g, ln_b_b))

    y = jnp.concatenate([y_a, y_b], axis=-1)
    return y @ w_out + b_out

def _conv_ffn(x, w_up, conv_f_w, conv_f_b, w_down):
    h = _causal_depthwise_conv(x @ w_up, conv_f_w, conv_f_b)
    gate, val = h[..., :D_FF_2], h[..., D_FF_2:]
    return (jax.nn.silu(gate) * val) @ w_down

def second_block(x, w_in, b_in, ln_a_g, ln_a_b, w_spatial, b_spatial, conv_b_w, conv_b_b,
              ln_b_g, ln_b_b, w_out, b_out, ln1_g, ln1_b, w_up, conv_f_w, conv_f_b,
              w_down, ln2_g, ln2_b):
    for _ in range(DEPTH_2):
        mix = _token_mixing(x, w_in, b_in, ln_a_g, ln_a_b, w_spatial, b_spatial,
                            conv_b_w, conv_b_b, ln_b_g, ln_b_b, w_out, b_out)
        x = _layernorm(DEEPNORM_ALPHA * x + mix, ln1_g, ln1_b)
        ffn = _conv_ffn(x, w_up, conv_f_w, conv_f_b, w_down)
        x = _layernorm(DEEPNORM_ALPHA * x + ffn, ln2_g, ln2_b)
    return x


_first_inputs = second_inputs


def second_inputs(seed=0):
    import zlib

    import numpy as np

    out = dict(_first_inputs(seed))
    spreads = {}
    factors = {'b_in': 6.759,
     'ln_a_g': 8.0,
     'ln_a_b': 8.0,
     'b_spatial': 8.0,
     'conv_b_b': 7.041,
     'ln_b_g': 8.0,
     'ln_b_b': 8.0,
     'b_out': 3.441,
     'ln1_b': 2.753,
     'conv_f_b': 7.042,
     'ln2_g': 2.835,
     'ln2_b': 2.95}
    for name, (base, spread) in spreads.items():
        noise = np.random.default_rng([zlib.crc32(name.encode()), seed]).standard_normal(out[name].shape)
        drawn = base * np.exp(spread * noise) if base else spread * noise
        out[name] = __import__('jax').numpy.asarray(drawn.astype(out[name].dtype))
    for name, factor in factors.items():
        out[name] = (out[name] * factor).astype(out[name].dtype)
    return out


_narrow_inputs = second_inputs


def second_inputs(seed=0):

    out = dict(_narrow_inputs(seed))
    wider = {'ln_a_g': 8.09,
     'ln_a_b': 8.6,
     'b_spatial': 5.33,
     'ln_b_g': 4.86,
     'ln_b_b': 4.64,
     'b_out': 3.39,
     'ln2_g': 3.15,
     'ln2_b': 3.19}
    for name, times in wider.items():
        mean = out[name].mean()
        out[name] = (mean + times * (out[name] - mean)).astype(out[name].dtype)
    return out


def setup_inputs(seed=0):
    out = dict(first_inputs(seed))
    for name, value in second_inputs(seed + 1).items():
        if name != "x":
            out[name + "_2"] = value
    return out


def reference(
    x, c, ada_w, ada_b, ln_g, ln_b, ev_w_in, ev_conv_w, ev_conv_b, ev_rg_wa, ev_rg_ba, ev_rg_wx,
    ev_rg_bx, ev_rg_lam, ev_gla_w_up, ev_gla_b_up, ev_gla_norm_g, ev_w_out, od_w_in, od_b_f,
    od_q_norm_g, od_k_norm_g, od_w_out, mlp_w1, mlp_b1, mlp_w2, mlp_b2, w_in_2, b_in_2,
    ln_a_g_2, ln_a_b_2, w_spatial_2, b_spatial_2, conv_b_w_2, conv_b_b_2, ln_b_g_2, ln_b_b_2,
    w_out_2, b_out_2, ln1_g_2, ln1_b_2, w_up_2, conv_f_w_2, conv_f_b_2, w_down_2, ln2_g_2,
    ln2_b_2,
):
    x = first_block(
        x, c, ada_w, ada_b, ln_g, ln_b, ev_w_in, ev_conv_w, ev_conv_b, ev_rg_wa, ev_rg_ba,
        ev_rg_wx, ev_rg_bx, ev_rg_lam, ev_gla_w_up, ev_gla_b_up, ev_gla_norm_g, ev_w_out,
        od_w_in, od_b_f, od_q_norm_g, od_k_norm_g, od_w_out, mlp_w1, mlp_b1, mlp_w2, mlp_b2,
    )
    return second_block(
        x, w_in_2, b_in_2, ln_a_g_2, ln_a_b_2, w_spatial_2, b_spatial_2, conv_b_w_2, conv_b_b_2,
        ln_b_g_2, ln_b_b_2, w_out_2, b_out_2, ln1_g_2, ln1_b_2, w_up_2, conv_f_w_2, conv_f_b_2,
        w_down_2, ln2_g_2, ln2_b_2,
    )


_drawn_inputs = setup_inputs


def setup_inputs(seed=0):
    import zlib

    import numpy as np

    out = dict(_drawn_inputs(seed))
    spreads = {}
    factors = {'ev_conv_b': 2.803,
     'ev_rg_ba': 44.453,
     'ev_rg_bx': 31.743,
     'ev_gla_w_up': 2.748,
     'ev_gla_b_up': 8.0,
     'ev_gla_norm_g': 6.141,
     'od_b_f': 32.28,
     'od_q_norm_g': 8.0,
     'od_k_norm_g': 8.0,
     'mlp_b1': 3.722,
     'mlp_b2': 2.675,
     'ln1_g_2': 2.69}
    for name, (base, spread) in spreads.items():
        noise = np.random.default_rng([zlib.crc32(name.encode()), seed]).standard_normal(out[name].shape)
        drawn = base * np.exp(spread * noise) if base else spread * noise
        out[name] = __import__('jax').numpy.asarray(drawn.astype(out[name].dtype))
    for name, factor in factors.items():
        out[name] = (out[name] * factor).astype(out[name].dtype)
    return out
```

```python
from contextlib import ExitStack, contextmanager

import numpy as np

import concourse.bass as bass
from concourse import mybir

F32 = mybir.dt.float32
F32R = mybir.dt.float32r
ALU = mybir.AluOpType
ACT = mybir.ActivationFunctionType

P = 128
D = 1024
SEQ = 1024
HALF = 512
NK = D // P
NT = SEQ // P
ALPHA_1 = 4.0 ** 0.25
ALPHA_2 = 2.0 ** 0.25
LN_EPS = 1e-5
RMS_EPS = 1e-6
D_FF = 4096
FF_GROUP = 256
D_FF2 = 2816
RG = 512
GLA_CHUNK = 64
NEG = -1e30
NA, ND = 2, 4
CONV_B = 31
CONV_PAD = CONV_B - 1


class Tally:

    def __init__(self, eng, sem, start=0):
        self.eng, self.sem, self.n, self.it, self.per, self.j = eng, sem, start, None, 0, 0

    def enter(self, it, per):
        self.it, self.per, self.j = it, per, 0

    def leave(self, count):
        assert self.j == self.per, (self.sem, self.j, self.per)
        self.n += count * self.per
        self.it, self.j = None, 0

    def wait_at(self, k):
        v = self.n + self.j + k
        if self.it is None:
            if v > 0:
                self.eng.wait_ge(self.sem, v)
        elif self.per == 0:
            if v > 0:
                self.eng.wait_ge(self.sem, v)
        else:
            assert v > 0, (self.sem, v)
            self.eng.wait_ge(self.sem, self.it * self.per + v)

    def skip(self, k=1):
        self.j += k
        if self.it is None:
            self.n, self.j = self.n + self.j, 0

    def take(self, k=1):
        self.skip(k)
        self.wait_at(0)


class Chain:

    def __init__(self, eng, sem):
        self.t = Tally(eng, sem)

    def done(self, ins):
        ins.then_inc(self.t.sem, 1)
        self.t.take()


@contextmanager
def rounds(eng, count, *pairs):
    with eng.Fori(0, count) as it:
        for t, per in pairs:
            (t.t if isinstance(t, Chain) else t).enter(it, per)
        yield it
        for t, per in pairs:
            (t.t if isinstance(t, Chain) else t).leave(count)


def param_rows(A):
    r = lambda ap: ap.rearrange("(r q) -> r q", q=P)
    out = {}
    out["c"] = r(A["c"].rearrange("a d -> (a d)"))
    out["ada_b"] = r(A["ada_b"].rearrange("l j n -> (l j n)"))
    out["ln_g"] = r(A["ln_g"].rearrange("l j n -> (l j n)"))
    out["ln_b"] = r(A["ln_b"].rearrange("l j n -> (l j n)"))
    for n in ("ev_conv_b", "ev_rg_ba", "ev_rg_bx", "ev_rg_lam", "ev_gla_b_up", "ev_gla_norm_g", "mlp_b1", "mlp_b2"):
        out[n] = r(A[n].rearrange("l n -> (l n)"))
    out["ev_conv_w"] = r(A["ev_conv_w"].rearrange("l t n -> (l t n)"))
    for n in ("b_in_2", "conv_b_b_2", "ln_b_g_2", "ln_b_b_2", "b_out_2", "ln1_g_2", "ln1_b_2", "ln2_g_2",
              "ln2_b_2", "conv_f_b_2"):
        out[n] = r(A[n])
    out["conv_b_w_2"] = r(A["conv_b_w_2"].rearrange("t n -> (t n)"))
    out["conv_f_w_2"] = r(A["conv_f_w_2"].rearrange("t n -> (t n)"))
    return out


class Plan:

    def __init__(self):
        self.phases, self.order = {}, []
        self.items = self.tiles = 0
        self.slot_need = {}
        self.raw_last = {}

    def add(self, name, count, tiles, items):
        ph = dict(name=name, count=count, tiles=tiles, items=items, I=self.items, W=self.tiles)
        T = len(tiles)
        free, raws = [], []
        last_by_slot = {}
        for j, (_, last, slot) in enumerate(tiles):
            before = self.slot_need.get(slot, 0) - self.items
            if slot in last_by_slot:
                free.append(last_by_slot[slot] + 1)
            else:
                own = [l for _, l, s in tiles if s == slot][-1]
                free.append(max(before, own + 1 - items) if count > 1 else before)
            last_by_slot[slot] = last
        for j in range(T):
            r = j % NRAW
            before = self.raw_last.get(r, -1) + 1 - self.tiles
            if j >= NRAW:
                raws.append(j - NRAW + 1)
            else:
                own = max(q for q in range(T) if q % NRAW == r)
                raws.append(max(before, own + 1 - T) if count > 1 else before)
        ph["free"], ph["raws"] = free, raws
        for slot, last in last_by_slot.items():
            self.slot_need[slot] = self.items + (count - 1) * items + last + 1
        for j in range(T):
            self.raw_last[j % NRAW] = self.tiles + (count - 1) * T + j
        self.items += count * items
        self.tiles += count * T
        self.phases[name] = ph
        self.order.append(ph)

    def claim(self, slots):
        for s in slots:
            self.slot_need[s] = self.items


NRAW = 2


def build(nc, A, out):
    ctx = ExitStack()
    with ctx:
        base = 16512
        end = nc.sbuf_usable_end

        def at(name, shape, offset, dt=F32):
            size = int(np.prod(shape[1:])) * 4
            assert offset + size <= end, (name, offset + size, end)
            return nc.alloc_sbuf_tensor_at(name, shape, dt, offset=offset)

        KB = 1024
        X = at("X", [P, NK, SEQ], base)
        UH = at("UH", [P, NK, SEQ], base + 32 * KB, F32R)
        UL = at("UL", [P, NK, SEQ], base + 64 * KB, F32R)
        o = base + 96 * KB
        PV_W = 768
        names = {}

        def small(name, shape, dt=F32):
            nonlocal o
            t = at(name, shape, o, dt)
            o += (int(np.prod(shape[1:])) * 4 + 31) // 32 * 32
            return t

        PV = small("PV", [P, PV_W])
        VEC = small("VEC", [P, 40 * NK])
        MOD = small("MOD", [P, 4, 24])
        IDENT = small("IDENT", [P, P])
        ONES = small("ONES", [P, P])
        BLK = small("BLK", [P, P])
        MASKC = small("MASKC", [P, P])
        CS = small("CS", [P, NK])
        EPSL = small("EPSL", [P, 1])
        EPSR = small("EPSR", [P, 1])
        QKG = small("QKG", [P, 2])
        MASKA = small("MASKA", [P, P])
        MXT, NMX, RSUM, RINV = (small(n, [P, 16]) for n in ("MXT", "NMX", "RSUM", "RINV"))
        BF = small("BF", [16, 1])
        RAW = [at(f"RAW{i}", [P, 1024], o + 4 * KB * i) for i in range(NRAW)]
        o += 4 * KB * NRAW
        slot0 = o
        WH = [at(f"WH{i}", [P, 1024], o + 8 * KB * i, F32R) for i in range(8)]
        WL = [at(f"WL{i}", [P, 1024], o + 8 * KB * i + 4 * KB, F32R) for i in range(8)]
        scr = {n: slot0 + 8 * KB * n for n in range(9)}

        PS = nc.alloc_psum_tensor("PS", [P, 8 * HALF], F32)
        bank = lambda i, w=HALF: PS[:, i * HALF:i * HALF + w]

        sems = {}

        def S(name):
            if name not in sems:
                sems[name] = ctx.enter_context(nc.semaphore(name))
            return sems[name]

        prow = param_rows(A)
        pcol, r = {}, 0
        for n, ap in prow.items():
            pcol[n] = r
            r += ap.shape[0]
        n_prow = r
        n_ptile = (n_prow + P - 1) // P
        assert n_ptile * P <= PV_W

        def pv(name, j=0, w=1):
            return PV[:, pcol[name] + j:pcol[name] + j + w]

        vcol = {}

        def vec(name, w=NK):
            if name not in vcol:
                vcol[name] = (sum(x for _, x in vcol.values()), w)
                assert vcol[name][0] + w <= 40 * NK
            a, w = vcol[name]
            return VEC[:, a:a + w]

        plan = Plan()
        view3 = lambda t, k: t[:, :].rearrange("p (k m) -> p k m", k=k)

        def cols(w, m0, width=P):
            return w.rearrange("(k p) m -> p k m", p=P)[:, :, bass.ds(m0, width)]

        def rows2(w, k0, n, m0, width):
            return w.rearrange("(k p) m -> p k m", p=P)[:, bass.ds(k0, n), m0:m0 + width]

        def tile_m(w, m0_of, width=P):
            if width == P:
                return lambda it, r: [(view3(r, NK), cols(w, m0_of(it)))]
            return lambda it, r: [(r[:, 0:NK * width].rearrange("p (k m) -> p k m", k=NK), cols(w, m0_of(it), width))]

        def tile_row(w, k_of):
            return lambda it, r: [(view3(r, 1), rows2(w, k_of(it), 1, 0, D))]

        def tile_t(w, k0, starts):
            w_ = 256 // len(starts)
            return lambda it, r: [(view3(r, 4)[:, :, i * w_:(i + 1) * w_],
                                   w.rearrange("(k p) m -> p k m", p=P)[:, k0:k0 + 4, bass.ds(s(it), w_)])
                                  for i, s in enumerate(starts)]

        ev_in, ev_out = A["ev_w_in"][0], A["ev_w_out"][0]
        od_in, od_out = A["od_w_in"][0], A["od_w_out"][0]

        def plan_even():
            xr = lambda d: tile_m(ev_in, lambda it: (it + d) * P)
            yr = lambda d: tile_m(ev_in, lambda it: (it + d) * P + RG)
            wo = lambda d: tile_row(ev_out, lambda it: it + d)
            plan.add("rg_first", 1, [(xr(0), 2, 0), (yr(0), 3, 1)], 8)
            plan.add("rg", 3, [(xr(1), 2, 0), (yr(1), 3, 1), (wo(0), 19, 2)], 24)
            plan.add("rg_last", 1, [(wo(3), 15, 0)], 16)
            q0, k0, v0, g0, z0 = 2 * RG, 2 * RG + 256, 2 * RG + 512, 2 * RG + 1024, 2 * RG + 1536
            slot = 0
            for p in range(2):
                I = 0
                tiles = []

                def t(src, last):
                    nonlocal slot
                    tiles.append((src, last, slot % 3))
                    slot += 1

                if p == 0:
                    t(tile_m(ev_in, lambda it: z0, 16), 1)
                    I += 2
                I += 2
                t(tile_m(ev_in, lambda it, p=p: q0 + p * P), I + 1)
                t(tile_m(ev_in, lambda it, p=p: k0 + p * P), I + 3)
                I += 4
                t(tile_t(ev_in, 0, [lambda it, p=p: v0 + p * 256]), I + 7)
                t(tile_t(ev_in, 4, [lambda it, p=p: v0 + p * 256]), I + 7)
                I += 8
                I += 2 + 4 + 8
                t(tile_m(ev_in, lambda it, p=p: g0 + 2 * p * P), I + 1)
                t(tile_m(ev_in, lambda it, p=p: g0 + (2 * p + 1) * P), I + 3)
                I += 4
                t(tile_row(ev_out, lambda it, p=p: 4 + 2 * p), I + 17)
                t(tile_row(ev_out, lambda it, p=p: 5 + 2 * p), I + 35)
                plan.add(f"gla{p}", 1, tiles, I + 36)

        def plan_mlp(l):
            w1, w2 = A["mlp_w1"][l], A["mlp_w2"][l]
            tiles = []
            for q in range(2):
                for m in range(2):
                    tiles.append((tile_m(w1, lambda it, q=q, m=m: it * 512 + q * 256 + m * P),
                                  q * 20 + 2 + m, 4 * q + m))
                for t in range(2):
                    tiles.append((lambda it, r, q=q, t=t: [(view3(r, 2), rows2(w2, it * 4 + q * 2, 2, t * 512, 512))],
                                  q * 20 + 4 + 8 + 4 * t + 3, 4 * q + 2 + t))
            plan.add(f"mlp{l}", D_FF // (2 * FF_GROUP), tiles, 40)

        def plan_odd():
            plan.add("fl", 1, [(tile_m(od_in, lambda it: 4 * D, 16), 1, 0)], 2)
            vg = [lambda it: it * P + 2 * D, lambda it: it * P + 3 * D]
            plan.add("odd", 8, [(tile_m(od_in, lambda it: it * P), 2, 0),
                                (tile_m(od_in, lambda it: it * P + D), 3, 1),
                                (tile_t(od_in, 0, vg), 11, 2), (tile_t(od_in, 4, vg), 11, 3),
                                (tile_row(od_out, lambda it: it), 27, 4)], 28)

        def plan_spatial():
            w_in, w_out = A["w_in_2"], A["w_out_2"]
            v = [(tile_t(w_in, k0, [lambda it, p=p: 512 + p * 256]), 8 * p + 7, (2 * p + k0 // 4) % 3)
                 for p in range(2) for k0 in (0, 4)]
            plan.add("sv", 1, v, 16)
            plan.add("mix", 4, [(tile_m(w_in, lambda it: it * P + 1024), 2, 0),
                                (tile_m(w_in, lambda it: it * P + 1536), 3, 1),
                                (tile_m(w_in, lambda it: it * P), 5, 2),
                                (tile_row(w_out, lambda it: it), 23, 0)], 24)
            plan.add("yb", 4, [(tile_row(w_out, lambda it: it + 4), 15, 0)], 16)

        def plan_ffn():
            w = A["w_up_2"]
            tiles = [(tile_m(w, lambda it, m=m: it * 256 + m * P), 4 + m, m) for m in range(2)]
            tiles += [(tile_m(w, lambda it, m=m: it * 256 + m * P + D_FF2), 6 + m, 2 + m) for m in range(2)]
            tiles += [(lambda it, r, t=t: [(view3(r, 2), rows2(A["w_down_2"], it * 2, 2, t * 512, 512))],
                       8 + 8 + 4 * t + 3, 4 + t) for t in range(2)]
            plan.add("ffn", D_FF2 // 256, tiles, 24)

        plan_even()
        plan.claim(range(3, 8))
        plan_mlp(0)
        plan_odd()
        plan.claim(range(5, 8))
        plan_mlp(1)
        plan_spatial()
        plan.claim(range(3, 8))
        plan_ffn()
        PH = plan.phases

        top = scr[8] + 20 * KB
        SQ = [at(f"SQ{i}", [P, HALF], top + 2 * KB * i) for i in range(2)]
        RST = at("RST", [P, HALF], top + 4 * KB)
        TU = [at(f"TU{i}", [P, HALF], top + 6 * KB + 2 * KB * i) for i in range(2)]
        XIN = at("XIN", [P, NT, D], scr[3] + 4 * KB)
        PROW = at("PROW", [P, n_ptile, P], scr[3])
        ADAW = at("ADAW", [P, 1024], scr[8] + 16 * KB)
        HH = at("HH", [P, 2, SEQ], scr[8], F32R)
        HL = at("HL", [P, 2, SEQ], scr[8] + 8 * KB, F32R)
        ADS = at("ADS", [P, NK, D], base + 32 * KB)
        ADC = at("ADC", [P, NK, D], base + 64 * KB)
        ADG = at("ADG", [P, NK, D], scr[3] + 4 * KB)
        YO = [at(f"YO{i}", [P, D], scr[8] + 4 * KB * i) for i in range(2)]
        FZ = at("FZ", [P, 4, 2 + HALF + 6], scr[6])
        FY = at("FY", [P, 4, HALF], scr[6] + 9 * KB)
        FH = at("FH", [P, 2, SEQ], scr[6] + 17 * KB, F32R)
        FL = at("FL", [P, 2, SEQ], scr[6] + 25 * KB, F32R)
        e0 = scr[3]
        XR = at("XR", [P, 3 + SEQ], e0)
        XC = at("XC", [P, SEQ], e0 + 5 * KB)
        YG = at("YG", [P, SEQ], e0 + 9 * KB)
        GR = at("GR", [P, SEQ], e0 + 13 * KB)
        GI = at("GI", [P, SEQ], e0 + 17 * KB)
        TH = at("TH", [P, SEQ], e0 + 21 * KB)
        HS = at("HS", [P, SEQ], e0 + 25 * KB)
        AA = at("AA", [P, SEQ], e0 + 29 * KB)
        MH = at("MH", [P, SEQ], e0 + 33 * KB, F32R)
        ML = at("ML", [P, SEQ], e0 + 37 * KB, F32R)
        WGA = at("WGA", [P, P], e0 + 41 * KB)
        WGX = at("WGX", [P, P], e0 + 41 * KB + 512)
        B = [at(f"B{i}", [P, SEQ], e0 + 4 * KB * i) for i in range(7)]
        ATT = at("ATT", [P, 2, NT, P], e0)
        ZL = at("ZL", [16, SEQ], e0 + 28 * KB)
        CHM = at("CHM", [P, HALF], e0 + 32 * KB)
        VT = at("VT", [P, NT, 256], e0 + 34 * KB)
        STT_ = at("STT", [P, 16, P], e0 + 42 * KB)
        GMH = at("GMH", [P, SEQ], e0 + 16 * KB, F32R)
        GML = at("GML", [P, SEQ], e0 + 24 * KB, F32R)
        OO = [at(f"OO{i}", [P, HALF], e0 + 50 * KB + 2 * KB * i) for i in range(2)]
        GSQ = at("GSQ", [P, HALF], top)
        GRS = at("GRS", [P, HALF], top + 2 * KB)
        MASKG = at("MASKG", [P, P], top + 4 * KB)
        WUP = at("WUP", [16, 256], top + 5 * KB)
        DEC = at("DEC", [P, 16], top + 6 * KB)
        d0 = scr[5]
        QH = at("QH", [P, SEQ], d0, F32R)
        QL = at("QL", [P, SEQ], d0 + 4 * KB, F32R)
        KH = at("KH", [P, SEQ], d0 + 8 * KB, F32R)
        KL = at("KL", [P, SEQ], d0 + 12 * KB, F32R)
        V = at("V", [P, NT, P], d0 + 16 * KB)
        G = at("G", [P, NT, P], d0 + 20 * KB)
        NF = at("NF", [P, 2, SEQ], d0 + 24 * KB)
        PR = [at(f"PR{i}", [P, SEQ], d0 + 32 * KB + 4 * KB * i) for i in range(2)]
        PT = [at(f"PT{i}", [P, SEQ], d0 + 40 * KB + 4 * KB * i) for i in range(2)]
        QT = [at(f"QT{i}", [P, HALF], d0 + 32 * KB + 2 * KB * i) for i in range(2)]
        QSQ = at("QSQ", [P, HALF], d0 + 36 * KB)
        QRS = at("QRS", [P, HALF], d0 + 38 * KB)
        FE = at("FE", [16, SEQ], d0 + 40 * KB)
        FC = at("FC", [16, SEQ], d0 + 44 * KB)
        YB = at("YB", [P, CONV_PAD + SEQ + 2], e0)
        CX = at("CX", [P, 4, SEQ], e0 + 5 * KB)
        VS = at("VS", [P, NT, 512], e0 + 21 * KB)
        SMH = at("SMH", [P, SEQ], e0 + 37 * KB, F32R)
        SML = at("SML", [P, SEQ], e0 + 41 * KB, F32R)
        AB = at("AB", [P, HALF], e0 + 45 * KB)
        GB = at("GB", [P, HALF], e0 + 47 * KB)
        VH = at("VH", [P, NT, P], e0 + 49 * KB)
        BS = at("BS", [P, 4, P], top + 8 * KB)
        LAG = at("LAG", [P, 512], e0 + 53 * KB)
        LAB = at("LAB", [P, 512], e0 + 55 * KB)
        WST = at("WST", [P, 4, P], e0 + 57 * KB)
        UU = at("UU", [P, SEQ], top)
        TY = [at(f"TY{i}", [P, HALF], top + 4 * KB + 2 * KB * i) for i in range(2)]
        BROW = at("BROW", [1, 512], e0 + 41 * KB)
        WSR = at("WSR", [P, 4, P], e0 + 45 * KB)
        BST = at("BST", [P, 32, 6], e0 + 49 * KB)
        MV = at("MV", [P, 32, 2], e0 + 49 * KB + 768)
        VR = at("VR", [P, 32], e0 + 49 * KB + 1024)
        negf = nc.dram_tensor("neg_f_cum", [16, SEQ], F32, kind="Internal").ap()

        n_prow_dma = sum((pcol[n] + ap.shape[0] - 1) // P - pcol[n] // P + 1 for n, ap in prow.items())
        block = ctx.enter_context(nc.Block())

        @block.tensor
        def _(pe):
            w_ready = Tally(pe, S("w_ready"))
            a_free, d_free = Tally(pe, S("a_free")), Tally(pe, S("d_free"))
            sq = Tally(pe, S("sq"))
            ada_in = Tally(pe, S("ada_in"))
            done = S("gemm_done")
            turn = {"a": 0, "d": 0}

            def a_bank():
                b = turn["a"] % NA
                turn["a"] += 1
                a_free.take()
                return b

            def d_bank():
                b = NA + turn["d"] % ND
                turn["d"] += 1
                d_free.take()
                return b

            def three(out, parts, signal=None):
                for i, (wh, wl, xh, xl) in enumerate(parts):
                    pe.matmul(out, wh, xh, start=(i == 0), stop=False)
                    pe.matmul(out, wh, xl, start=False, stop=False)
                    mm = pe.matmul(out, wl, xh, start=False, stop=(i == len(parts) - 1))
                mm.then_inc(done if signal is None else signal, 1)

            def w_tile(ph, j):
                w_ready.take()
                s = ph["tiles"][j][2]
                return WH[s], WL[s]

            def half(h):
                return slice(h * HALF, (h + 1) * HALF)

            def u_item(tile, h, width=P, fresh=None):
                b = a_bank()
                parts = []
                for k in range(NK):
                    if fresh is not None:
                        pe.wait_ge(S(f"u_ready{h}"), NK * fresh + k + 1)
                    c = slice(k * width, (k + 1) * width)
                    parts = [(tile[0][:, c], tile[1][:, c], UH[:, k, half(h)], UL[:, k, half(h)])]
                    for wh, wl, xh, xl in parts:
                        pe.matmul(bank(b)[0:width], wh, xh, start=(k == 0), stop=False)
                        pe.matmul(bank(b)[0:width], wh, xl, start=False, stop=False)
                        mm = pe.matmul(bank(b)[0:width], wl, xh, start=False, stop=(k == NK - 1))
                mm.then_inc(done, 1)

            def token_item(ta, tb, t, extra=None):
                b = a_bank()
                o = bank(b, 256)
                for k in range(NK):
                    w = ta if k < 4 else tb
                    c = slice((k % 4) * 256, (k % 4 + 1) * 256)
                    x = slice(t * P, (t + 1) * P)
                    pe.matmul(o, UH[:, k, x], w[0][:, c], start=(k == 0), stop=False)
                    pe.matmul(o, UL[:, k, x], w[0][:, c], start=False, stop=False)
                    mm = pe.matmul(o, UH[:, k, x], w[1][:, c], start=False, stop=(k == NK - 1 and extra is None))
                if extra is not None:
                    mm = pe.matmul(o, ONES[0:1, :], extra, start=False, stop=True)
                mm.then_inc(done, 1)

            def out_row(tile, mh, ml):
                for h in range(2):
                    for m in range(NK):
                        b = d_bank()
                        c = slice(m * P, (m + 1) * P)
                        three(bank(b), [(tile[0][:, c], tile[1][:, c], mh[:, half(h)], ml[:, half(h)])])

            def down(tiles, hh, hl, ready, h):
                for m in range(NK):
                    if m % 4 == 0 and h == 0:
                        tiles.append(w_tile(*ready[m // 4]))
                    t = tiles[m // 4]
                    b = d_bank()
                    three(bank(b), [(t[0][:, k * 512 + (m % 4) * P:k * 512 + (m % 4 + 1) * P],
                                     t[1][:, k * 512 + (m % 4) * P:k * 512 + (m % 4 + 1) * P],
                                     hh[:, k, half(h)], hl[:, k, half(h)]) for k in range(2)])

            def ada_item(col):
                ada_in.take(16)
                for k in range(NK):
                    mm = pe.matmul(bank(7)[:, col], ADAW[:, k * P:(k + 1) * P], CS[:, k:k + 1],
                                   start=(k == 0), stop=(k == NK - 1))
                mm.then_inc(S("ada_done"), 1)

            t_xt = Tally(pe, S("xt_free"))

            def norm_sums(kt, x_of):
                for h in range(2):
                    d_free.wait_at(ND)
                    for k in range(kt):
                        mm = pe.matmul(bank(6), ONES[:, :], x_of(k, h), start=(k == 0), stop=(k == kt - 1))
                    mm.then_inc(S("stat_done"), 1)
                    if norms_done[0]:
                        pe.wait_ge(S("std"), norms_done[0])
                    for k in range(kt):
                        sq.take()
                        mm = pe.matmul(bank(7), ONES[:, :], SQ[k % 2][:, :], start=(k == 0), stop=(k == kt - 1))
                        mm.then_inc(S("sq_used"), 1)
                    norms_done[0] += 1

            norms_done = [0]

            pe.sem_inc(S("o_done"), 2)
            pe.wait_ge(S("consts"), 1)
            pe.wait_ge(S("prow_in"), 16 * n_prow_dma)
            for i in range(n_ptile):
                mm = pe.transpose(PS[:, 6 * HALF + i * P:6 * HALF + (i + 1) * P], PROW[:, i, :], IDENT[:, :])
            mm.then_inc(S("pv_done"), 1)
            for h in range(2):
                for k in range(NK):
                    n = h * NK + k
                    t_xt.wait_at(n - 5)
                    for t in range(4):
                        if k == 0 and t == 0:
                            pe.wait_ge(S(f"x_in{h}"), 16)
                        mm = pe.transpose(PS[:, (n % 6) * HALF + t * P:(n % 6) * HALF + (t + 1) * P],
                                          XIN[:, 4 * h + t, k * P:(k + 1) * P], IDENT[:, :])
                    mm.then_inc(S("xt_done"), 1)
            pe.wait_ge(S("cs_ready"), 1)
            for i, w in enumerate((ADS, ADC, ADG)):
                pe.wait_ge(S(f"ada0_in{i}"), 16)
                for m in range(NK):
                    for k in range(NK):
                        mm = pe.matmul(bank(7 - i // 2)[:, i * NK + m:i * NK + m + 1], w[:, k, m * P:(m + 1) * P],
                                       CS[:, k:k + 1], start=(k == 0), stop=(k == NK - 1))
                mm.then_inc(S("ada_done"), 1)

            def mlp(l, fresh):
                ph = PH[f"mlp{l}"]
                pairs = [(w_ready, 8), (a_free, 8), (d_free, 32), (h_ready, 8)]
                if l == 0:
                    pairs.append((ada_in, 16 * 6))
                    pe.wait_ge(S("std"), norms_done[0])
                with rounds(pe, ph["count"], *pairs) as it:
                    for q in range(2):
                        t = []
                        for h in range(2):
                            for m in range(2):
                                if h == 0:
                                    t.append(w_tile(ph, 4 * q + m))
                                u_item(t[m], h, fresh=fresh if q == 0 and m == 0 else None)
                                if l == 0 and 2 * h + m < 3:
                                    i = q * 3 + 2 * h + m
                                    ada_item(bass.ds(q * 24 + it * 3 + 2 * h + m, 1))
                        t = []
                        for h in range(2):
                            h_ready.take(2)
                            down(t, HH, HL, [(ph, 4 * q + 2), (ph, 4 * q + 3)], h)

            h_ready = Tally(pe, S("h_ready"), 2)
            xk = lambda k, h: X[:, k, half(h)]
            fresh = 0

            def even():
                m_ready = Tally(pe, S("m_ready"))
                xc_ready = Tally(pe, S("xc_ready"))
                wg_in = Tally(pe, S("wg_in"))

                def xr_yr(ph, fresh=None):
                    t = []
                    for h in range(2):
                        for m in range(2):
                            if h == 0:
                                t.append(w_tile(ph, m))
                            u_item(t[m], h, fresh=fresh if m == 0 else None)
                            if ph["name"] == "rg":
                                ada_item(bass.ds(rg_it[0] * 4 + 2 * h + m, 1))

                def gates():
                    wg_in.take(64)
                    for h in range(2):
                        xc_ready.take()
                        for w in (WGA, WGX):
                            b = a_bank()
                            pe.matmul(bank(b), w[:, :], XC[:, half(h)], start=True, stop=True).then_inc(done, 1)

                rg_it = [None]
                xr_yr(PH["rg_first"], fresh=0)
                gates()
                pe.wait_ge(S("mod_ready"), 1)
                with rounds(pe, 3, (w_ready, 3), (a_free, 8), (d_free, 16), (m_ready, 1), (xc_ready, 2),
                            (wg_in, 64), (ada_in, 64)) as it:
                    rg_it[0] = it
                    xr_yr(PH["rg"])
                    m_ready.take()
                    out_row(w_tile(PH["rg"], 2), MH, ML)
                    gates()
                m_ready.take()
                out_row(w_tile(PH["rg_last"], 0), MH, ML)

                qk = Tally(pe, S("qk_ready"))
                gst = Tally(pe, S("gla_std"))
                ada_n = 12
                for p in range(2):
                    ph = PH[f"gla{p}"]
                    j = 0
                    if p == 0:
                        t = w_tile(ph, j)
                        j += 1
                        for h in range(2):
                            u_item(t, h, width=16)
                        pe.wait_ge(S("wup_in"), 16)
                        a_free.wait_at(NA)
                    for h in range(2):
                        b = a_bank()
                        pe.matmul(bank(b), WUP[:, p * P:(p + 1) * P], ZL[:, half(h)],
                                  start=True, stop=True).then_inc(done, 1)
                    for _ in range(2):
                        t = w_tile(ph, j)
                        j += 1
                        for h in range(2):
                            u_item(t, h)
                            ada_item(slice(ada_n, ada_n + 1))
                            ada_n += 1
                    ta, tb = w_tile(ph, j), w_tile(ph, j + 1)
                    j += 2
                    for t in range(NT):
                        token_item(ta, tb, t)
                    qk.take(3)
                    for g in range(2):
                        b = d_bank()
                        for t in range(4):
                            mm = pe.transpose(PS[:, b * HALF + t * P:b * HALF + (t + 1) * P],
                                              B[4][:, (4 * g + t) * P:(4 * g + t + 1) * P], IDENT[:, :])
                        mm.then_inc(done, 1)
                    for hh in range(2):
                        r = slice(64 * hh, 64 * hh + 64)
                        for g in range(2):
                            b = d_bank()
                            for t in range(4):
                                c = slice((4 * g + t) * P, (4 * g + t + 1) * P)
                                mm = pe.matmul(PS[:, b * HALF + t * P:b * HALF + (t + 1) * P],
                                               B[3][r, c], B[5][r, c], start=(t == 0), stop=(t == 3),
                                               skip_group_check=True)
                            mm.then_inc(done, 1)
                    a_free.wait_at(NA)
                    d_free.wait_at(ND)
                    for t in range(0, NT, 2):
                        for e in range(2):
                            b = d_bank()
                            r = slice(64 * e, 64 * e + 64)
                            for i in range(2):
                                mm = pe.matmul(PS[:, b * HALF + i * 256:b * HALF + (i + 1) * 256],
                                               B[6][r, (t + i) * P:(t + i + 1) * P], VT[r, t + i, :],
                                               start=(i == 0), stop=(i == 1), skip_group_check=True)
                            mm.then_inc(done, 1)
                    for i in range(2):
                        t = w_tile(ph, j)
                        j += 1
                        for h in range(2):
                            u_item(t, h)
                            if h == 0:
                                ada_item(slice(ada_n, ada_n + 1))
                                ada_n += 1
                    d_free.wait_at(ND)
                    for hh in range(2):
                        r = slice(64 * hh, 64 * hh + 64)
                        for h in range(2):
                            b = a_bank()
                            for t in range(4 * h, 4 * h + 4):
                                o = PS[:, b * HALF + (t % 4) * P:b * HALF + (t % 4 + 1) * P]
                                pe.matmul(o, VT[:, t, hh * P:(hh + 1) * P], ATT[:, hh, t, :],
                                          start=(t % 4 == 0), stop=False, skip_group_check=True)
                            for n in range(8 * h, 8 * h + 8):
                                o = PS[:, b * HALF + (n % 8) * 64:b * HALF + (n % 8 + 1) * 64]
                                mm = pe.matmul(o, STT_[r, n, :], B[5][r, n * 64:(n + 1) * 64],
                                               start=False, stop=(n % 8 == 7), skip_group_check=True)
                            mm.then_inc(done, 1)
                            a_free.wait_at(NA)
                            pe.matmul(bank(6), ONES[:, :], GSQ[:, :], start=True, stop=True)\
                                .then_inc(S("gla_sum"), 1)
                            gst.take()
                        m_ready.take(2)
                        out_row(w_tile(ph, j), GMH, GML)
                        j += 1

            def odd(fresh):
                t = w_tile(PH["fl"], 0)
                for h in range(2):
                    u_item(t, h, width=16, fresh=fresh)
                qst = Tally(pe, S("q_std"))
                qkr = Tally(pe, S("qkn_ready"), 2)
                s_free = Tally(pe, S("s_free"))
                probs = Tally(pe, S("probs"))
                pt_a, pt_d = Tally(pe, S("pt_a")), Tally(pe, S("pt_d"))
                o_free = Tally(pe, S("o_free"))
                m_ready = Tally(pe, S("ot_ready"))
                ph = PH["odd"]
                n_d = 2 * sum(1 for tb in range(NT) if tb >= 4)
                with rounds(pe, 8, (w_ready, 5), (a_free, 12), (d_free, 16), (qst, 4), (qkr, 4),
                            (s_free, 16), (probs, 16), (pt_a, 16), (pt_d, n_d), (o_free, 16),
                            (m_ready, 2)) as it:
                    d_free.wait_at(ND)
                    tiles = []
                    for h in range(2):
                        for m in range(2):
                            if h == 0:
                                tiles.append(w_tile(ph, m))
                            u_item(tiles[m], h)
                            a_free.wait_at(NA)
                            pe.matmul(bank(6), BLK[:, :], QSQ[:, :], start=True, stop=True)\
                                .then_inc(S("q_sum"), 1)
                            qst.take()
                    ta, tb_ = w_tile(ph, 2), w_tile(ph, 3)
                    for t in range(NT):
                        token_item(ta, tb_, t)
                    a_free.wait_at(NA)
                    qkr.take(4)

                    def scores(n):
                        hh, tb = n // NT, n % NT
                        r = slice(64 * hh, 64 * hh + 64)
                        w = (tb // 2 + 1) * 256
                        q = slice(tb * P, (tb + 1) * P)
                        b = 2 * (n % 2)
                        if n >= 2:
                            s_free.take()
                        for c in range(0, w, HALF):
                            e = min(c + HALF, w)
                            o = PS[:, b * HALF + c:b * HALF + e]
                            pe.matmul(o, QH[r, q], KH[r, c:e], start=True, stop=False, skip_group_check=True)
                            pe.matmul(o, QH[r, q], KL[r, c:e], start=False, stop=False, skip_group_check=True)
                            pe.matmul(o, QL[r, q], KH[r, c:e], start=False, stop=False, skip_group_check=True)
                        pe.matmul(PS[:, b * HALF + tb * P:b * HALF + (tb + 1) * P], IDENT[:, :], MASKA[:, :],
                                  start=False, stop=True, skip_group_check=True).then_inc(S("s_done"), 1)

                    def turn_probs(n):
                        tb = n % NT
                        probs.take()
                        for s in range(tb + 1):
                            if s == 0 and n:
                                pt_a.take()
                            if s == 4 and n_turn[0]:
                                pt_d.take()
                            if s == 4:
                                n_turn[0] += 1
                            mm = pe.transpose(PS[:, 4 * HALF + s * P:4 * HALF + (s + 1) * P],
                                              PR[n % 2][:, s * P:(s + 1) * P], IDENT[:, :])
                            if s == min(tb, 3):
                                mm.then_inc(S("pt4_done"), 1)
                            elif s == tb:
                                mm.then_inc(S("pt5_done"), 1)

                    def values(n):
                        hh, tb = n // NT, n % NT
                        if n >= 2:
                            o_free.take()
                        pt_a.wait_at(1)
                        if tb >= 4:
                            pt_d.wait_at(1)
                        for s in range(tb + 1):
                            mm = pe.matmul(bank(6 + n % 2, 64), PT[n % 2][:, s * P:(s + 1) * P],
                                           V[:, s, 64 * hh:64 * hh + 64], start=(s == 0), stop=(s == tb))
                        mm.then_inc(S("o_done"), 1)

                    n_turn = [0]
                    scores(0)
                    scores(1)
                    for n in range(2 * NT):
                        turn_probs(n)
                        if n + 2 < 2 * NT:
                            scores(n + 2)
                        values(n)
                    s_free.take(2)
                    pt_a.take()
                    pt_d.take()
                    o_free.take(2)
                    for g in range(2):
                        for t in range(4):
                            mm = pe.transpose(PS[:, (4 + g) * HALF + t * P:(4 + g) * HALF + (t + 1) * P],
                                              G[:, 4 * g + t, :], IDENT[:, :])
                        mm.then_inc(S("ot_done"), 1)
                    m_ready.take(2)
                    out_row(w_tile(ph, 4), QH, QL)

            def spatial(fresh):
                for h in range(2):
                    pe.wait_ge(S(f"u_ready{h}"), NK * (fresh + 1))
                pe.wait_ge(S("sp_in"), 16 * 5)
                for hh in range(4):
                    mm = pe.transpose(PS[:, 6 * HALF + hh * P:6 * HALF + (hh + 1) * P], WSR[:, hh, :], IDENT[:, :])
                mm.then_inc(S("wst_done"), 1)
                ph = PH["sv"]
                for p in range(2):
                    ta, tb = w_tile(ph, 2 * p), w_tile(ph, 2 * p + 1)
                    for t in range(NT):
                        token_item(ta, tb, t, extra=BROW[0:1, 256 * p:256 * p + 256])
                m_ready = Tally(pe, S("sm_ready"))
                ph = PH["mix"]
                vh = Tally(pe, S("vh_ready"))
                with rounds(pe, 4, (w_ready, 4), (a_free, 8), (d_free, 16), (m_ready, 2), (vh, 1)) as it:
                    t = []
                    for h in range(2):
                        for m in range(2):
                            if h == 0:
                                t.append(w_tile(ph, m))
                            u_item(t[m], h)
                    t = w_tile(ph, 2)
                    for h in range(2):
                        u_item(t, h)
                    vh.take()
                    for h in range(2):
                        b = a_bank()
                        for c in range(4):
                            mm = pe.matmul(PS[:, b * HALF + c * P:b * HALF + (c + 1) * P],
                                           VH[:, 4 * h + c, :], WST[:, bass.ds(it, 1), :].rearrange("p a b -> p (a b)"),
                                           start=(c == 0), stop=(c == 3), skip_group_check=True)
                        mm.then_inc(done, 1)
                    m_ready.take(2)
                    out_row(w_tile(ph, 3), SMH, SML)
                pe.wait_ge(S("cx_ready"), 4)
                norm_sums(4, lambda k, h: CX[:, k, half(h)])
                ph = PH["yb"]
                with rounds(pe, 4, (w_ready, 1), (d_free, 16), (m_ready, 2)) as it:
                    m_ready.take(2)
                    out_row(w_tile(ph, 0), SMH, SML)

            def ffn(fresh):
                ph = PH["ffn"]
                with rounds(pe, ph["count"], (w_ready, 6), (a_free, 8), (d_free, 16), (h_ready, 4)) as it:
                    t = []
                    for h in range(2):
                        for m in range(4):
                            if h == 0:
                                t.append(w_tile(ph, m))
                            u_item(t[m], h, fresh=fresh if m == 0 else None)
                    t = []
                    for h in range(2):
                        h_ready.take(2)
                        down(t, FH, FL, [(ph, 4), (ph, 5)], h)

            even()
            norm_sums(NK, xk)
            pe.wait_ge(S("mod_ready"), 2)
            mlp(0, 1)
            norm_sums(NK, xk)
            odd(2)
            norm_sums(NK, xk)
            mlp(1, 3)
            norm_sums(NK, xk)
            spatial(4)
            norm_sums(NK, xk)
            ffn(5)
            norm_sums(NK, xk)
            for t in range(NT):
                for g in range(2):
                    n = 2 * t + g
                    pe.wait_ge(S("y_ready"), NK * (t // 4 + 1))
                    if n >= 4:
                        pe.wait_ge(S("yo_ready"), n - 3)
                    for k in range(4):
                        mm = pe.transpose(PS[:, (n % 4) * HALF + k * P:(n % 4) * HALF + (k + 1) * P],
                                          X[:, 4 * g + k, t * P:(t + 1) * P], IDENT[:, :])
                    mm.then_inc(S("y_done"), 1)

        @block.scalar
        def _(act):
            gd = Tally(act, S("gemm_done"))
            cen, sq_used, tt = Tally(act, S("cen")), Tally(act, S("sq_used"), -2), Tally(act, S("tt"))
            ada_done = Tally(act, S("ada_done"))
            chain = Chain(act, S("act_chain"))
            mine = Tally(act, S("a_free"), NA)
            turn = [0]
            half = lambda h: slice(h * HALF, (h + 1) * HALF)
            col = lambda t, j: t[:, j:j + 1]

            def a_bank():
                gd.take()
                turn[0] += 1
                return bank((turn[0] - 1) % NA)

            def settle():
                act.sem_inc(S("act_turn"), 1)

            def free(ins):
                ins.then_inc(S("a_free"), 1)
                mine.skip()

            def ada_load(src):
                act.dma_start(view3(ADAW, NK), src).then_inc(S("ada_in"), 16)

            ada_w = lambda l, j, m: cols(A["ada_w"][l, j], m * P)

            def tail_tile(h, k, xg, xb):
                tt.take()
                act.activation(UH[:, k, half(h)], TU[k % 2][:, :], ACT.Copy).then_inc(S("uh"), 1)
                x = X[:, k, half(h)]
                if xg is None:
                    ins = act.activation(x, x, ACT.Copy, scale=ALPHA_1)
                else:
                    ins = act.activation(x, x, ACT.Identity, bias=col(xb, k), scale=col(xg, k))
                ins.then_inc(S("x_ready"), 1)

            def norm_std(kt, tile_of, h):
                for k in range(kt):
                    cen.take()
                    sq_used.take()
                    act.activation(SQ[k % 2][:, :], tile_of(k, h), ACT.Square).then_inc(S("sq"), 1)
                sq_used.wait_at(2)
                act.activation(RST[:, :], bank(7), ACT.Sqrt, bias=EPSL[:, :], scale=1.0 / (kt * P))\
                    .then_inc(S("std"), 1)

            def norm(xg, xb):
                for h in range(2):
                    norm_std(NK, lambda k, h: X[:, k, half(h)], h)
                    for k in range(NK):
                        tail_tile(h, k, xg, xb)

            act.sem_inc(S("a_free"), NA)
            ev_wa, ev_wx = A["ev_rg_wa"][0], A["ev_rg_wx"][0]

            def gate_blocks(c):
                for w, t in ((ev_wa, WGA), (ev_wx, WGX)):
                    for i in range(2):
                        act.dma_start(t[64 * i:64 * i + 64, 64 * i:64 * i + 64],
                                      w[bass.ds(2 * c + i, 1), :, :].rearrange("a p n -> (a p) n"))\
                            .then_inc(S("wg_in"), 16)

            act.wait_ge(S("consts"), 1)
            act.dma_start(WUP[:, :], A["ev_gla_w_up"][0]).then_inc(S("wup_in"), 16)
            act.dma_start(BF[:, :], A["od_b_f"].rearrange("a h -> h a")).then_inc(S("bf_in"), 16)
            for i, n in enumerate(("od_q_norm_g", "od_k_norm_g")):
                for e in range(2):
                    act.dma_start(QKG[64 * e:64 * e + 64, i:i + 1], A[n].rearrange("a h -> h a"))\
                        .then_inc(S("bf_in"), 16)
            act.wait_ge(S("pv_done"), 1)
            chain.done(act.activation(PV[:, 0:n_ptile * P], PS[:, 6 * HALF:6 * HALF + n_ptile * P], ACT.Copy))
            act.activation(CS[:, :], pv("c", 0, NK), ACT.Silu).then_inc(S("cs_ready"), 1)
            lam, le, ll = pv("ev_rg_lam", 0, 4), vec("le", 4), vec("ll", 4)
            chain.done(act.activation(le, lam, ACT.Abs))
            chain.done(act.activation(le, le, ACT.Exp, scale=-1.0))
            act.activation(ll, le, ACT.Ln, bias=1.0).then_inc(S("lam_e"), 1)
            for n in range(2 * NK):
                act.wait_ge(S("xt_done"), n + 1)
                act.activation(X[:, n % NK, half(n // NK)], bank(n % 6), ACT.Copy).then_inc(S("xt_free"), 1)
            act.dma_start(ADG[:, :, :], A["ada_w"][0, 0].rearrange("(k p) m -> p k m", p=P)[:, :, 2 * D:3 * D])\
                .then_inc(S("ada0_in2"), 16)
            for h in range(2):
                for k in range(NK):
                    tail_tile(h, k, None, None)
            ada_done.skip(3)

            def even():
                lru = Tally(act, S("lru"))

                def xr_yr(it):
                    loop = it is not None
                    if loop:
                        ada_load(ada_w(0, 1, it * 4))
                        gate_blocks(it + 1)
                    for h in range(2):
                        b = a_bank()
                        free(act.activation(XR[:, 3 + h * HALF:3 + (h + 1) * HALF], b, ACT.Copy))
                        if loop:
                            ada_done.take()
                            ada_load(ada_w(0, 1, it * 4 + 2 * h + 1))
                        b = a_bank()
                        free(act.activation(YG[:, half(h)], b, ACT.Gelu_apprx_tanh))
                        if loop:
                            ada_done.take()
                            if h == 0:
                                ada_load(ada_w(0, 1, it * 4 + 2))

                def gates(c):
                    cc = bass.ds(c, 1)
                    gv = lambda n: PV[:, bass.ds(c + pcol[n], 1)]
                    for h in range(2):
                        b = a_bank()
                        settle()
                        free(act.activation(GR[:, half(h)], b, ACT.Sigmoid, bias=gv("ev_rg_ba")))
                        b = a_bank()
                        settle()
                        free(act.activation(GI[:, half(h)], b, ACT.Sigmoid, bias=gv("ev_rg_bx")))
                    mine.wait_at(0)
                    settle()
                    act.activation(AA[:, :], GR[:, :], ACT.Exp, scale=vec("lam8", 4)[:, cc])
                    act.activation(TH[:, :], GR[:, :], ACT.Tanh, scale=vec("lam8n", 4)[:, cc])\
                        .then_inc(S("rg_a"), 1)
                    lru.take()
                    act.activation(TH[:, :], TH[:, :], ACT.Sqrt).then_inc(S("rg_a"), 1)
                    lru.take()
                    act.activation(MH[:, :], HS[:, :], ACT.Copy).then_inc(S("rg_a"), 1)

                gate_blocks(0)
                xr_yr(None)
                act.wait_ge(S("lam_ready"), 1)
                gates(0)
                with rounds(act, 3, (gd, 24), (mine, 8), (ada_done, 4), (lru, 2)) as it:
                    xr_yr(it)
                    gd.skip(16)
                    gates(it + 1)
                gd.skip(16)

                ada_n = 12
                gl, gsum, go = Tally(act, S("gl")), Tally(act, S("gla_sum")), Tally(act, S("gla_o"))
                ada_load(ada_w(0, 1, ada_n))

                def ada_next():
                    nonlocal ada_n
                    ada_done.take()
                    ada_n += 1
                    if ada_n < 24:
                        ada_load(ada_w(0, 1, ada_n))

                for p in range(2):
                    if p == 0:
                        for h in range(2):
                            free(act.activation(ZL[:, half(h)], a_bank()[0:16], ACT.Copy))
                    for h in range(2):
                        b = a_bank()
                        bu = pv("ev_gla_b_up", p)
                        act.activation(B[0][:, half(h)], b, ACT.Identity, bias=bu)
                        free(act.activation(B[2][:, half(h)], b, ACT.Abs, bias=bu))
                    mine.wait_at(0)
                    chain.done(act.activation(B[2][:, :], B[2][:, :], ACT.Exp, scale=-1.0))
                    act.activation(B[3][:, :], B[2][:, :], ACT.Ln, bias=1.0).then_inc(S("z_ready"), 1)
                    for t, s in ((B[5], 0.125), (B[6], 1.0)):
                        for h in range(2):
                            free(act.activation(t[:, half(h)], a_bank(), ACT.Copy, scale=s))
                            ada_next()
                    gl.take()
                    act.activation(B[2][:, :], B[1][:, :], ACT.Exp, scale=1 / 16)
                    act.activation(B[3][:, :], B[1][:, :], ACT.Exp, scale=-1 / 16)
                    act.activation(DEC[:, :], B[1][:, 63::64], ACT.Exp, scale=1 / 16)
                    act.activation(B[4][:, :], B[4][:, :], ACT.Exp, scale=1 / 16).then_inc(S("exps"), 1)
                    for t in range(NT):
                        free(act.activation(VT[:, t, :], a_bank()[:, 0:256], ACT.Copy))
                    gd.skip(14)
                    for i in range(2):
                        for h in range(2):
                            free(act.activation(B[2 + i][:, half(h)], a_bank(), ACT.Silu))
                            if h == 0:
                                ada_next()
                    for hh in range(2):
                        for h in range(2):
                            n = 4 * p + 2 * hh + h
                            b = a_bank()
                            act.activation(OO[h][:, :], b, ACT.Copy)
                            free(act.activation(GSQ[:, :], b, ACT.Square))
                            gsum.take()
                            act.activation(GRS[:, :], bank(6), ACT.Sqrt, bias=EPSR[:, :], scale=1.0 / P)\
                                .then_inc(S("gla_std"), 1)
                            go.take()
                            act.activation(GMH[:, half(h)], OO[h][:, :], ACT.Copy).then_inc(S("gmh"), 1)
                        gd.skip(16)

            h_done = Tally(act, S("h_ready"))

            def mlp(l):
                pairs = [(gd, 40), (mine, 8), (h_done, 8)] + ([(ada_done, 6)] if l == 0 else [])
                with rounds(act, 8, *pairs) as it:
                    for q in range(2):
                        if l == 0:
                            ada_load(ada_w(1, q, it * 3))
                        for h in range(2):
                            for m in range(2):
                                i = 2 * h + m
                                b = a_bank()
                                h_done.take()
                                settle()
                                r = SQ[i % 2]
                                b1 = PV[:, bass.ds(it * 4 + (pcol["mlp_b1"] + 32 * l + 2 * q + m), 1)]
                                free(act.activation(r[:, :], b, ACT.Relu, bias=b1))
                                mine.wait_at(0)
                                act.activation(HH[:, m, half(h)], r[:, :], ACT.Square)
                                act.activation(r[:, :], r[:, :], ACT.Square).then_inc(S("hh_ready"), 1)
                                if l == 0 and i < 3:
                                    ada_done.take()
                                    if i < 2:
                                        ada_load(ada_w(1, q, it * 3 + i + 1))
                        gd.skip(16)

            def odd():
                for h in range(2):
                    b = a_bank()
                    act.wait_ge(S("bf_in"), 16 * 5)
                    act.activation(FC[:, half(h)], b[0:16], ACT.Identity, bias=BF[:, :])
                    free(act.activation(FE[:, half(h)], b[0:16], ACT.Abs, bias=BF[:, :]))
                mine.wait_at(0)
                chain.done(act.activation(FE[:, :], FE[:, :], ACT.Exp, scale=-1.0))
                act.activation(FE[:, :], FE[:, :], ACT.Ln, bias=1.0).then_inc(S("fe_ready"), 1)
                act.wait_ge(S("fc_ready"), 1)
                act.dma_start(negf, FC[:, :]).then_inc(S("negf_out"), 16)
                act.wait_ge(S("negf_out"), 16)
                qs, qd = Tally(act, S("q_sum")), Tally(act, S("qn_done"))
                qkr = Tally(act, S("qkn_ready"))
                pn = Tally(act, S("p_ready"))
                pt4, od = Tally(act, S("pt4_done")), Tally(act, S("o_done"))
                ot = Tally(act, S("ot_done"))
                of = Tally(act, S("o_free"))
                with rounds(act, 8, (gd, 28), (mine, 12), (qs, 4), (qd, 4), (qkr, 4), (pn, 16), (pt4, 16), (od, 16),
                            (ot, 2), (of, 16)) as it:
                    for e in range(2):
                        act.dma_start(NF[:, e, :], negf[bass.ds(2 * it + e, 1), :].partition_broadcast(P)
                                      .rearrange("p a n -> p (a n)")).then_inc(S("nf_in"), 16)
                    for h in range(2):
                        for m, (th, src) in enumerate(((QH, 0), (KH, 1))):
                            i = (2 * h + m) % 2
                            b = a_bank()
                            qkr.take()
                            act.activation(QT[i][:, :], b, ACT.Copy)
                            free(act.activation(QSQ[:, :], b, ACT.Square))
                            qs.take()
                            act.activation(QRS[:, :], bank(6), ACT.Sqrt, bias=EPSR[:, :], scale=1.0 / 64)\
                                .then_inc(S("q_std"), 1)
                            qd.take()
                            act.activation(th[:, half(h)], QT[i][:, :], ACT.Copy).then_inc(S("qkh"), 1)
                    for t in range(NT):
                        b = a_bank()
                        act.activation(V[:, t, :], b[:, 0:P], ACT.Copy)
                        free(act.activation(G[:, t, :], b[:, P:2 * P], ACT.Sigmoid))
                    for n in range(2 * NT):
                        tb = n % NT
                        w = (tb + 1) * P
                        pn.take()
                        act.activation(PR[n % 2][:, 0:w], PR[n % 2][:, 0:w], ACT.Exp, bias=NMX[:, n:n + 1],
                                       accum_out=RSUM[:, n:n + 1]).then_inc(S("probs"), 1)
                        w4 = min(w, HALF)
                        pt4.take()
                        od.take()
                        act.activation(PT[n % 2][:, 0:w4], bank(4, w4), ACT.Copy).then_inc(S("pt_a"), 1)
                    of.take(16)
                    for g in range(2):
                        ot.take()
                        act.activation(PR[0][:, half(g)], bank(4 + g), ACT.Copy)
                        act.activation(QH[:, half(g)], bank(4 + g), ACT.Copy).then_inc(S("oth"), 1)
                    gd.skip(16)

            def spatial():
                act.wait_ge(S("u_ready1"), NK * 5)
                act.dma_start(WSR[:, :, :], A["w_spatial_2"].rearrange("h t s -> t h s")).then_inc(S("sp_in"), 16)
                act.dma_start(BROW[:, :], A["b_in_2"].rearrange("(a n) -> a n", a=1)[:, 512:1024])\
                    .then_inc(S("sp_in"), 16)
                act.dma_start(BS[:, :, :], A["b_spatial_2"].partition_broadcast(P)).then_inc(S("sp_in"), 16)
                for n, t in (("ln_a_g_2", LAG), ("ln_a_b_2", LAB)):
                    act.dma_start(t[:, :].rearrange("p (h d) -> p h d", h=4), A[n].partition_broadcast(P))\
                        .then_inc(S("sp_in"), 16)
                for t in range(2 * NT):
                    p, tt_ = t // NT, t % NT
                    free(act.activation(VS[:, tt_, 256 * p:256 * p + 256], a_bank()[:, 0:256], ACT.Gelu))
                act.wait_ge(S("va_var"), 1)
                act.activation(VR[:, :], MV[:, :, 1], ACT.Sqrt, bias=EPSL[:, :]).then_inc(S("va_std"), 1)
                ab = Tally(act, S("ab_used"))
                ty = Tally(act, S("ty_ready"))
                with rounds(act, 4, (gd, 24), (mine, 8), (ab, 2), (ty, 2)) as it:
                    for h in range(2):
                        ab.take()
                        bi = lambda j: PV[:, bass.ds(it + (pcol["b_in_2"] + j), 1)]
                        b = a_bank()
                        settle()
                        free(act.activation(AB[:, :], b, ACT.Identity, bias=bi(8)))
                        b = a_bank()
                        settle()
                        free(act.activation(GB[:, :], b, ACT.Sigmoid, bias=bi(12)))
                    for h in range(2):
                        b = a_bank()
                        settle()
                        free(act.activation(UU[:, half(h)], b, ACT.Gelu, bias=bi(0)))
                    for h in range(2):
                        free(act.activation(TY[h][:, :], a_bank(), ACT.Copy))
                    for h in range(2):
                        ty.take()
                        act.activation(SMH[:, half(h)], TY[h][:, :], ACT.Copy).then_inc(S("smh"), 1)
                    gd.skip(16)
                for h in range(2):
                    norm_std(4, lambda k, h: CX[:, k, half(h)], h)
                cx = Tally(act, S("cx_norm"))
                cx.take(8)
                sml = Tally(act, S("sm_ready"), 8 - 2)
                with rounds(act, 4, (gd, 16), (sml, 2), (chain_y, 2)) as it:
                    for h in range(2):
                        sml.take()
                        settle()
                        gb = lambda n: PV[:, bass.ds(it + pcol[n], 1)]
                        chain_y.done(act.activation(TY[h][:, :], CX[:, bass.ds(it, 1), half(h)]
                                                    .rearrange("p a n -> p (a n)"), ACT.Silu,
                                                    bias=gb("ln_b_b_2"), scale=gb("ln_b_g_2")))
                        if h == 0:
                            gd.wait_at(0)
                        act.activation(SMH[:, half(h)], TY[h][:, :], ACT.Copy).then_inc(S("smh"), 1)
                    gd.skip(16)

            chain_y = Chain(act, S("silu_chain"))

            def ffn():
                fc = Tally(act, S("conv_ready"))
                fp = Tally(act, S("prod_ready"))
                with rounds(act, D_FF2 // 256, (gd, 24), (mine, 8), (h_done, 4), (fc, 8), (fp, 4)) as it:
                    for h in range(2):
                        for m in range(4):
                            b = a_bank()
                            if m == 0:
                                h_done.take(2)
                            ch = lambda n, r: PV[:, bass.ds(it * 2 + (pcol[n] + 44 * r + (m if m < 2 else 20 + m)), 1)]
                            act.activation(FZ[:, m, 2:2 + HALF], b, ACT.Copy)
                            free(act.activation(FY[:, m, :], b, ACT.Identity, bias=ch("conv_f_b_2", 0),
                                                scale=ch("conv_f_w_2", 2)))
                        for m in range(2):
                            fc.take()
                            act.activation(FY[:, m, :], FY[:, m, :], ACT.Silu).then_inc(S("silu"), 1)
                        fc.skip(2)
                        for m in range(2):
                            fp.take()
                            act.activation(FH[:, m, half(h)], FY[:, m, :], ACT.Copy).then_inc(S("fh"), 1)
                    gd.skip(16)

            even()
            norm(vec("xg1"), vec("xb1"))
            mlp(0)
            norm(vec("xg2"), vec("xb2"))
            odd()
            norm(vec("xg3"), vec("xb3"))
            mlp(1)
            norm(vec("xg4"), vec("xb4"))
            spatial()
            norm(vec("xg5"), vec("xb5"))
            ffn()
            xn = Tally(act, S("xn"))
            for h in range(2):
                norm_std(NK, lambda k, h: X[:, k, half(h)], h)
                for k in range(NK):
                    xn.take()
                    x = X[:, k, half(h)]
                    act.activation(x, x, ACT.Identity, bias=pv("ln2_b_2", k), scale=pv("ln2_g_2", k))\
                        .then_inc(S("y_ready"), 1)
            for n in range(2 * NT):
                t = n // 2
                act.wait_ge(S("y_done"), n + 1)
                if t >= 2 and n % 2 == 0:
                    act.wait_ge(S(f"out_done{t % 2}"), 16 * (t // 2))
                act.activation(YO[t % 2][:, (n % 2) * HALF:(n % 2 + 1) * HALF], bank(n % 4), ACT.Copy)\
                    .then_inc(S("yo_ready"), 1)

        @block.vector
        def _(dve):
            gd = Tally(dve, S("gemm_done"))
            stat, uh, std = Tally(dve, S("stat_done")), Tally(dve, S("uh")), Tally(dve, S("std"))
            af = Tally(dve, S("a_free"), NA)
            mine = Tally(dve, S("d_free"), ND)
            x_ready = Tally(dve, S("x_ready"))
            chain = Chain(dve, S("dve_chain"))
            turn = [0]
            u_done = [Tally(dve, S(f"u_ready{h}")) for h in range(2)]
            half = lambda h: slice(h * HALF, (h + 1) * HALF)

            def d_bank():
                gd.take()
                turn[0] += 1
                return bank(NA + (turn[0] - 1) % ND)

            def free(ins):
                ins.then_inc(S("d_free"), 1)
                mine.skip()

            def add_x(gate, halves=(0, 1)):
                for h in halves:
                    for m in range(NK):
                        b = d_bank()
                        g = 1.0 if gate is None else MOD[:, gate, 16 + m:17 + m]
                        x = X[:, m, half(h)]
                        free(dve.scalar_tensor_tensor(out=x, in0=b, scalar=g, in1=x, op0=ALU.mult, op1=ALU.add))

            def tail(h, ug, ub, first=False):
                def rest(k):
                    uh.take()
                    dve.tensor_tensor(UL[:, k, half(h)], TU[k % 2][:, :], UH[:, k, half(h)].bitcast(F32),
                                      ALU.subtract).then_inc(S(f"u_ready{h}"), 1)
                    u_done[h].skip()
                for k in range(NK):
                    x = X[:, k, half(h)]
                    if first:
                        dve.wait_ge(S("xt_free"), h * NK + k + 1)
                        u_done[h if k else 0].wait_at(0)
                    else:
                        chain.done(dve.tensor_tensor(x, x, RST[:, :], ALU.mult))
                    dve.tensor_scalar(TU[k % 2][:, :], x, ug[:, k:k + 1], ub[:, k:k + 1], ALU.mult, ALU.add)\
                        .then_inc(S("tt"), 1)
                    if k:
                        rest(k - 1)
                rest(NK - 1)

            def centre(kt, tile_of, h):
                stat.take()
                for k in range(kt):
                    x = tile_of(k, h)
                    dve.scalar_tensor_tensor(out=x, in0=bank(6), scalar=-1.0 / (kt * P), in1=x,
                                             op0=ALU.mult, op1=ALU.add).then_inc(S("cen"), 1)
                std.take()
                chain.done(dve.reciprocal(RST[:, :], RST[:, :]))

            def norm(ug, ub):
                mine.wait_at(0)
                for h in range(2):
                    centre(NK, lambda k, h: X[:, k, half(h)], h)
                    tail(h, ug, ub)
                x_ready.take(2 * NK)

            ts = lambda out, a, s1, s2, o0, o1=None: chain.done(
                dve.tensor_scalar(out, a, s1, s2, o0, o1) if o1 is not None else dve.tensor_scalar(out, a, s1, s2, o0))
            tt = lambda out, a, b, op: chain.done(dve.tensor_tensor(out, a, b, op))

            def ln_vectors(n, mod, alpha, bias=None, gate=None):
                g, b = (pv("ln_g", (n - 1) * NK, NK), pv("ln_b", (n - 1) * NK, NK)) if n <= 4 else \
                    (pv("ln1_g_2", 0, NK), pv("ln1_b_2", 0, NK))
                ug, ub, xg, xb, t = (vec(f"{s}{n}") for s in ("ug", "ub", "xg", "xb", "tmp"))
                if mod is not None:
                    tt(ug, g, MOD[:, mod, 8:16], ALU.mult)
                    tt(ub, b, MOD[:, mod, 8:16], ALU.mult)
                    tt(ub, ub, MOD[:, mod, 0:8], ALU.add)
                ts(xg, g, alpha, None, ALU.mult)
                ts(xb, b, alpha, None, ALU.mult)
                if bias is not None:
                    if gate is not None:
                        tt(t, bias, MOD[:, gate, 16:24], ALU.mult)
                        bias = t
                    tt(xb, xb, bias, ALU.add)
                return (ug, ub) if mod is not None else (g, b)

            def modulation(l, src, a=0, b=24):
                ad = pv("ada_b", 24 * l + a, b - a)
                tt(MOD[:, l, a:b], src, ad, ALU.add)
                lo = max(a, 8)
                ts(MOD[:, l, lo:b], MOD[:, l, lo:b], 1.0, None, ALU.add)

            dve.sem_inc(S("d_free"), ND)
            dve.sem_inc(S("h_ready"), 2)
            dve.sem_inc(S("qkn_ready"), 2)
            dve.sem_inc(S("ab_used"), 1)
            chain.done(dve.memset(BLK[:, :], 0.0))
            for i in range(2):
                ins = dve.memset(BLK[64 * i:64 * i + 64, 64 * i:64 * i + 64], 1.0)
            chain.done(ins)
            dve.wait_ge(S("consts"), 1)
            chain.done(dve.memset(MASKG[0:64, 64:128], 0.0))
            dve.wait_ge(S("lam_e"), 1)
            lam, le, ll = pv("ev_rg_lam", 0, 4), vec("le", 4), vec("ll", 4)
            u, c = vec("lu", 4), vec("lc", 4)
            ts(u, le, 1.0, None, ALU.add)
            ts(c, u, 1.0, None, ALU.subtract)
            tt(c, le, c, ALU.subtract)
            chain.done(dve.reciprocal(u, u))
            tt(c, c, u, ALU.mult)
            tt(ll, ll, c, ALU.add)
            chain.done(dve.scalar_tensor_tensor(out=ll, in0=lam, scalar=0.0, in1=ll, op0=ALU.min, op1=ALU.subtract))
            ts(vec("lam8", 4), ll, 8.0, None, ALU.mult)
            dve.tensor_scalar(vec("lam8n", 4), ll, -8.0, None, ALU.mult).then_inc(S("lam_ready"), 1)
            dve.wait_ge(S("ada_done"), 2)
            modulation(0, bank(7)[:, 0:16], 0, 16)
            for h in range(2):
                tail(h, MOD[:, 0, 8:16], MOD[:, 0, 0:8], first=True)
            dve.wait_ge(S("ada_done"), 3)
            ad = pv("ada_b", 16, 8)
            tt(MOD[:, 0, 16:24], bank(6)[:, 16:24], ad, ALU.add)
            dve.tensor_scalar(MOD[:, 0, 16:24], MOD[:, 0, 16:24], 1.0, None, ALU.add).then_inc(S("mod_ready"), 1)
            dve.wait_ge(S("mod_ready"), 1)
            x_ready.take(2 * NK)
            dve.wait_ge(S("bf_in"), 16 * 5)
            dve.memset(XR[:, 0:3], 0.0)
            ts(QKG[:, 0:1], QKG[:, 0:1], 0.125, None, ALU.mult)

            def even():
                rga = Tally(dve, S("rg_a"))
                cch = Chain(dve, S("conv_chain"))

                def conv_and_gates(c):
                    pc = lambda n, j=0: PV[:, bass.ds(c + (pcol[n] + j), 1)]
                    for h in range(2):
                        af.take()
                        xc = XC[:, half(h)]
                        cch.done(dve.tensor_scalar(xc, XR[:, 3 + h * HALF:3 + h * HALF + HALF],
                                                   pc("ev_conv_w", 12), pc("ev_conv_b"), ALU.mult, ALU.add))
                        for k in range(2, -1, -1):
                            ins = dve.scalar_tensor_tensor(out=xc, in0=XR[:, k + h * HALF:k + h * HALF + HALF],
                                                           scalar=pc("ev_conv_w", 4 * k), in1=xc,
                                                           op0=ALU.mult, op1=ALU.add)
                            if k:
                                cch.done(ins)
                            else:
                                ins.then_inc(S("xc_ready"), 1)
                        af.take()

                def lru():
                    rga.take()
                    cch.done(dve.tensor_tensor(HS[:, :], AA[:, :], AA[:, :], ALU.mult))
                    dve.scalar_tensor_tensor(out=TH[:, :], in0=HS[:, :], scalar=1.0, in1=TH[:, :],
                                             op0=ALU.add, op1=ALU.mult).then_inc(S("lru"), 1)
                    af.take(4)
                    cch.done(dve.tensor_tensor(GI[:, :], GI[:, :], XC[:, :], ALU.mult))
                    rga.take()
                    cch.done(dve.tensor_tensor(GI[:, :], GI[:, :], TH[:, :], ALU.mult))
                    cch.done(dve.tensor_tensor_scan(HS[:, :], AA[:, :], GI[:, :], 0.0, ALU.mult, ALU.add))
                    dve.tensor_tensor(HS[:, :], HS[:, :], YG[:, :], ALU.mult).then_inc(S("lru"), 1)
                    rga.take()
                    dve.tensor_tensor(ML[:, :], HS[:, :], MH[:, :].bitcast(F32), ALU.subtract)\
                        .then_inc(S("m_ready"), 1)

                gd.skip(4)
                conv_and_gates(0)
                gd.skip(4)
                lru()
                with rounds(dve, 3, (gd, 24), (mine, 16), (rga, 3), (cch, 10), (af, 8)) as it:
                    gd.skip(4)
                    conv_and_gates(it + 1)
                    add_x(0)
                    gd.skip(4)
                    lru()
                add_x(0)

                exps, gmh = Tally(dve, S("exps")), Tally(dve, S("gmh"))
                gst = Tally(dve, S("gla_std"))
                chain.done(dve.memset(CHM[:, :], 1.0))
                chain.done(dve.memset(CHM[:, ::GLA_CHUNK], 0.0))
                for p in range(2):
                    if p == 0:
                        gd.skip(2)
                        af.skip(2)
                    gd.skip(14)
                    af.skip(2)
                    dve.wait_ge(S("z_ready"), p + 1)
                    chain.done(dve.scalar_tensor_tensor(out=B[0][:, :], in0=B[0][:, :], scalar=0.0, in1=B[3][:, :],
                                                        op0=ALU.min, op1=ALU.subtract))
                    for h in range(2):
                        chain.done(dve.tensor_tensor_scan(B[1][:, half(h)], CHM[:, :], B[0][:, half(h)], 0.0,
                                                          ALU.mult, ALU.add))
                    v16 = lambda t: t[:, :].rearrange("p (n s) -> p n s", s=GLA_CHUNK)
                    last = v16(B[1])[:, :, 63:64].broadcast_to([P, 16, GLA_CHUNK])
                    dve.tensor_tensor(v16(B[4]), last, v16(B[1]), ALU.subtract).then_inc(S("gl"), 1)
                    exps.take()
                    af.take(4)
                    dve.tensor_tensor(B[5][:, :], B[5][:, :], B[2][:, :], ALU.mult).then_inc(S("qk_ready"), 1)
                    dve.tensor_tensor(B[3][:, :], B[6][:, :], B[3][:, :], ALU.mult).then_inc(S("qk_ready"), 1)
                    dve.tensor_tensor(B[4][:, :], B[6][:, :], B[4][:, :], ALU.mult).then_inc(S("qk_ready"), 1)
                    for g in range(2):
                        free(dve.tensor_copy(B[6][:, half(g)], d_bank()))
                    for hh in range(2):
                        for g in range(2):
                            b = d_bank()
                            free(dve.tensor_tensor(ATT[:, hh, 4 * g:4 * g + 4, :],
                                                   b.rearrange("p (t c) -> p t c", t=4),
                                                   MASKG[:, :].unsqueeze(1).broadcast_to([P, 4, P]), ALU.mult))
                    chain.done(dve.memset(STT_[:, 0, :], 0.0))
                    for q in range(4):
                        banks = (d_bank(), d_bank())
                        for i in range(4):
                            n = 4 * q + i
                            if n == 15:
                                dve.sem_inc(S("d_free"), 1)
                                mine.skip()
                                break
                            for hh in range(2):
                                r = slice(64 * hh, 64 * hh + 64)
                                ins = dve.scalar_tensor_tensor(
                                    out=STT_[r, n + 1, :], in0=STT_[r, n, :], scalar=DEC[r, n:n + 1],
                                    in1=banks[i % 2][r, (i // 2) * 256 + hh * P:(i // 2) * 256 + (hh + 1) * P],
                                    op0=ALU.mult, op1=ALU.add)
                            if i < 2:
                                chain.done(ins)
                            else:
                                free(ins)
                                mine.wait_at(0)
                    af.skip(8)
                    gd.skip(4)
                    af.take(4)
                    for hh in range(2):
                        gd.skip(2)
                        for h in range(2):
                            af.take()
                            gst.take()
                            chain.done(dve.reciprocal(GRS[:, :], GRS[:, :]))
                            chain.done(dve.scalar_tensor_tensor(out=OO[h][:, :], in0=OO[h][:, :],
                                                                scalar=pv("ev_gla_norm_g", 2 * p + hh),
                                                                in1=B[2 + hh][:, half(h)], op0=ALU.mult, op1=ALU.mult))
                            dve.tensor_tensor(OO[h][:, :], OO[h][:, :], GRS[:, :], ALU.mult).then_inc(S("gla_o"), 1)
                            gmh.take()
                            dve.tensor_tensor(GML[:, half(h)], OO[h][:, :], GMH[:, half(h)].bitcast(F32),
                                              ALU.subtract).then_inc(S("m_ready"), 1)
                        add_x(0)

            hh_ready = Tally(dve, S("hh_ready"))

            def mlp(l, gate):
                with rounds(dve, 8, (gd, 40), (mine, 32), (hh_ready, 8)) as it:
                    for q in range(2):
                        gd.skip(4)
                        for h in range(2):
                            for m in range(2):
                                hh_ready.take()
                                dve.tensor_tensor(HL[:, m, half(h)], SQ[(2 * h + m) % 2][:, :],
                                                  HH[:, m, half(h)].bitcast(F32), ALU.subtract)\
                                    .then_inc(S("h_ready"), 1)
                        add_x(gate)
                af.skip(64)

            def odd():
                dve.wait_ge(S("fe_ready"), 1)
                chain.done(dve.scalar_tensor_tensor(out=FE[:, :], in0=FC[:, :], scalar=0.0, in1=FE[:, :],
                                                    op0=ALU.min, op1=ALU.subtract))
                dve.tensor_tensor_scan(FC[:, :], ONES[0:16, 0:1].broadcast_to([16, SEQ]), FE[:, :], 0.0,
                                       ALU.mult, ALU.subtract).then_inc(S("fc_ready"), 1)
                gd.skip(2)
                qst, qkh = Tally(dve, S("q_std")), Tally(dve, S("qkh"))
                nf = Tally(dve, S("nf_in"))
                sd, sf = Tally(dve, S("s_done")), Tally(dve, S("s_free"))
                pt4, pt5 = Tally(dve, S("pt4_done")), Tally(dve, S("pt5_done"))
                od = Tally(dve, S("o_done"), 2)
                oth = Tally(dve, S("oth"))
                och = Chain(dve, S("odd_chain"))
                with rounds(dve, 8, (gd, 28), (mine, 16), (qst, 4), (qkh, 4), (nf, 32), (sd, 16), (sf, 16), (pt4, 16),
                            (pt5, 8), (od, 16), (oth, 2), (och, 20)) as it:
                    for h in range(2):
                        for m, (th, tl) in enumerate(((QH, QL), (KH, KL))):
                            t = QT[m]
                            qst.take()
                            och.done(dve.reciprocal(QRS[:, :], QRS[:, :]))
                            dve.scalar_tensor_tensor(out=t[:, :], in0=t[:, :], scalar=QKG[:, m:m + 1],
                                                     in1=QRS[:, :], op0=ALU.mult, op1=ALU.mult)\
                                .then_inc(S("qn_done"), 1)
                            qkh.take()
                            dve.tensor_tensor(tl[:, half(h)], t[:, :], th[:, half(h)].bitcast(F32),
                                              ALU.subtract).then_inc(S("qkn_ready"), 1)
                    nf.take(32)
                    gd.skip(12)

                    def scores(n):
                        hh, tb = n // NT, n % NT
                        w = (tb + 1) * P
                        b = 2 * (n % 2)
                        sd.take()
                        dve.sem_inc(S("ttr_turn"), 1)
                        dve.tensor_tensor_reduce(out=PR[n % 2][:, 0:w], in0=PS[:, b * HALF:b * HALF + w],
                                                 in1=NF[:, hh, 0:w], scale=1.0, scalar=-3.0e38, op0=ALU.add,
                                                 op1=ALU.max, accum_out=MXT[:, n:n + 1]).then_inc(S("s_free"), 1)
                        sf.take()
                        dve.tensor_scalar(NMX[:, n:n + 1], MXT[:, n:n + 1], -1.0, None, ALU.mult)\
                            .then_inc(S("p_ready"), 1)

                    scores(0)
                    scores(1)
                    for n in range(2 * NT):
                        hh, tb = n // NT, n % NT
                        w = (tb + 1) * P
                        pt4.take()
                        if tb >= 4:
                            pt5.take()
                            dve.tensor_copy(PT[n % 2][:, HALF:w], PS[:, 5 * HALF:5 * HALF + w - HALF])\
                                .then_inc(S("pt_d"), 1)
                        if n + 2 < 2 * NT:
                            scores(n + 2)
                        od.take()
                        och.done(dve.reciprocal(RINV[:, n:n + 1], RSUM[:, n:n + 1]))
                        g = G[:, tb, 64 * hh:64 * hh + 64]
                        dve.scalar_tensor_tensor(out=g, in0=bank(6 + n % 2, 64), scalar=RINV[:, n:n + 1],
                                                 in1=g, op0=ALU.mult, op1=ALU.mult).then_inc(S("o_free"), 1)
                    for g in range(2):
                        oth.take()
                        dve.tensor_tensor(QL[:, half(g)], PR[0][:, half(g)], QH[:, half(g)].bitcast(F32),
                                          ALU.subtract).then_inc(S("ot_ready"), 1)
                    add_x(2)
                af.skip(2 + 8 * 12)

            def spatial():
                dve.wait_ge(S("wst_done"), 1)
                dve.wait_ge(S("sp_in"), 16 * 5)
                chain.done(dve.tensor_tensor(WST[:, :, :], bank(6).rearrange("p (h t) -> p h t", h=4),
                                             MASKC[:, :].unsqueeze(1).broadcast_to([P, 4, P]), ALU.mult))
                gd.skip(16)
                for p in range(2):
                    for t in range(NT):
                        af.take()
                        for e in range(2):
                            hh = 2 * p + e
                            ins = dve.bn_stats(BST[:, 4 * t + hh, :], VS[:, t, hh * P:(hh + 1) * P])
                chain.done(ins)
                for j in range(32):
                    ins = dve.bn_aggr(MV[:, j, :], BST[:, j, :])
                ins.then_inc(S("va_var"), 1)
                dve.wait_ge(S("va_std"), 1)
                chain.done(dve.reciprocal(VR[:, :], VR[:, :]))
                for j in range(32):
                    v = VS[:, j // 4, (j % 4) * P:(j % 4 + 1) * P]
                    ins = dve.tensor_scalar(v, v, MV[:, j, 0:1], VR[:, j:j + 1], ALU.subtract, ALU.mult)
                chain.done(ins)
                dve.memset(YB[:, 0:CONV_PAD], 0.0)
                smh = Tally(dve, S("smh"))
                sch = Chain(dve, S("sp_chain"))
                with rounds(dve, 4, (gd, 24), (mine, 16), (af, 8), (smh, 2), (sch, 33)) as it:
                    g = lambda t: t[:, bass.ds(it * P, P)].unsqueeze(1).broadcast_to([P, NT, P])
                    sch.done(dve.tensor_tensor(VH[:, :, :], VS[:, :, bass.ds(it * P, P)], g(LAG), ALU.mult))
                    dve.tensor_tensor(VH[:, :, :], VH[:, :, :], g(LAB), ALU.add).then_inc(S("vh_ready"), 1)
                    for h in range(2):
                        af.take(2)
                        dve.tensor_tensor(YB[:, CONV_PAD + h * HALF:CONV_PAD + (h + 1) * HALF], AB[:, :], GB[:, :],
                                          ALU.mult).then_inc(S("ab_used"), 1)
                    af.take(4)
                    gd.skip(8)
                    for h in range(2):
                        t4 = TY[h][:, :].rearrange("p (c t) -> p c t", c=4)
                        sch.done(dve.tensor_tensor(t4, t4, BS[:, bass.ds(it, 1), :].broadcast_to([P, 4, P]), ALU.add))
                        dve.tensor_tensor(TY[h][:, :], TY[h][:, :], UU[:, half(h)], ALU.mult)\
                            .then_inc(S("ty_ready"), 1)
                    for h in range(2):
                        smh.take()
                        dve.tensor_tensor(SML[:, half(h)], TY[h][:, :], SMH[:, half(h)].bitcast(F32),
                                          ALU.subtract).then_inc(S("sm_ready"), 1)
                    add_x(None)
                    cx = CX[:, bass.ds(it, 1), :].rearrange("p a n -> p (a n)")
                    pc = lambda n, j=0: PV[:, bass.ds(it + (pcol[n] + j), 1)]
                    sch.done(dve.tensor_scalar(cx, YB[:, CONV_PAD:CONV_PAD + SEQ], pc("conv_b_w_2", 4 * CONV_PAD),
                                               pc("conv_b_b_2"), ALU.mult, ALU.add))
                    for k in range(CONV_PAD):
                        ins = dve.scalar_tensor_tensor(out=cx, in0=YB[:, k:k + SEQ], scalar=pc("conv_b_w_2", 4 * k),
                                                       in1=cx, op0=ALU.mult, op1=ALU.add)
                        if k < CONV_PAD - 1:
                            sch.done(ins)
                        else:
                            ins.then_inc(S("cx_ready"), 1)
                dve.wait_ge(S("cx_ready"), 4)
                for h in range(2):
                    centre(4, lambda k, h: CX[:, k, half(h)], h)
                    for k in range(4):
                        c = CX[:, k, half(h)]
                        dve.tensor_tensor(c, c, RST[:, :], ALU.mult).then_inc(S("cx_norm"), 1)
                with rounds(dve, 4, (gd, 16), (mine, 16), (smh, 2)) as it:
                    for h in range(2):
                        smh.take()
                        dve.tensor_tensor(SML[:, half(h)], TY[h][:, :], SMH[:, half(h)].bitcast(F32),
                                          ALU.subtract).then_inc(S("sm_ready"), 1)
                    add_x(None)

            def ffn():
                for m in range(4):
                    ins = dve.memset(FZ[:, m, 0:2], 0.0)
                chain.done(ins)
                silu, fh = Tally(dve, S("silu")), Tally(dve, S("fh"))
                fch = Chain(dve, S("ffn_chain"))
                conv = Tally(dve, S("conv_ready"))
                with rounds(dve, D_FF2 // 256, (gd, 24), (conv, 8), (mine, 16), (af, 8), (silu, 4), (fh, 4), (fch, 16)) as it:
                    for h in range(2):
                        for m in range(4):
                            af.take()
                            w = lambda r: PV[:, bass.ds(it * 2 + (pcol["conv_f_w_2"] + 44 * r + (m if m < 2 else 20 + m)), 1)]
                            y = FY[:, m, :]
                            fch.done(dve.scalar_tensor_tensor(out=y, in0=FZ[:, m, 1:1 + HALF], scalar=w(1), in1=y,
                                                              op0=ALU.mult, op1=ALU.add))
                            dve.scalar_tensor_tensor(out=y, in0=FZ[:, m, 0:HALF], scalar=w(0), in1=y,
                                                     op0=ALU.mult, op1=ALU.add).then_inc(S("conv_ready"), 1)
                            conv.take()
                            if h == 0:
                                fch.done(dve.tensor_copy(FZ[:, m, 0:2], FZ[:, m, HALF:HALF + 2]))
                            else:
                                fch.done(dve.memset(FZ[:, m, 0:2], 0.0))
                        for m in range(2):
                            silu.take()
                            dve.tensor_tensor(FY[:, m, :], FY[:, m, :], FY[:, 2 + m, :], ALU.mult)\
                                .then_inc(S("prod_ready"), 1)
                        for m in range(2):
                            fh.take()
                            dve.tensor_tensor(FL[:, m, half(h)], FY[:, m, :], FH[:, m, half(h)].bitcast(F32),
                                              ALU.subtract).then_inc(S("h_ready"), 1)
                    gd.skip(8)
                    add_x(None)

            even()
            dve.wait_ge(S("ada_done"), 3 + 24)
            modulation(1, bank(7)[:, 0:24])
            dve.sem_inc(S("mod_ready"), 1)
            norm(*ln_vectors(1, 1, ALPHA_1, pv("mlp_b2", 0, NK), 1))
            mlp(0, 1)
            dve.wait_ge(S("ada_done"), 3 + 24 + 48)
            modulation(2, bank(7)[:, 0:24])
            modulation(3, bank(7)[:, 24:48])
            dve.sem_inc(S("mod_ready"), 1)
            norm(*ln_vectors(2, 2, ALPHA_1))
            odd()
            norm(*ln_vectors(3, 3, ALPHA_1, pv("mlp_b2", NK, NK), 3))
            mlp(1, 3)
            norm(*ln_vectors(4, None, ALPHA_2, pv("b_out_2", 0, NK)))
            spatial()
            norm(*ln_vectors(5, None, ALPHA_2))
            ffn()
            mine.wait_at(0)
            for h in range(2):
                centre(NK, lambda k, h: X[:, k, half(h)], h)
                for k in range(NK):
                    x = X[:, k, half(h)]
                    dve.tensor_tensor(x, x, RST[:, :], ALU.mult).then_inc(S("xn"), 1)

        @block.sync
        def _(sp):
            xin = A["x"].rearrange("a (t p) d -> p (a t) d", p=P)
            for h in range(2):
                sp.dma_start(XIN[:, 4 * h:4 * h + 4, :], xin[:, 4 * h:4 * h + 4, :]).then_inc(S(f"x_in{h}"), 16)
            sp.wait_ge(S("prow_zero"), 1)
            for n, ap in prow.items():
                done = 0
                while done < ap.shape[0]:
                    r = pcol[n] + done
                    k = min(ap.shape[0] - done, P - r % P)
                    sp.dma_start(PROW[r % P:r % P + k, r // P, :], ap[done:done + k, :]).then_inc(S("prow_in"), 16)
                    done += k
            ada = A["ada_w"][0, 0].rearrange("(k p) m -> p k m", p=P)
            for i, t in enumerate((ADS, ADC)):
                sp.dma_start(t[:, :, :], ada[:, :, i * D:(i + 1) * D]).then_inc(S(f"ada0_in{i}"), 16)
            ready = S("w_ready")
            for ph in plan.order:
                T = len(ph["tiles"])

                def load(it):
                    for j, (src, _, _) in enumerate(ph["tiles"]):
                        v = ph["W"] + ph["raws"][j]
                        if ph["count"] > 1:
                            assert v > 0
                            sp.wait_ge(ready, it * T + v)
                        elif v > 0:
                            sp.wait_ge(ready, v)
                        sp.sem_inc(S("load_turn"), 1)
                        for dst, ap in src(it, RAW[j % NRAW]):
                            sp.dma_start(dst, ap).then_inc(S(f"raw_in{j % NRAW}"), 16)

                if ph["count"] > 1:
                    with sp.Fori(0, ph["count"]) as it:
                        load(it)
                else:
                    load(0)
            orow = out.rearrange("a (t p) d -> (a t) p d", p=P)
            for t in range(NT):
                sp.wait_ge(S("yo_ready"), 2 * t + 2)
                sp.dma_start(orow[t], YO[t % 2][:, :]).then_inc(S(f"out_done{t % 2}"), 16)
            for i in range(2):
                sp.wait_ge(S(f"out_done{i}"), 16 * NT // 2)

        @block.gpsimd
        def _(pool):
            chain = Chain(pool, S("pool_chain"))
            pool.memset(PROW[:, n_ptile - 1, :], 0.0).then_inc(S("prow_zero"), 1)
            for t, v in ((IDENT, 0.0), (ONES, 1.0), (MASKC, 1.0), (MASKG, 1.0), (MASKA, 0.0),
                         (EPSL, LN_EPS), (EPSR, RMS_EPS), (WGA, 0.0), (WGX, 0.0)):
                ins = pool.memset(t[:, :], v)
            chain.done(ins)
            ins = pool.affine_select(out=IDENT[:, :], in_=IDENT[:, :], compare_op=ALU.not_equal, fill=1.0, base=0,
                                     pattern=[[-1, P]], channel_multiplier=1)
            ins = pool.affine_select(out=MASKC[:, :], in_=MASKC[:, :], compare_op=ALU.is_ge, fill=0.0, base=0,
                                     pattern=[[1, P]], channel_multiplier=-1)
            ins = pool.affine_select(out=MASKA[:, :], in_=MASKA[:, :], compare_op=ALU.is_ge, fill=NEG, base=0,
                                     pattern=[[-1, P]], channel_multiplier=1)
            pool.affine_select(out=MASKG[:, :], in_=MASKG[:, :], compare_op=ALU.is_ge, fill=0.0, base=0,
                               pattern=[[1, P]], channel_multiplier=-1).then_inc(S("consts"), 1)

            raw = [Tally(pool, S(f"raw_in{i}")) for i in range(NRAW)]
            hi = Tally(pool, S("w_hi"))
            for ph in plan.order:
                T = len(ph["tiles"])

                def split(it):
                    for j, (src, _, slot) in enumerate(ph["tiles"]):
                        r = RAW[j % NRAW]
                        parts = src(0, r)
                        raw[j % NRAW].take(16 * len(parts))
                        v = ph["I"] + ph["free"][j]
                        if ph["count"] > 1:
                            assert v > 0
                            pool.wait_ge(S("gemm_done"), it * ph["items"] + v)
                        elif v > 0:
                            pool.wait_ge(S("gemm_done"), v)
                        pool.sem_inc(S("split_turn"), 1)
                        n = sum(int(np.prod(d.shape[1:])) for d, _ in parts)
                        pool.tensor_scalar(WH[slot][:, 0:n], r[:, 0:n], 1.0, None, ALU.mult).then_inc(S("w_hi"), 1)
                        hi.take()
                        pool.tensor_tensor(WL[slot][:, 0:n], r[:, 0:n], WH[slot][:, 0:n].bitcast(F32),
                                           ALU.subtract).then_inc(ready, 1)

                ready = S("w_ready")
                if ph["count"] > 1:
                    per = [16 * sum(len(t[0](0, RAW[0])) for j, t in enumerate(ph["tiles"]) if j % NRAW == i)
                           for i in range(NRAW)]
                    pairs = [(raw[i], per[i]) for i in range(NRAW) if per[i]] + [(hi, T)]
                    with rounds(pool, ph["count"], *pairs) as it:
                        split(it)
                else:
                    split(0)


_INS = ["x", "c", "ada_w", "ada_b", "ln_g", "ln_b", "ev_w_in", "ev_conv_w", "ev_conv_b", "ev_rg_wa", "ev_rg_ba",
        "ev_rg_wx", "ev_rg_bx", "ev_rg_lam", "ev_gla_w_up", "ev_gla_b_up", "ev_gla_norm_g", "ev_w_out", "od_w_in",
        "od_b_f", "od_q_norm_g", "od_k_norm_g", "od_w_out", "mlp_w1", "mlp_b1", "mlp_w2", "mlp_b2", "w_in_2", "b_in_2",
        "ln_a_g_2", "ln_a_b_2", "w_spatial_2", "b_spatial_2", "conv_b_w_2", "conv_b_b_2", "ln_b_g_2", "ln_b_b_2",
        "w_out_2", "b_out_2", "ln1_g_2", "ln1_b_2", "w_up_2", "conv_f_w_2", "conv_f_b_2", "w_down_2", "ln2_g_2",
        "ln2_b_2"]
_OUTS = [((1, 1024, 1024), "float32")]


def kernel(**inputs):
    import numpy as _np
    import concourse.bacc as _bacc
    from concourse import mybir as _mybir
    from concourse.bass_utils import run_bass_kernel_spmd as _run

    nc = _bacc.Bacc("TRN2", target_bir_lowering=False, num_devices=1)
    arrays, aps = {}, {}
    for name in _INS:
        a = _np.ascontiguousarray(inputs[name])
        arrays[f"in_{name}_dram"] = a
        aps[name] = nc.dram_tensor(f"in_{name}_dram", a.shape, _mybir.dt.from_np(a.dtype), kind="ExternalInput").ap()
    shape, dtype = _OUTS[0]
    out = nc.dram_tensor("out_0_dram", shape, _mybir.dt.from_np(_np.dtype(dtype)), kind="ExternalOutput").ap()
    build(nc, aps, out)
    r = _run(nc, [arrays], core_ids=[0])
    return _np.array(r.results[0]["out_0_dram"])
```

```python
from contextlib import ExitStack, contextmanager

import numpy as np

import concourse.bass as bass
from concourse import mybir

F32 = mybir.dt.float32
F32R = mybir.dt.float32r
ALU = mybir.AluOpType
ACT = mybir.ActivationFunctionType

P = 128
D = 1024
SEQ = 1024
HALF = 512
NK = D // P
NT = SEQ // P
ALPHA_1 = 4.0 ** 0.25
ALPHA_2 = 2.0 ** 0.25
LN_EPS = 1e-5
RMS_EPS = 1e-6
D_FF = 4096
FF_GROUP = 256
D_FF2 = 2816
RG = 512
GLA_CHUNK = 64
NEG = -1e30
NA, ND = 2, 4
CONV_B = 31
CONV_PAD = CONV_B - 1
POOL_TAPS = 3


class Tally:

    def __init__(self, eng, sem, start=0):
        self.eng, self.sem, self.n, self.it, self.per, self.j = eng, sem, start, None, 0, 0

    def enter(self, it, per):
        self.it, self.per, self.j = it, per, 0

    def leave(self, count):
        assert self.j == self.per, (self.sem, self.j, self.per)
        self.n += count * self.per
        self.it, self.j = None, 0

    def wait_at(self, k):
        v = self.n + self.j + k
        if self.it is None:
            if v > 0:
                self.eng.wait_ge(self.sem, v)
        elif self.per == 0:
            if v > 0:
                self.eng.wait_ge(self.sem, v)
        else:
            assert v > 0, (self.sem, v)
            self.eng.wait_ge(self.sem, self.it * self.per + v)

    def skip(self, k=1):
        self.j += k
        if self.it is None:
            self.n, self.j = self.n + self.j, 0

    def take(self, k=1):
        self.skip(k)
        self.wait_at(0)


class Chain:

    def __init__(self, eng, sem):
        self.t = Tally(eng, sem)

    def done(self, ins):
        ins.then_inc(self.t.sem, 1)
        self.t.take()


@contextmanager
def rounds(eng, count, *pairs):
    with eng.Fori(0, count) as it:
        for t, per in pairs:
            (t.t if isinstance(t, Chain) else t).enter(it, per)
        yield it
        for t, per in pairs:
            (t.t if isinstance(t, Chain) else t).leave(count)


def param_rows(A):
    r = lambda ap: ap.rearrange("(r q) -> r q", q=P)
    out = {}
    out["c"] = r(A["c"].rearrange("a d -> (a d)"))
    out["ada_b"] = r(A["ada_b"].rearrange("l j n -> (l j n)"))
    out["ln_g"] = r(A["ln_g"].rearrange("l j n -> (l j n)"))
    out["ln_b"] = r(A["ln_b"].rearrange("l j n -> (l j n)"))
    for n in ("ev_conv_b", "ev_rg_ba", "ev_rg_bx", "ev_rg_lam", "ev_gla_b_up", "ev_gla_norm_g", "mlp_b1", "mlp_b2"):
        out[n] = r(A[n].rearrange("l n -> (l n)"))
    out["ev_conv_w"] = r(A["ev_conv_w"].rearrange("l t n -> (l t n)"))
    for n in ("b_in_2", "conv_b_b_2", "ln_b_g_2", "ln_b_b_2", "b_out_2", "ln1_g_2", "ln1_b_2", "ln2_g_2",
              "ln2_b_2", "conv_f_b_2"):
        out[n] = r(A[n])
    out["conv_b_w_2"] = r(A["conv_b_w_2"].rearrange("t n -> (t n)"))
    out["conv_f_w_2"] = r(A["conv_f_w_2"].rearrange("t n -> (t n)"))
    return out


class Plan:

    def __init__(self):
        self.phases, self.order = {}, []
        self.items = self.tiles = 0
        self.slot_need = {}
        self.raw_last = {}

    def add(self, name, count, tiles, items):
        ph = dict(name=name, count=count, tiles=tiles, items=items, I=self.items, W=self.tiles)
        T = len(tiles)
        free, first, raws = [], [], []
        last_by_slot = {}
        for j, (_, last, slot) in enumerate(tiles):
            before = self.slot_need.get(slot, 0) - self.items
            if slot in last_by_slot:
                free.append(last_by_slot[slot] + 1)
                first.append(last_by_slot[slot] + 1)
            else:
                own = [l for _, l, s in tiles if s == slot][-1]
                free.append(own + 1 - items)
                first.append(before)
            last_by_slot[slot] = last
        for j in range(T):
            r = j % NRAW
            before = self.raw_last.get(r, -1) + 1 - self.tiles
            if j >= NRAW:
                raws.append(j - NRAW + 1)
            else:
                own = max(q for q in range(T) if q % NRAW == r)
                raws.append(max(before, own + 1 - T) if count > 1 else before)
        ph["free"], ph["first"], ph["raws"] = free, first, raws
        for slot, last in last_by_slot.items():
            self.slot_need[slot] = self.items + (count - 1) * items + last + 1
        for j in range(T):
            self.raw_last[j % NRAW] = self.tiles + (count - 1) * T + j
        self.items += count * items
        self.tiles += count * T
        self.phases[name] = ph
        self.order.append(ph)

    def claim(self, slots):
        for s in slots:
            self.slot_need[s] = self.items


NRAW = 2


def build(nc, A, out):
    ctx = ExitStack()
    with ctx:
        base = 16512
        end = nc.sbuf_usable_end

        def at(name, shape, offset, dt=F32):
            size = int(np.prod(shape[1:])) * 4
            assert offset + size <= end, (name, offset + size, end)
            return nc.alloc_sbuf_tensor_at(name, shape, dt, offset=offset)

        KB = 1024
        X = at("X", [P, NK, SEQ], base)
        UH = at("UH", [P, NK, SEQ], base + 32 * KB, F32R)
        UL = at("UL", [P, NK, SEQ], base + 64 * KB, F32R)
        o = base + 96 * KB
        PV_W = 768
        names = {}

        def small(name, shape, dt=F32):
            nonlocal o
            t = at(name, shape, o, dt)
            o += (int(np.prod(shape[1:])) * 4 + 31) // 32 * 32
            return t

        PV = small("PV", [P, PV_W])
        VEC = small("VEC", [P, 40 * NK])
        MOD = small("MOD", [P, 4, 24])
        IDENT = small("IDENT", [P, P])
        ONES = small("ONES", [P, P])
        BLK = small("BLK", [P, P])
        MASKC = small("MASKC", [P, P])
        CS = small("CS", [P, NK])
        EPSL = small("EPSL", [P, 1])
        EPSR = small("EPSR", [P, 1])
        QKG = small("QKG", [P, 2])
        MASKA = small("MASKA", [P, P])
        MXT, NMX, RSUM, RINV = (small(n, [P, 16]) for n in ("MXT", "NMX", "RSUM", "RINV"))
        BF = small("BF", [16, 1])
        RAW = [at(f"RAW{i}", [P, 1024], o + 4 * KB * i) for i in range(NRAW)]
        o += 4 * KB * NRAW
        slot0 = o
        WH = [at(f"WH{i}", [P, 1024], o + 8 * KB * i, F32R) for i in range(8)]
        WL = [at(f"WL{i}", [P, 1024], o + 8 * KB * i + 4 * KB, F32R) for i in range(8)]
        scr = {n: slot0 + 8 * KB * n for n in range(9)}

        PS = nc.alloc_psum_tensor("PS", [P, 8 * HALF], F32)
        bank = lambda i, w=HALF: PS[:, i * HALF:i * HALF + w]

        sems = {}

        def S(name):
            if name not in sems:
                sems[name] = ctx.enter_context(nc.semaphore(name))
            return sems[name]

        prow = param_rows(A)
        pcol, r = {}, 0
        for n, ap in prow.items():
            pcol[n] = r
            r += ap.shape[0]
        n_prow = r
        n_ptile = (n_prow + P - 1) // P
        assert n_ptile * P <= PV_W

        def pv(name, j=0, w=1):
            return PV[:, pcol[name] + j:pcol[name] + j + w]

        vcol = {}

        def vec(name, w=NK):
            if name not in vcol:
                vcol[name] = (sum(x for _, x in vcol.values()), w)
                assert vcol[name][0] + w <= 40 * NK
            a, w = vcol[name]
            return VEC[:, a:a + w]

        plan = Plan()
        view3 = lambda t, k: t[:, :].rearrange("p (k m) -> p k m", k=k)

        def cols(w, m0, width=P):
            return w.rearrange("(k p) m -> p k m", p=P)[:, :, bass.ds(m0, width)]

        def rows2(w, k0, n, m0, width):
            return w.rearrange("(k p) m -> p k m", p=P)[:, bass.ds(k0, n), m0:m0 + width]

        def tile_m(w, m0_of, width=P):
            if width == P:
                return lambda it, r: [(view3(r, NK), cols(w, m0_of(it)))]
            return lambda it, r: [(r[:, 0:NK * width].rearrange("p (k m) -> p k m", k=NK), cols(w, m0_of(it), width))]

        def tile_row(w, k_of):
            return lambda it, r: [(view3(r, 1), rows2(w, k_of(it), 1, 0, D))]

        def tile_t(w, k0, starts):
            w_ = 256 // len(starts)
            return lambda it, r: [(view3(r, 4)[:, :, i * w_:(i + 1) * w_],
                                   w.rearrange("(k p) m -> p k m", p=P)[:, k0:k0 + 4, bass.ds(s(it), w_)])
                                  for i, s in enumerate(starts)]

        ev_in, ev_out = A["ev_w_in"][0], A["ev_w_out"][0]
        od_in, od_out = A["od_w_in"][0], A["od_w_out"][0]

        def plan_even():
            xr = lambda d: tile_m(ev_in, lambda it: (it + d) * P)
            yr = lambda d: tile_m(ev_in, lambda it: (it + d) * P + RG)
            wo = lambda d: tile_row(ev_out, lambda it: it + d)
            plan.add("rg_first", 1, [(xr(0), 2, 0), (yr(0), 3, 1)], 8)
            plan.add("rg", 3, [(xr(1), 2, 0), (yr(1), 3, 1), (wo(0), 19, 2)], 24)
            plan.add("rg_last", 1, [(wo(3), 15, 0)], 16)
            q0, k0, v0, g0, z0 = 2 * RG, 2 * RG + 256, 2 * RG + 512, 2 * RG + 1024, 2 * RG + 1536
            slot = 0
            for p in range(2):
                I = 0
                tiles = []

                def t(src, last):
                    nonlocal slot
                    tiles.append((src, last, slot % 3))
                    slot += 1

                if p == 0:
                    t(tile_m(ev_in, lambda it: z0, 16), 1)
                    I += 2
                I += 2
                t(tile_m(ev_in, lambda it, p=p: q0 + p * P), I + 1)
                t(tile_m(ev_in, lambda it, p=p: k0 + p * P), I + 3)
                I += 4
                t(tile_t(ev_in, 0, [lambda it, p=p: v0 + p * 256]), I + 7)
                t(tile_t(ev_in, 4, [lambda it, p=p: v0 + p * 256]), I + 7)
                I += 8
                I += 2 + 4 + 8
                t(tile_m(ev_in, lambda it, p=p: g0 + 2 * p * P), I + 1)
                t(tile_m(ev_in, lambda it, p=p: g0 + (2 * p + 1) * P), I + 3)
                I += 4
                t(tile_row(ev_out, lambda it, p=p: 4 + 2 * p), I + 19)
                t(tile_row(ev_out, lambda it, p=p: 5 + 2 * p), I + 35)
                plan.add(f"gla{p}", 1, tiles, I + 36)

        def plan_mlp(l):
            w1, w2 = A["mlp_w1"][l], A["mlp_w2"][l]
            tiles = []
            for q in range(2):
                for m in range(2):
                    tiles.append((tile_m(w1, lambda it, q=q, m=m: it * 512 + q * 256 + m * P),
                                  q * 20 + 2 + m, 4 * q + m))
                for t in range(2):
                    tiles.append((lambda it, r, q=q, t=t: [(view3(r, 2), rows2(w2, it * 4 + q * 2, 2, t * 512, 512))],
                                  q * 20 + 4 + 8 + 4 * t + 3, 4 * q + 2 + t))
            plan.add(f"mlp{l}", D_FF // (2 * FF_GROUP), tiles, 40)

        def plan_odd():
            plan.add("fl", 1, [(tile_m(od_in, lambda it: 4 * D, 16), 1, 5)], 2)
            vg = [lambda it: it * P + 2 * D, lambda it: it * P + 3 * D]
            plan.add("odd", 8, [(tile_m(od_in, lambda it: it * P), 2, 0),
                                (tile_m(od_in, lambda it: it * P + D), 3, 1),
                                (tile_t(od_in, 0, vg), 11, 2), (tile_t(od_in, 4, vg), 11, 3),
                                (tile_row(od_out, lambda it: it), 27, 4)], 28)

        def plan_spatial():
            w_in, w_out = A["w_in_2"], A["w_out_2"]
            v = [(tile_t(w_in, k0, [lambda it, p=p: 512 + p * 256]), 8 * p + 7, 2 * p + k0 // 4)
                 for p in range(2) for k0 in (0, 4)]
            plan.add("sv", 1, v, 16)
            plan.add("mix", 4, [(tile_m(w_in, lambda it: it * P + 1024), 2, 0),
                                (tile_m(w_in, lambda it: it * P + 1536), 3, 1),
                                (tile_m(w_in, lambda it: it * P), 7, 0),
                                (tile_row(w_out, lambda it: it), 23, 2)], 24)
            plan.add("yb", 4, [(tile_row(w_out, lambda it: it + 4), 15, 0)], 16)

        def plan_ffn():
            w = A["w_up_2"]
            tiles = [(tile_m(w, lambda it, m=m: it * 256 + m * P), 4 + m, m) for m in range(2)]
            tiles += [(tile_m(w, lambda it, m=m: it * 256 + m * P + D_FF2), 6 + m, 2 + m) for m in range(2)]
            tiles += [(lambda it, r, t=t: [(view3(r, 2), rows2(A["w_down_2"], it * 2, 2, t * 512, 512))],
                       8 + 8 + 4 * t + 3, 4 + t) for t in range(2)]
            plan.add("ffn", D_FF2 // 256, tiles, 24)

        plan_even()
        plan.claim(range(3, 8))
        plan_mlp(0)
        plan_odd()
        plan.claim(range(5, 8))
        plan_mlp(1)
        plan_spatial()
        plan.claim(range(3, 8))
        plan_ffn()
        PH = plan.phases

        top = scr[8] + 20 * KB
        SQ = [at(f"SQ{i}", [P, HALF], top + 2 * KB * i) for i in range(2)]
        RST = [at(f"RST{i}", [P, HALF], top + (4, 10)[i] * KB) for i in range(2)]
        TU = [at(f"TU{i}", [P, HALF], top + 6 * KB + 2 * KB * i) for i in range(2)]
        XIN = at("XIN", [P, NT, D], scr[3] + 4 * KB)
        PROW = at("PROW", [P, n_ptile, P], scr[3])
        ADR = [at(f"ADR{i}", [P, 2, D], scr[3] + (42 + 8 * i) * KB) for i in range(2)]
        ADRS = at("ADRS", [P, D], top + 6 * KB)
        ADM = [at(f"ADM{i}", [P, 2, 384], a) for i, a in enumerate((scr[8] + 16 * KB, top + 4 * KB))]
        ADMS = at("ADMS", [P, 2, 384], top + 7 * KB)
        HH = at("HH", [P, 2, SEQ], scr[8], F32R)
        HL = at("HL", [P, 2, SEQ], scr[8] + 8 * KB, F32R)
        ADS = at("ADS", [P, NK, 2 * D], base + 32 * KB)
        ADSS = at("ADSS", [P, 3 * D], scr[3] + 46 * KB)
        ADG = at("ADG", [P, NK, D], scr[3] + 13 * KB)
        YO = [at(f"YO{i}", [P, D], scr[8] + 4 * KB * i) for i in range(2)]
        FZ = at("FZ", [P, 4, 2 + HALF + 6], scr[6])
        FY = at("FY", [P, 4, HALF], scr[6] + 9 * KB)
        FH = at("FH", [P, 2, SEQ], scr[6] + 17 * KB, F32R)
        FL = at("FL", [P, 2, SEQ], scr[6] + 25 * KB, F32R)
        e0 = scr[3]
        XR = at("XR", [P, 3 + SEQ], e0)
        XC = at("XC", [P, SEQ], e0 + 5 * KB)
        YG = at("YG", [P, SEQ], e0 + 9 * KB)
        GR = at("GR", [P, SEQ], e0 + 13 * KB)
        GI = at("GI", [P, SEQ], e0 + 17 * KB)
        TH = at("TH", [P, SEQ], e0 + 21 * KB)
        HS = at("HS", [P, SEQ], e0 + 25 * KB)
        AA = at("AA", [P, SEQ], e0 + 29 * KB)
        MH = at("MH", [P, SEQ], e0 + 33 * KB, F32R)
        ML = at("ML", [P, SEQ], e0 + 37 * KB, F32R)
        WGA = at("WGA", [P, P], e0 + 58 * KB)
        WGX = at("WGX", [P, P], e0 + 58 * KB + 512)
        B = [at(f"B{i}", [P, SEQ], e0 + 4 * KB * i) for i in range(7)]
        ATT = at("ATT", [P, 2, NT, P], e0)
        ZL = at("ZL", [16, SEQ], e0 + 28 * KB)
        CHM = at("CHM", [P, HALF], e0 + 32 * KB)
        VT = at("VT", [P, NT, 256], e0 + 34 * KB)
        STT_ = at("STT", [P, 16, P], e0 + 42 * KB)
        GMH = [at(f"GMH{i}", [P, SEQ], e0 + (16, 20)[i] * KB, F32R) for i in range(2)]
        GML = [at(f"GML{i}", [P, SEQ], e0 + (24, 54)[i] * KB, F32R) for i in range(2)]
        OO = [at(f"OO{i}", [P, HALF], e0 + 50 * KB + 2 * KB * i) for i in range(2)]
        GSQ = at("GSQ", [P, HALF], top)
        GRS = at("GRS", [P, HALF], top + 2 * KB)
        MASKG = at("MASKG", [P, P], top + 4 * KB)
        WUP = at("WUP", [16, 256], top + 5 * KB)
        DEC = at("DEC", [P, 16], top + 6 * KB)
        d0 = scr[5]
        QH = at("QH", [P, SEQ], d0, F32R)
        QL = at("QL", [P, SEQ], d0 + 4 * KB, F32R)
        KH = at("KH", [P, SEQ], d0 + 8 * KB, F32R)
        KL = at("KL", [P, SEQ], d0 + 12 * KB, F32R)
        V = at("V", [P, NT, P], d0 + 16 * KB)
        G = at("G", [P, NT, P], d0 + 20 * KB)
        NF = at("NF", [P, 2, SEQ], d0 + 24 * KB)
        PR = [at(f"PR{i}", [P, SEQ], d0 + 32 * KB + 4 * KB * i) for i in range(2)]
        PT = [at(f"PT{i}", [P, SEQ], d0 + 40 * KB + 4 * KB * i) for i in range(2)]
        QT = [at(f"QT{i}", [P, HALF], d0 + (32, 34, 44, 46)[i] * KB) for i in range(4)]
        QSQ = [at(f"QSQ{i}", [P, HALF], d0 + 36 * KB + 2 * KB * i) for i in range(2)]
        QRS = [at(f"QRS{i}", [P, HALF], d0 + 40 * KB + 2 * KB * i) for i in range(2)]
        FE = at("FE", [16, SEQ], d0 + 40 * KB)
        FC = at("FC", [16, SEQ], d0 + 44 * KB)
        YB = at("YB", [P, CONV_PAD + SEQ + 2], e0)
        CX = at("CX", [P, 4, SEQ], e0 + 5 * KB)
        VS = at("VS", [P, NT, 512], e0 + 21 * KB)
        SMH = at("SMH", [P, SEQ], e0 + 37 * KB, F32R)
        SML = at("SML", [P, SEQ], e0 + 41 * KB, F32R)
        AB = [at(f"AB{i}", [P, HALF], e0 + (45, 53)[i] * KB) for i in range(2)]
        GB = [at(f"GB{i}", [P, HALF], e0 + (47, 55)[i] * KB) for i in range(2)]
        VH = at("VH", [P, NT, P], e0 + 49 * KB)
        BS = at("BS", [P, 4, P], top + 8 * KB)
        LAG = at("LAG", [P, 512], e0 + 53 * KB)
        LAB = at("LAB", [P, 512], e0 + 55 * KB)
        WST = at("WST", [P, 4, P], e0 + 57 * KB)
        UU = at("UU", [P, SEQ], e0 + 41 * KB)
        CP = at("CP", [P, SEQ], top)
        TW = at("TW", [P, CONV_B], top + 10 * KB)
        TP = at("TP", [P, HALF], top + 10 * KB + 128)
        TY = [at(f"TY{i}", [P, HALF], top + 4 * KB + 2 * KB * i) for i in range(2)]
        BROW = at("BROW", [1, 512], e0 + 41 * KB)
        WSR = at("WSR", [P, 4, P], e0 + 45 * KB)
        BST = at("BST", [P, 32, 6], e0 + 49 * KB)
        MV = at("MV", [P, 32, 2], e0 + 49 * KB + 768)
        VR = at("VR", [P, 32], e0 + 49 * KB + 1024)
        negf = nc.dram_tensor("neg_f_cum", [16, SEQ], F32, kind="Internal").ap()

        def norm_vec(n):
            if n <= 3:
                return vec(f"ug{n}"), vec(f"ub{n}")
            return (pv("ln_g", 3 * NK, NK), pv("ln_b", 3 * NK, NK)) if n == 4 else \
                (pv("ln1_g_2", 0, NK), pv("ln1_b_2", 0, NK))

        n_prow_dma = sum((pcol[n] + ap.shape[0] - 1) // P - pcol[n] // P + 1 for n, ap in prow.items())
        block = ctx.enter_context(nc.Block())

        @block.tensor
        def _(pe):
            w_ready = Tally(pe, S("w_ready"))
            a_free, d_free = Tally(pe, S("a_free")), Tally(pe, S("d_free"))
            sq = Tally(pe, S("sq"))
            ada_sum = Tally(pe, S("ada_sum"))
            done = S("gemm_done")
            turn = {"a": 0, "d": 0}

            def a_bank():
                b = turn["a"] % NA
                turn["a"] += 1
                a_free.take()
                return b

            def d_bank():
                b = NA + turn["d"] % ND
                turn["d"] += 1
                d_free.take()
                return b

            def three(out, parts, signal=None):
                for i, (wh, wl, xh, xl) in enumerate(parts):
                    pe.matmul(out, wh, xh, start=(i == 0), stop=False)
                    pe.matmul(out, wh, xl, start=False, stop=False)
                    mm = pe.matmul(out, wl, xh, start=False, stop=(i == len(parts) - 1))
                mm.then_inc(done if signal is None else signal, 1)

            def w_tile(ph, j):
                w_ready.take()
                s = ph["tiles"][j][2]
                return WH[s], WL[s]

            def half(h):
                return slice(h * HALF, (h + 1) * HALF)

            def u_item(tile, h, width=P, fresh=None):
                b = a_bank()
                parts = []
                for k in range(NK):
                    if fresh is not None:
                        pe.wait_ge(S(f"u_ready{h}"), NK * fresh + k + 1)
                    c = slice(k * width, (k + 1) * width)
                    parts = [(tile[0][:, c], tile[1][:, c], UH[:, k, half(h)], UL[:, k, half(h)])]
                    for wh, wl, xh, xl in parts:
                        pe.matmul(bank(b)[0:width], wh, xh, start=(k == 0), stop=False)
                        pe.matmul(bank(b)[0:width], wh, xl, start=False, stop=False)
                        mm = pe.matmul(bank(b)[0:width], wl, xh, start=False, stop=(k == NK - 1))
                mm.then_inc(done, 1)

            def token_item(ta, tb, t, extra=None):
                b = a_bank()
                o = bank(b, 256)
                for k in range(NK):
                    w = ta if k < 4 else tb
                    c = slice((k % 4) * 256, (k % 4 + 1) * 256)
                    x = slice(t * P, (t + 1) * P)
                    pe.matmul(o, UL[:, k, x], w[0][:, c], start=(k == 0), stop=False)
                    pe.matmul(o, UH[:, k, x], w[0][:, c], start=False, stop=False)
                    mm = pe.matmul(o, UH[:, k, x], w[1][:, c], start=False, stop=(k == NK - 1 and extra is None))
                if extra is not None:
                    mm = pe.matmul(o, ONES[0:1, :], extra, start=False, stop=True)
                mm.then_inc(done, 1)

            def out_row(tile, mh, ml):
                for h in range(2):
                    for m in range(NK):
                        b = d_bank()
                        c = slice(m * P, (m + 1) * P)
                        three(bank(b), [(tile[0][:, c], tile[1][:, c], mh[:, half(h)], ml[:, half(h)])])

            def down(tiles, hh, hl, ready, h):
                for m in range(NK):
                    if m % 4 == 0 and h == 0:
                        tiles.append(w_tile(*ready[m // 4]))
                    t = tiles[m // 4]
                    b = d_bank()
                    three(bank(b), [(t[0][:, k * 512 + (m % 4) * P:k * 512 + (m % 4 + 1) * P],
                                     t[1][:, k * 512 + (m % 4) * P:k * 512 + (m % 4 + 1) * P],
                                     hh[:, k, half(h)], hl[:, k, half(h)]) for k in range(2)])

            def ada_columns(sums, col):
                ada_sum.take()
                for i, s in enumerate(sums):
                    mm = pe.matmul(bank(7)[:, col(i)], s, ONES[:, 0:1], start=True, stop=True,
                                   skip_group_check=True)
                mm.then_inc(S("ada_done"), 1)

            t_xt = Tally(pe, S("xt_free"))

            def norm_sums(kt, x_of):
                d_free.wait_at(ND)
                for h, b in ((0, 6), (1, 5)):
                    for k in range(kt):
                        mm = pe.matmul(bank(b), ONES[:, :], x_of(k, h), start=(k == 0), stop=(k == kt - 1))
                    mm.then_inc(S("stat_done"), 1)
                if norms_done[0]:
                    pe.wait_ge(S("std"), norms_done[0])
                for h, b in ((0, 7), (1, 4)):
                    for k in range(kt):
                        sq.take()
                        mm = pe.matmul(bank(b), ONES[:, :], SQ[k % 2][:, :], start=(k == 0), stop=(k == kt - 1))
                        mm.then_inc(S("sq_used"), 1)
                norms_done[0] += 2

            norms_done = [0]

            pe.sem_inc(S("o_done"), 2)
            pe.wait_ge(S("consts"), 1)
            pe.wait_ge(S("prow_in"), 16 * n_prow_dma)
            for i in range(n_ptile):
                mm = pe.transpose(PS[:, 6 * HALF + i * P:6 * HALF + (i + 1) * P], PROW[:, i, :], IDENT[:, :])
            mm.then_inc(S("pv_done"), 1)
            for h in range(2):
                for k in range(NK):
                    n = h * NK + k
                    t_xt.wait_at(n - 5)
                    for t in range(4):
                        if k == 0 and t == 0:
                            pe.wait_ge(S(f"x_in{h}"), 16)
                        mm = pe.transpose(PS[:, (n % 6) * HALF + t * P:(n % 6) * HALF + (t + 1) * P],
                                          XIN[:, 4 * h + t, k * P:(k + 1) * P], IDENT[:, :])
                    mm.then_inc(S("xt_done"), 1)
            ada_columns([ADSS[:, i * P:(i + 1) * P] for i in range(16)], lambda i: slice(i, i + 1))

            def mlp(l, fresh):
                ph = PH[f"mlp{l}"]
                pairs = [(w_ready, 8), (a_free, 8), (d_free, 32), (h_ready, 8)]
                if l == 0:
                    pairs.append((ada_sum, 1))
                    pe.wait_ge(S("std"), norms_done[0])
                with rounds(pe, ph["count"], *pairs) as it:
                    for q in range(2):
                        t = []
                        for h in range(2):
                            for m in range(2):
                                if h == 0:
                                    t.append(w_tile(ph, 4 * q + m))
                                u_item(t[m], h, fresh=fresh if q == 0 and m == 0 else None)
                        t = []
                        for h in range(2):
                            h_ready.take(2)
                            down(t, HH, HL, [(ph, 4 * q + 2), (ph, 4 * q + 3)], h)
                    if l == 0:
                        ada_columns([ADMS[:, i // 3, (i % 3) * P:(i % 3 + 1) * P] for i in range(6)],
                                    lambda i: bass.ds(it * 3 + (24 * (i // 3) + i % 3), 1))

            h_ready = Tally(pe, S("h_ready"), 2)
            xk = lambda k, h: X[:, k, half(h)]
            fresh = 0

            def even():
                m_ready = Tally(pe, S("m_ready"))
                xc_ready = Tally(pe, S("xc_ready"))
                wg_in = Tally(pe, S("wg_in"))

                def xr_yr(ph, fresh=None):
                    t = []
                    for h in range(2):
                        for m in range(2):
                            if h == 0:
                                t.append(w_tile(ph, m))
                            u_item(t[m], h, fresh=fresh if m == 0 else None)

                def gates():
                    wg_in.take(64)
                    for h in range(2):
                        xc_ready.take()
                        for w in (WGA, WGX):
                            b = a_bank()
                            pe.matmul(bank(b), w[:, :], XC[:, half(h)], start=True, stop=True).then_inc(done, 1)

                xr_yr(PH["rg_first"], fresh=0)
                ada_columns([ADSS[:, 2 * D + i * P:2 * D + (i + 1) * P] for i in range(8)],
                            lambda i: slice(16 + i, 17 + i))
                gates()
                pe.wait_ge(S("mod_ready"), 1)
                with rounds(pe, 3, (w_ready, 3), (a_free, 8), (d_free, 16), (m_ready, 1), (xc_ready, 2),
                            (wg_in, 64), (ada_sum, 1)) as it:
                    xr_yr(PH["rg"])
                    m_ready.take()
                    out_row(w_tile(PH["rg"], 2), MH, ML)
                    gates()
                    ada_columns([ADRS[:, i * P:(i + 1) * P] for i in range(8)], lambda i: bass.ds(it * 8 + i, 1))
                m_ready.take()
                out_row(w_tile(PH["rg_last"], 0), MH, ML)

                qk = Tally(pe, S("qk_ready"))
                gst = Tally(pe, S("gla_std"))
                for p in range(2):
                    ph = PH[f"gla{p}"]
                    j = 0
                    if p == 0:
                        t = w_tile(ph, j)
                        j += 1
                        for h in range(2):
                            u_item(t, h, width=16)
                        pe.wait_ge(S("wup_in"), 16)
                        a_free.wait_at(NA)
                    for h in range(2):
                        b = a_bank()
                        pe.matmul(bank(b), WUP[:, p * P:(p + 1) * P], ZL[:, half(h)],
                                  start=True, stop=True).then_inc(done, 1)
                    for _ in range(2):
                        t = w_tile(ph, j)
                        j += 1
                        for h in range(2):
                            u_item(t, h)
                    ta, tb = w_tile(ph, j), w_tile(ph, j + 1)
                    j += 2
                    for t in range(NT):
                        token_item(ta, tb, t)
                    qk.take(3)
                    for g in range(2):
                        b = d_bank()
                        for t in range(4):
                            mm = pe.transpose(PS[:, b * HALF + t * P:b * HALF + (t + 1) * P],
                                              B[4][:, (4 * g + t) * P:(4 * g + t + 1) * P], IDENT[:, :])
                        mm.then_inc(done, 1)
                    for hh in range(2):
                        r = slice(64 * hh, 64 * hh + 64)
                        for g in range(2):
                            b = d_bank()
                            for t in range(4):
                                c = slice((4 * g + t) * P, (4 * g + t + 1) * P)
                                mm = pe.matmul(PS[:, b * HALF + t * P:b * HALF + (t + 1) * P],
                                               B[3][r, c], B[5][r, c], start=(t == 0), stop=(t == 3),
                                               skip_group_check=True)
                            mm.then_inc(done, 1)
                    a_free.wait_at(NA)
                    d_free.wait_at(ND)
                    for t in range(0, NT, 2):
                        for e in range(2):
                            b = d_bank()
                            r = slice(64 * e, 64 * e + 64)
                            for i in range(2):
                                mm = pe.matmul(PS[:, b * HALF + i * 256:b * HALF + (i + 1) * 256],
                                               B[6][r, (t + i) * P:(t + i + 1) * P], VT[r, t + i, :],
                                               start=(i == 0), stop=(i == 1), skip_group_check=True)
                            mm.then_inc(done, 1)
                    for i in range(2):
                        t = w_tile(ph, j)
                        j += 1
                        for h in range(2):
                            u_item(t, h)
                    d_free.wait_at(ND)
                    for hh in range(2):
                        r = slice(64 * hh, 64 * hh + 64)
                        for h in range(2):
                            b = a_bank()
                            for t in range(4 * h, 4 * h + 4):
                                o = PS[:, b * HALF + (t % 4) * P:b * HALF + (t % 4 + 1) * P]
                                pe.matmul(o, VT[:, t, hh * P:(hh + 1) * P], ATT[:, hh, t, :],
                                          start=(t % 4 == 0), stop=False, skip_group_check=True)
                            for n in range(8 * h, 8 * h + 8):
                                o = PS[:, b * HALF + (n % 8) * 64:b * HALF + (n % 8 + 1) * 64]
                                mm = pe.matmul(o, STT_[r, n, :], B[5][r, n * 64:(n + 1) * 64],
                                               start=False, stop=(n % 8 == 7), skip_group_check=True)
                            mm.then_inc(done, 1)
                            a_free.wait_at(NA)
                            pe.matmul(bank(6), ONES[:, :], GSQ[:, :], start=True, stop=True)\
                                .then_inc(S("gla_sum"), 1)
                            gst.take()
                    for hh in range(2):
                        m_ready.take(2)
                        out_row(w_tile(ph, j), GMH[hh], GML[hh])
                        j += 1

            def odd(fresh):
                t = w_tile(PH["fl"], 0)
                for h in range(2):
                    u_item(t, h, width=16, fresh=fresh)
                qst = Tally(pe, S("q_std"))
                qkr = Tally(pe, S("qkn_ready"))
                s_free = Tally(pe, S("s_free"))
                probs = Tally(pe, S("probs"))
                pt_a, pt_d = Tally(pe, S("pt_a")), Tally(pe, S("pt_d"))
                o_free = Tally(pe, S("o_free"))
                m_ready = Tally(pe, S("ot_ready"))
                ph = PH["odd"]
                n_d = 2 * sum(1 for tb in range(NT) if tb >= 4)
                with rounds(pe, 8, (w_ready, 5), (a_free, 12), (d_free, 16), (qst, 4), (qkr, 4),
                            (s_free, 16), (probs, 16), (pt_a, 16), (pt_d, n_d), (o_free, 16),
                            (m_ready, 2)) as it:
                    d_free.wait_at(ND)
                    tiles = []

                    def head_sums(i):
                        if i >= 2:
                            qst.take()
                        a_free.wait_at(i - i_done[0] + NA)
                        pe.matmul(bank(6 + i % 2), BLK[:, :], QSQ[i % 2][:, :], start=True, stop=True)\
                            .then_inc(S("q_sum"), 1)

                    i_done = [0]
                    for i in range(4):
                        if i < 2:
                            tiles.append(w_tile(ph, i))
                        i_done[0] = i
                        u_item(tiles[i % 2], i // 2)
                        if i:
                            head_sums(i - 1)
                    head_sums(3)
                    ta, tb_ = w_tile(ph, 2), w_tile(ph, 3)
                    for t in range(NT):
                        token_item(ta, tb_, t)
                    a_free.wait_at(NA)
                    qst.take(2)
                    qkr.take(4)

                    def scores(n):
                        hh, tb = n // NT, n % NT
                        r = slice(64 * hh, 64 * hh + 64)
                        w = (tb // 2 + 1) * 256
                        q = slice(tb * P, (tb + 1) * P)
                        b = 2 * (n % 2)
                        if n >= 2:
                            s_free.take()
                        for c in range(0, w, HALF):
                            e = min(c + HALF, w)
                            o = PS[:, b * HALF + c:b * HALF + e]
                            pe.matmul(o, QH[r, q], KH[r, c:e], start=True, stop=False, skip_group_check=True)
                            pe.matmul(o, QH[r, q], KL[r, c:e], start=False, stop=False, skip_group_check=True)
                            pe.matmul(o, QL[r, q], KH[r, c:e], start=False, stop=False, skip_group_check=True)
                        pe.matmul(PS[:, b * HALF + tb * P:b * HALF + (tb + 1) * P], IDENT[:, :], MASKA[:, :],
                                  start=False, stop=True, skip_group_check=True).then_inc(S("s_done"), 1)

                    def turn_probs(n):
                        tb = n % NT
                        probs.take()
                        for s in range(tb + 1):
                            if s == 0 and n:
                                pt_a.take()
                            if s == 4 and n_turn[0]:
                                pt_d.take()
                            if s == 4:
                                n_turn[0] += 1
                            mm = pe.transpose(PS[:, 4 * HALF + s * P:4 * HALF + (s + 1) * P],
                                              PR[n % 2][:, s * P:(s + 1) * P], IDENT[:, :])
                            if s == min(tb, 3):
                                mm.then_inc(S("pt4_done"), 1)
                            elif s == tb:
                                mm.then_inc(S("pt5_done"), 1)

                    def values(n):
                        hh, tb = n // NT, n % NT
                        if n >= 2:
                            o_free.take()
                        pt_a.wait_at(n + 1 - pt_a.j)
                        wide = 4 * hh + max(0, tb - 3)
                        if wide > pt_d.j:
                            pt_d.wait_at(wide - pt_d.j)
                        for s in range(tb + 1):
                            mm = pe.matmul(bank(6 + n % 2, 64), PT[n % 2][:, s * P:(s + 1) * P],
                                           V[:, s, 64 * hh:64 * hh + 64], start=(s == 0), stop=(s == tb))
                        mm.then_inc(S("o_done"), 1)

                    n_turn = [0]
                    scores(0)
                    scores(1)
                    for n in range(2 * NT):
                        turn_probs(n)
                        if n + 2 < 2 * NT:
                            scores(n + 2)
                        if n:
                            values(n - 1)
                    values(2 * NT - 1)
                    s_free.take(2)
                    pt_a.take()
                    pt_d.take()
                    o_free.take(2)
                    for g in range(2):
                        for t in range(4):
                            mm = pe.transpose(PS[:, (4 + g) * HALF + t * P:(4 + g) * HALF + (t + 1) * P],
                                              G[:, 4 * g + t, :], IDENT[:, :])
                        mm.then_inc(S("ot_done"), 1)
                    m_ready.take(2)
                    out_row(w_tile(ph, 4), QH, QL)

            def spatial(fresh):
                pe.wait_ge(S("sp_in"), 16 * 4)
                pe.wait_ge(S("std"), norms_done[0] - 1)
                for hh in range(4):
                    mm = pe.transpose(PS[:, 6 * HALF + hh * P:6 * HALF + (hh + 1) * P], WSR[:, hh, :], IDENT[:, :])
                mm.then_inc(S("wst_done"), 1)
                ph = PH["sv"]
                for p in range(2):
                    ta, tb = w_tile(ph, 2 * p), w_tile(ph, 2 * p + 1)
                    for t in range(NT):
                        if p == 0 and t % 4 == 0:
                            pe.wait_ge(S(f"u_ready{t // 4}"), NK * (fresh + 1))
                        token_item(ta, tb, t, extra=BROW[0:1, 256 * p:256 * p + 256])
                m_ready = Tally(pe, S("sm_ready"))
                ph = PH["mix"]
                vh = Tally(pe, S("vh_ready"))
                with rounds(pe, 4, (w_ready, 4), (a_free, 8), (d_free, 16), (m_ready, 2), (vh, 1)) as it:
                    t = []
                    for h in range(2):
                        for m in range(2):
                            if h == 0:
                                t.append(w_tile(ph, m))
                            u_item(t[m], h)
                    vh.take()
                    for h in range(2):
                        b = a_bank()
                        for c in range(4):
                            mm = pe.matmul(PS[:, b * HALF + c * P:b * HALF + (c + 1) * P],
                                           VH[:, 4 * h + c, :], WST[:, bass.ds(it, 1), :].rearrange("p a b -> p (a b)"),
                                           start=(c == 0), stop=(c == 3), skip_group_check=True)
                        mm.then_inc(done, 1)
                    t = w_tile(ph, 2)
                    for h in range(2):
                        u_item(t, h)
                    m_ready.take(2)
                    out_row(w_tile(ph, 3), SMH, SML)
                pe.wait_ge(S("cx_ready"), 4)
                norm_sums(4, lambda k, h: CX[:, k, half(h)])
                ph = PH["yb"]
                with rounds(pe, 4, (w_ready, 1), (d_free, 16), (m_ready, 2)) as it:
                    m_ready.take(2)
                    out_row(w_tile(ph, 0), SMH, SML)

            def ffn(fresh):
                ph = PH["ffn"]
                with rounds(pe, ph["count"], (w_ready, 6), (a_free, 8), (d_free, 16), (h_ready, 4)) as it:
                    t = []
                    for h in range(2):
                        for m in range(4):
                            if h == 0:
                                t.append(w_tile(ph, m))
                            u_item(t[m], h, fresh=fresh if m == 0 else None)
                    t = []
                    for h in range(2):
                        h_ready.take(2)
                        down(t, FH, FL, [(ph, 4), (ph, 5)], h)

            even()
            norm_sums(NK, xk)
            pe.wait_ge(S("mod_ready"), 2)
            mlp(0, 1)
            norm_sums(NK, xk)
            odd(2)
            norm_sums(NK, xk)
            mlp(1, 3)
            norm_sums(NK, xk)
            spatial(4)
            norm_sums(NK, xk)
            ffn(5)
            norm_sums(NK, xk)
            for t in range(NT):
                for g in range(2):
                    n = 2 * t + g
                    pe.wait_ge(S("y_ready"), NK * (t // 4 + 1))
                    if n >= 4:
                        pe.wait_ge(S("yo_ready"), n - 3)
                    for k in range(4):
                        mm = pe.transpose(PS[:, (n % 4) * HALF + k * P:(n % 4) * HALF + (k + 1) * P],
                                          X[:, 4 * g + k, t * P:(t + 1) * P], IDENT[:, :])
                    mm.then_inc(S("y_done"), 1)

        @block.scalar
        def _(act):
            gd = Tally(act, S("gemm_done"))
            cen, sq_used, tt = Tally(act, S("cen")), Tally(act, S("sq_used"), -2), Tally(act, S("tt"))
            chain = Chain(act, S("act_chain"))
            mine = Tally(act, S("a_free"), NA)
            turn = [0]
            half = lambda h: slice(h * HALF, (h + 1) * HALF)
            col = lambda t, j: t[:, j:j + 1]

            def a_bank():
                gd.take()
                turn[0] += 1
                return bank((turn[0] - 1) % NA)

            def settle():
                act.sem_inc(S("act_turn"), 1)

            def free(ins):
                ins.then_inc(S("a_free"), 1)
                mine.skip()

            ada_step = Tally(act, S("ada_step"), 2 * NK)
            ada_row = lambda l, j, k, n: A["ada_w"][l, j].rearrange("(k p) m -> p k m", p=P)[:, k:k + n, :]

            def squares(kt, tile_of, h):
                for k in range(kt):
                    cen.take()
                    sq_used.take()
                    act.activation(SQ[k % 2][:, :], tile_of(k, h), ACT.Square).then_inc(S("sq"), 1)

            def std(kt, h):
                sq_used.wait_at(2)
                act.activation(RST[h][:, :], bank((7, 4)[h]), ACT.Sqrt, bias=EPSL[:, :], scale=1.0 / (kt * P))\
                    .then_inc(S("std"), 1)

            def norm_stds(kt, tile_of):
                squares(kt, tile_of, 0)
                std(kt, 0)
                squares(kt, tile_of, 1)

            def norm(n):
                ug, ub = norm_vec(n)
                norm_stds(NK, lambda k, h: X[:, k, half(h)])
                for h in range(2):
                    for k in range(NK):
                        tt.take()
                        if h == 0 and k == 2:
                            std(NK, 1)
                        if k % 2 == 0 and h * NK + k >= 2:
                            act.wait_ge(S(f"u_ready{(h * NK + k - 2) // NK}"), NK * n + (k - 2) % NK + 1)
                        x = X[:, k, half(h)]
                        if k % 2 == 0:
                            act.activation(TU[0][:, :], x, ACT.Identity, bias=col(ub, k), scale=col(ug, k))
                        act.activation(UH[:, k, half(h)], x, ACT.Identity, bias=col(ub, k), scale=col(ug, k))\
                            .then_inc(S("uh"), 1)

            act.sem_inc(S("a_free"), NA)
            ev_wa, ev_wx = A["ev_rg_wa"][0], A["ev_rg_wx"][0]

            def gate_blocks(c):
                for w, t in ((ev_wa, WGA), (ev_wx, WGX)):
                    for i in range(2):
                        act.dma_start(t[64 * i:64 * i + 64, 64 * i:64 * i + 64],
                                      w[bass.ds(2 * c + i, 1), :, :].rearrange("a p n -> (a p) n"))\
                            .then_inc(S("wg_in"), 16)

            act.wait_ge(S("consts"), 1)
            act.dma_start(WUP[:, :], A["ev_gla_w_up"][0]).then_inc(S("wup_in"), 16)
            act.dma_start(BF[:, :], A["od_b_f"].rearrange("a h -> h a")).then_inc(S("bf_in"), 16)
            for i, n in enumerate(("od_q_norm_g", "od_k_norm_g")):
                for e in range(2):
                    act.dma_start(QKG[64 * e:64 * e + 64, i:i + 1], A[n].rearrange("a h -> h a"))\
                        .then_inc(S("bf_in"), 16)
            act.wait_ge(S("pv_done"), 1)
            chain.done(act.activation(PV[:, 0:n_ptile * P], PS[:, 6 * HALF:6 * HALF + n_ptile * P], ACT.Copy))
            act.activation(CS[:, :], pv("c", 0, NK), ACT.Silu).then_inc(S("cs_ready"), 1)
            lam, le, ll = pv("ev_rg_lam", 0, 4), vec("le", 4), vec("ll", 4)
            chain.done(act.activation(le, lam, ACT.Abs))
            chain.done(act.activation(le, le, ACT.Exp, scale=-1.0))
            act.activation(ll, le, ACT.Ln, bias=1.0).then_inc(S("lam_e"), 1)
            for n in range(2 * NK):
                act.wait_ge(S("xt_done"), n + 1)
                act.activation(X[:, n % NK, half(n // NK)], bank(n % 6), ACT.Copy).then_inc(S("xt_free"), 1)
            act.dma_start(ADG[:, :, :], ada_row(0, 0, 0, NK)[:, :, 2 * D:3 * D]).then_inc(S("ada0_gate_in"), 16)
            for h in range(2):
                for k in range(NK):
                    tt.take()
                    act.activation(UH[:, k, half(h)], TU[k % 2][:, :], ACT.Copy).then_inc(S("uh"), 1)
                    x = X[:, k, half(h)]
                    act.activation(x, x, ACT.Copy, scale=ALPHA_1).then_inc(S("x_ready"), 1)

            def even():
                lru = Tally(act, S("lru"))

                def ada_rows(it, r):
                    act.dma_start(ADR[r % 2][:, :, :], ada_row(0, 1, 2 * r, 2)[:, :, bass.ds(it * D, D)])\
                        .then_inc(S(f"ada_in{r % 2}"), 16)

                def xr_yr(it):
                    loop = it is not None
                    if loop:
                        ada_step.wait_at(0)
                        ada_rows(it, 0)
                        ada_rows(it, 1)
                        gate_blocks(it + 1)
                    for h in range(2):
                        b = a_bank()
                        free(act.activation(XR[:, 3 + h * HALF:3 + (h + 1) * HALF], b, ACT.Copy))
                        b = a_bank()
                        free(act.activation(YG[:, half(h)], b, ACT.Gelu_apprx_tanh))
                    if loop:
                        for r in (2, 3):
                            ada_step.take(2)
                            ada_rows(it, r)
                        ada_step.skip(4)

                def gates(c):
                    cc = bass.ds(c, 1)
                    gv = lambda n: PV[:, bass.ds(c + pcol[n], 1)]
                    for h in range(2):
                        b = a_bank()
                        settle()
                        free(act.activation(GR[:, half(h)], b, ACT.Sigmoid, bias=gv("ev_rg_ba")))
                        b = a_bank()
                        settle()
                        free(act.activation(GI[:, half(h)], b, ACT.Sigmoid, bias=gv("ev_rg_bx")))
                    mine.wait_at(0)
                    settle()
                    act.activation(AA[:, :], GR[:, :], ACT.Exp, scale=vec("lam8", 4)[:, cc])
                    act.activation(TH[:, :], GR[:, :], ACT.Tanh, scale=vec("lam8n", 4)[:, cc])\
                        .then_inc(S("rg_a"), 1)
                    lru.take()
                    act.activation(TH[:, :], TH[:, :], ACT.Sqrt).then_inc(S("rg_a"), 1)
                    lru.take()
                    act.activation(MH[:, :], HS[:, :], ACT.Copy).then_inc(S("rg_a"), 1)

                gate_blocks(0)
                xr_yr(None)
                act.wait_ge(S("lam_ready"), 1)
                gates(0)
                with rounds(act, 3, (gd, 24), (mine, 8), (ada_step, 8), (lru, 2)) as it:
                    xr_yr(it)
                    gd.skip(16)
                    gates(it + 1)
                gd.skip(16)

                gl, gsum, go = Tally(act, S("gl")), Tally(act, S("gla_sum")), Tally(act, S("gla_o"))

                for p in range(2):
                    if p == 0:
                        for h in range(2):
                            free(act.activation(ZL[:, half(h)], a_bank()[0:16], ACT.Copy))
                    for h in range(2):
                        b = a_bank()
                        bu = pv("ev_gla_b_up", p)
                        act.activation(B[0][:, half(h)], b, ACT.Identity, bias=bu)
                        free(act.activation(B[2][:, half(h)], b, ACT.Abs, bias=bu))
                    mine.wait_at(0)
                    chain.done(act.activation(B[2][:, :], B[2][:, :], ACT.Exp, scale=-1.0))
                    act.activation(B[3][:, :], B[2][:, :], ACT.Ln, bias=1.0).then_inc(S("z_ready"), 1)
                    for t, s in ((B[5], 0.125), (B[6], 1.0)):
                        for h in range(2):
                            free(act.activation(t[:, half(h)], a_bank(), ACT.Copy, scale=s))
                    gl.take()
                    act.activation(B[2][:, :], B[1][:, :], ACT.Exp, scale=1 / 16)
                    act.activation(B[3][:, :], B[1][:, :], ACT.Exp, scale=-1 / 16)
                    act.activation(DEC[:, :], B[1][:, 63::64], ACT.Exp, scale=1 / 16)
                    act.activation(B[4][:, :], B[4][:, :], ACT.Exp, scale=1 / 16).then_inc(S("exps"), 1)
                    for t in range(NT):
                        free(act.activation(VT[:, t, :], a_bank()[:, 0:256], ACT.Copy))
                    gd.skip(14)
                    for i in range(2):
                        for h in range(2):
                            free(act.activation(B[2 + i][:, half(h)], a_bank(), ACT.Silu))
                    for hh in range(2):
                        for h in range(2):
                            n = 4 * p + 2 * hh + h
                            b = a_bank()
                            if hh:
                                act.wait_ge(S("m_ready"), 4 + 4 * p + h + 1)
                            act.activation(OO[h][:, :], b, ACT.Copy)
                            free(act.activation(GSQ[:, :], b, ACT.Square))
                            gsum.take()
                            act.activation(GRS[:, :], bank(6), ACT.Sqrt, bias=EPSR[:, :], scale=1.0 / P)\
                                .then_inc(S("gla_std"), 1)
                            go.take()
                            act.activation(GMH[hh][:, half(h)], OO[h][:, :], ACT.Copy).then_inc(S("gmh"), 1)
                    gd.skip(32)

            h_done = Tally(act, S("h_ready"))

            def mlp(l):
                pairs = [(gd, 40), (mine, 8), (h_done, 8)] + ([(ada_step, 8)] if l == 0 else [])
                with rounds(act, 8, *pairs) as it:
                    for q in range(2):
                        for h in range(2):
                            for m in range(2):
                                i = 2 * h + m
                                b = a_bank()
                                h_done.take()
                                settle()
                                r = SQ[i % 2]
                                b1 = PV[:, bass.ds(it * 4 + (pcol["mlp_b1"] + 32 * l + 2 * q + m), 1)]
                                free(act.activation(r[:, :], b, ACT.Relu, bias=b1))
                                mine.wait_at(0)
                                act.activation(HH[:, m, half(h)], r[:, :], ACT.Square)
                                act.activation(r[:, :], r[:, :], ACT.Square).then_inc(S("hh_ready"), 1)
                        if l == 0:
                            for k in range(4 * q, 4 * q + 4):
                                if k < 2:
                                    ada_step.wait_at(0)
                                else:
                                    ada_step.take()
                                act.dma_start(ADM[k % 2][:, :, :],
                                              A["ada_w"][1].rearrange("j (k p) m -> k p j m", p=P)
                                              [k, :, :, bass.ds(it * 384, 384)]).then_inc(S(f"ada_in{k % 2}"), 16)
                            if q:
                                ada_step.skip(2)
                        gd.skip(16)

            def odd():
                for h in range(2):
                    b = a_bank()
                    act.wait_ge(S("bf_in"), 16 * 5)
                    act.activation(FC[:, half(h)], b[0:16], ACT.Identity, bias=BF[:, :])
                    free(act.activation(FE[:, half(h)], b[0:16], ACT.Abs, bias=BF[:, :]))
                mine.wait_at(0)
                chain.done(act.activation(FE[:, :], FE[:, :], ACT.Exp, scale=-1.0))
                act.activation(FE[:, :], FE[:, :], ACT.Ln, bias=1.0).then_inc(S("fe_ready"), 1)
                act.wait_ge(S("fc_ready"), 1)
                act.dma_start(negf, FC[:, :]).then_inc(S("negf_out"), 16)
                act.wait_ge(S("negf_out"), 16)
                qs, qd = Tally(act, S("q_sum")), Tally(act, S("qn_done"))
                pn = Tally(act, S("p_ready"))
                pt4, od = Tally(act, S("pt4_done")), Tally(act, S("o_done"))
                ot = Tally(act, S("ot_done"))
                of = Tally(act, S("o_free"))
                with rounds(act, 8, (gd, 28), (mine, 12), (qs, 4), (qd, 4), (pn, 16), (pt4, 16), (od, 16),
                            (ot, 2), (of, 16)) as it:
                    for e in range(2):
                        act.dma_start(NF[:, e, :], negf[bass.ds(2 * it + e, 1), :].partition_broadcast(P)
                                      .rearrange("p a n -> p (a n)")).then_inc(S("nf_in"), 16)

                    def q_item(i):
                        b = a_bank()
                        act.activation(QT[i][:, :], b, ACT.Copy)
                        free(act.activation(QSQ[i % 2][:, :], b, ACT.Square))

                    def q_std(i):
                        qs.take()
                        act.activation(QRS[i % 2][:, :], bank(6 + i % 2), ACT.Sqrt, bias=EPSR[:, :], scale=1.0 / 64)\
                            .then_inc(S("q_std"), 1)

                    def q_round(i):
                        qd.take()
                        act.activation((QH, KH)[i % 2][:, half(i // 2)], QT[i][:, :], ACT.Copy)\
                            .then_inc(S("qkh"), 1)

                    q_item(0)
                    q_item(1)
                    q_std(0)
                    q_item(2)
                    q_std(1)
                    q_round(0)
                    q_item(3)
                    q_std(2)
                    q_round(1)
                    q_std(3)
                    q_round(2)
                    q_round(3)
                    for t in range(NT):
                        b = a_bank()
                        act.activation(V[:, t, :], b[:, 0:P], ACT.Copy)
                        free(act.activation(G[:, t, :], b[:, P:2 * P], ACT.Sigmoid))

                    def exp(n):
                        w = (n % NT + 1) * P
                        pn.take()
                        act.activation(PR[n % 2][:, 0:w], PR[n % 2][:, 0:w], ACT.Exp, bias=NMX[:, n:n + 1],
                                       accum_out=RSUM[:, n:n + 1]).then_inc(S("probs"), 1)

                    exp(0)
                    for n in range(2 * NT):
                        if n + 1 < 2 * NT:
                            exp(n + 1)
                        w4 = min((n % NT + 1) * P, HALF)
                        pt4.take()
                        od.take()
                        act.activation(PT[n % 2][:, 0:w4], bank(4, w4), ACT.Copy).then_inc(S("pt_a"), 1)
                    of.take(16)
                    for g in range(2):
                        ot.take()
                        act.activation(PR[0][:, half(g)], bank(4 + g), ACT.Copy)
                        act.activation(QH[:, half(g)], bank(4 + g), ACT.Copy).then_inc(S("oth"), 1)
                    gd.skip(16)

            def spatial_loads():
                gd.wait_at(0)
                act.dma_start(WSR[:, :, :], A["w_spatial_2"].rearrange("h t s -> t h s")).then_inc(S("sp_in"), 16)
                act.dma_start(BROW[:, :], A["b_in_2"].rearrange("(a n) -> a n", a=1)[:, 512:1024])\
                    .then_inc(S("sp_in"), 16)
                for n, t in (("ln_a_g_2", LAG), ("ln_a_b_2", LAB)):
                    act.dma_start(t[:, :].rearrange("p (h d) -> p h d", h=4), A[n].partition_broadcast(P))\
                        .then_inc(S("sp_in"), 16)

            def spatial():
                act.wait_ge(S("u_ready1"), NK * 5)
                act.dma_start(BS[:, :, :], A["b_spatial_2"].partition_broadcast(P)).then_inc(S("bs_in"), 16)
                for t in range(2 * NT):
                    p, tt_ = t // NT, t % NT
                    free(act.activation(VS[:, tt_, 256 * p:256 * p + 256], a_bank()[:, 0:256], ACT.Gelu))
                act.wait_ge(S("va_var"), 1)
                act.activation(VR[:, :], MV[:, :, 1], ACT.Sqrt, bias=EPSL[:, :]).then_inc(S("va_std"), 1)
                ab = Tally(act, S("ab_used"))
                ty = Tally(act, S("ty_ready"))
                cp = Tally(act, S("cp_ready"))
                with rounds(act, 4, (gd, 24), (mine, 8), (ab, 2), (ty, 2), (cp, 1)) as it:
                    bi = lambda j: PV[:, bass.ds(it + (pcol["b_in_2"] + j), 1)]
                    for h in range(2):
                        ab.take()
                        if h:
                            cp.take()
                            settle()
                            taps = pv("conv_b_w_2", 0, 4 * CONV_B).rearrange("p (k c) -> p c k", c=4)
                            act.activation(TW[:, :], taps[:, bass.ds(it, 1), :].rearrange("p a k -> p (a k)"),
                                           ACT.Copy)
                            act.activation(VH[:, :, :], VS[:, :, bass.ds(it * P, P)], ACT.Copy)\
                                .then_inc(S("vh_ready"), 1)
                        b = a_bank()
                        settle()
                        free(act.activation(AB[h][:, :], b, ACT.Identity, bias=bi(8)))
                        b = a_bank()
                        settle()
                        free(act.activation(GB[h][:, :], b, ACT.Sigmoid, bias=bi(12)))
                    for h in range(2):
                        free(act.activation(TY[h][:, :], a_bank(), ACT.Copy))
                    for h in range(2):
                        b = a_bank()
                        settle()
                        free(act.activation(UU[:, half(h)], b, ACT.Gelu, bias=bi(0)))
                    for h in range(2):
                        ty.take()
                        act.activation(SMH[:, half(h)], TY[h][:, :], ACT.Copy).then_inc(S("smh"), 1)
                    gd.skip(16)
                norm_stds(4, lambda k, h: CX[:, k, half(h)])
                std(4, 1)
                cx = Tally(act, S("cx_norm"))
                cx.take(8)
                sml = Tally(act, S("sm_ready"), 8 - 2)
                with rounds(act, 4, (gd, 16), (sml, 2), (chain_y, 2)) as it:
                    for h in range(2):
                        sml.take()
                        settle()
                        gb = lambda n: PV[:, bass.ds(it + pcol[n], 1)]
                        chain_y.done(act.activation(TY[h][:, :], CX[:, bass.ds(it, 1), half(h)]
                                                    .rearrange("p a n -> p (a n)"), ACT.Silu,
                                                    bias=gb("ln_b_b_2"), scale=gb("ln_b_g_2")))
                        if h == 0:
                            gd.wait_at(0)
                        act.activation(SMH[:, half(h)], TY[h][:, :], ACT.Copy).then_inc(S("smh"), 1)
                    gd.skip(16)

            chain_y = Chain(act, S("silu_chain"))

            def ffn():
                fc = Tally(act, S("conv_ready"))
                fp = Tally(act, S("prod_ready"))
                with rounds(act, D_FF2 // 256, (gd, 24), (mine, 8), (h_done, 4), (fc, 8), (fp, 4)) as it:
                    for h in range(2):
                        for m in range(4):
                            b = a_bank()
                            if m == 0:
                                h_done.take(2)
                            ch = lambda n, r: PV[:, bass.ds(it * 2 + (pcol[n] + 44 * r + (m if m < 2 else 20 + m)), 1)]
                            act.activation(FZ[:, m, 2:2 + HALF], b, ACT.Copy)
                            free(act.activation(FY[:, m, :], b, ACT.Identity, bias=ch("conv_f_b_2", 0),
                                                scale=ch("conv_f_w_2", 2)))
                        for m in range(2):
                            fc.take()
                            act.activation(FY[:, m, :], FY[:, m, :], ACT.Silu).then_inc(S("silu"), 1)
                        fc.skip(2)
                        for m in range(2):
                            fp.take()
                            act.activation(FH[:, m, half(h)], FY[:, m, :], ACT.Copy).then_inc(S("fh"), 1)
                    gd.skip(16)

            even()
            norm(1)
            mlp(0)
            norm(2)
            odd()
            norm(3)
            mlp(1)
            spatial_loads()
            norm(4)
            spatial()
            norm(5)
            ffn()
            xn = Tally(act, S("xn"))
            norm_stds(NK, lambda k, h: X[:, k, half(h)])
            for h in range(2):
                if h:
                    std(NK, 1)
                for k in range(NK):
                    xn.take()
                    x = X[:, k, half(h)]
                    act.activation(x, x, ACT.Identity, bias=pv("ln2_b_2", k), scale=pv("ln2_g_2", k))\
                        .then_inc(S("y_ready"), 1)
            for n in range(2 * NT):
                t = n // 2
                act.wait_ge(S("y_done"), n + 1)
                if t >= 2 and n % 2 == 0:
                    act.wait_ge(S(f"out_done{t % 2}"), 16 * (t // 2))
                act.activation(YO[t % 2][:, (n % 2) * HALF:(n % 2 + 1) * HALF], bank(n % 4), ACT.Copy)\
                    .then_inc(S("yo_ready"), 1)

        @block.vector
        def _(dve):
            gd = Tally(dve, S("gemm_done"))
            stat, uh, std = Tally(dve, S("stat_done")), Tally(dve, S("uh")), Tally(dve, S("std"))
            af = Tally(dve, S("a_free"), NA)
            mine = Tally(dve, S("d_free"), ND)
            x_ready = Tally(dve, S("x_ready"))
            chain = Chain(dve, S("dve_chain"))
            ada_in, ada_step = [Tally(dve, S(f"ada_in{i}")) for i in range(2)], Tally(dve, S("ada_step"))
            turn = [0]
            u_done = [Tally(dve, S(f"u_ready{h}")) for h in range(2)]
            half = lambda h: slice(h * HALF, (h + 1) * HALF)

            def d_bank():
                gd.take()
                turn[0] += 1
                return bank(NA + (turn[0] - 1) % ND)

            def free(ins):
                ins.then_inc(S("d_free"), 1)
                mine.skip()

            def ada_add(out, w, k, signal=None):
                c = CS[:, k:k + 1]
                if k == 0:
                    ins = dve.tensor_scalar(out, w, c, None, ALU.mult)
                else:
                    ins = dve.scalar_tensor_tensor(out=out, in0=w, scalar=c, in1=out, op0=ALU.mult, op1=ALU.add)
                ins.then_inc(S("ada_step"), 1)
                ada_step.take()
                if k == NK - 1:
                    dve.sem_inc(S("ada_sum"), 1)

            def add_x(gate, halves=(0, 1), between=None):
                for h in halves:
                    for m in range(NK):
                        b = d_bank()
                        g = 1.0 if gate is None else MOD[:, gate, 16 + m:17 + m]
                        x = X[:, m, half(h)]
                        free(dve.scalar_tensor_tensor(out=x, in0=b, scalar=g, in1=x, op0=ALU.mult, op1=ALU.add))
                        if between is not None:
                            between(NK * h + m)

            def modulate(ug, ub, first=False):
                def rest(n):
                    h, k = divmod(n, NK)
                    uh.take()
                    dve.tensor_tensor(UL[:, k, half(h)], TU[k % 2][:, :], UH[:, k, half(h)].bitcast(F32),
                                      ALU.subtract).then_inc(S(f"u_ready{h}"), 1)
                    u_done[h].skip()

                for n in range(2 * NK):
                    h, k = divmod(n, NK)
                    x = X[:, k, half(h)]
                    u = lambda: dve.tensor_scalar(TU[k % 2][:, :], x, ug[:, k:k + 1], ub[:, k:k + 1],
                                                  ALU.mult, ALU.add).then_inc(S("tt"), 1)
                    if first:
                        dve.wait_ge(S("xt_free"), n + 1)
                        u_done[h if k > 1 else 0].wait_at(0)
                        u()
                    else:
                        if n == 6:
                            inverse(1)
                        ins = dve.tensor_tensor(x, x, RST[h][:, :], ALU.mult)
                        if k % 2 == 0:
                            ins.then_inc(S("tt"), 1)
                        else:
                            chain.done(ins)
                            u()
                    if n:
                        rest(n - 1)
                rest(2 * NK - 1)

            def centre(kt, tile_of, h):
                stat.take()
                for k in range(kt):
                    x = tile_of(k, h)
                    dve.scalar_tensor_tensor(out=x, in0=bank((6, 5)[h]), scalar=-1.0 / (kt * P), in1=x,
                                             op0=ALU.mult, op1=ALU.add).then_inc(S("cen"), 1)

            def centre_both(kt, tile_of):
                for h in range(2):
                    centre(kt, tile_of, h)

            def inverse(h):
                std.take()
                chain.done(dve.reciprocal(RST[h][:, :], RST[h][:, :]))

            def norm(ug, ub):
                mine.wait_at(0)
                centre_both(NK, lambda k, h: X[:, k, half(h)])
                inverse(0)
                modulate(ug, ub)
                x_ready.take(2 * NK)

            ts = lambda out, a, s1, s2, o0, o1=None: chain.done(
                dve.tensor_scalar(out, a, s1, s2, o0, o1) if o1 is not None else dve.tensor_scalar(out, a, s1, s2, o0))
            tt = lambda out, a, b, op: chain.done(dve.tensor_tensor(out, a, b, op))

            def ln_vectors(n, mod, alpha, bias=None, gate=None):
                g, b = (pv("ln_g", (n - 1) * NK, NK), pv("ln_b", (n - 1) * NK, NK)) if n <= 4 else \
                    (pv("ln1_g_2", 0, NK), pv("ln1_b_2", 0, NK))
                ug, ub, xg, xb, t = (vec(f"{s}{n}") for s in ("ug", "ub", "xg", "xb", "tmp"))
                if mod is not None:
                    tt(ug, g, MOD[:, mod, 8:16], ALU.mult)
                    tt(ub, b, MOD[:, mod, 8:16], ALU.mult)
                    tt(ub, ub, MOD[:, mod, 0:8], ALU.add)
                ts(xg, g, alpha, None, ALU.mult)
                ts(xb, b, alpha, None, ALU.mult)
                if bias is not None:
                    if gate is not None:
                        tt(t, bias, MOD[:, gate, 16:24], ALU.mult)
                        bias = t
                    tt(xb, xb, bias, ALU.add)
                return (ug, ub) if mod is not None else (g, b)

            def modulation(l, src, a=0, b=24):
                ad = pv("ada_b", 24 * l + a, b - a)
                tt(MOD[:, l, a:b], src, ad, ALU.add)
                lo = max(a, 8)
                ts(MOD[:, l, lo:b], MOD[:, l, lo:b], 1.0, None, ALU.add)

            dve.sem_inc(S("d_free"), ND)
            dve.sem_inc(S("h_ready"), 2)
            dve.sem_inc(S("ab_used"), 1)
            chain.done(dve.memset(BLK[:, :], 0.0))
            for i in range(2):
                ins = dve.memset(BLK[64 * i:64 * i + 64, 64 * i:64 * i + 64], 1.0)
            chain.done(ins)
            dve.wait_ge(S("consts"), 1)
            chain.done(dve.memset(MASKG[0:64, 64:128], 0.0))
            dve.wait_ge(S("lam_e"), 1)
            lam, le, ll = pv("ev_rg_lam", 0, 4), vec("le", 4), vec("ll", 4)
            u, c = vec("lu", 4), vec("lc", 4)
            ts(u, le, 1.0, None, ALU.add)
            ts(c, u, 1.0, None, ALU.subtract)
            tt(c, le, c, ALU.subtract)
            chain.done(dve.reciprocal(u, u))
            tt(c, c, u, ALU.mult)
            tt(ll, ll, c, ALU.add)
            chain.done(dve.scalar_tensor_tensor(out=ll, in0=lam, scalar=0.0, in1=ll, op0=ALU.min, op1=ALU.subtract))
            ts(vec("lam8", 4), ll, 8.0, None, ALU.mult)
            dve.tensor_scalar(vec("lam8n", 4), ll, -8.0, None, ALU.mult).then_inc(S("lam_ready"), 1)
            for k in range(NK):
                dve.wait_ge(S(f"ada0_in{k}"), 16)
                ada_add(ADSS[:, 0:2 * D], ADS[:, k, :], k)
            dve.wait_ge(S("ada_done"), 1)
            modulation(0, bank(7)[:, 0:16], 0, 16)
            modulate(MOD[:, 0, 8:16], MOD[:, 0, 0:8], first=True)
            dve.wait_ge(S("ada0_gate_in"), 16)
            for k in range(NK):
                ada_add(ADSS[:, 2 * D:3 * D], ADG[:, k, :], k)
            x_ready.take(2 * NK)
            dve.wait_ge(S("bf_in"), 16 * 5)
            dve.memset(XR[:, 0:3], 0.0)
            ts(QKG[:, 0:1], QKG[:, 0:1], 0.125, None, ALU.mult)

            def even():
                rga = Tally(dve, S("rg_a"))
                cch = Chain(dve, S("conv_chain"))

                def conv_and_gates(c):
                    pc = lambda n, j=0: PV[:, bass.ds(c + (pcol[n] + j), 1)]
                    for h in range(2):
                        af.take()
                        xc = XC[:, half(h)]
                        cch.done(dve.tensor_scalar(xc, XR[:, 3 + h * HALF:3 + h * HALF + HALF],
                                                   pc("ev_conv_w", 12), pc("ev_conv_b"), ALU.mult, ALU.add))
                        for k in range(2, -1, -1):
                            ins = dve.scalar_tensor_tensor(out=xc, in0=XR[:, k + h * HALF:k + h * HALF + HALF],
                                                           scalar=pc("ev_conv_w", 4 * k), in1=xc,
                                                           op0=ALU.mult, op1=ALU.add)
                            if k:
                                cch.done(ins)
                            else:
                                ins.then_inc(S("xc_ready"), 1)
                        af.take()

                def lru():
                    rga.take()
                    cch.done(dve.tensor_tensor(HS[:, :], AA[:, :], AA[:, :], ALU.mult))
                    dve.scalar_tensor_tensor(out=TH[:, :], in0=HS[:, :], scalar=1.0, in1=TH[:, :],
                                             op0=ALU.add, op1=ALU.mult).then_inc(S("lru"), 1)
                    af.take(4)
                    cch.done(dve.tensor_tensor(GI[:, :], GI[:, :], XC[:, :], ALU.mult))
                    rga.take()
                    cch.done(dve.tensor_tensor(GI[:, :], GI[:, :], TH[:, :], ALU.mult))
                    cch.done(dve.tensor_tensor_scan(HS[:, :], AA[:, :], GI[:, :], 0.0, ALU.mult, ALU.add))
                    dve.tensor_tensor(HS[:, :], HS[:, :], YG[:, :], ALU.mult).then_inc(S("lru"), 1)
                    rga.take()
                    dve.tensor_tensor(ML[:, :], HS[:, :], MH[:, :].bitcast(F32), ALU.subtract)\
                        .then_inc(S("m_ready"), 1)

                gd.skip(4)
                conv_and_gates(0)
                dve.wait_ge(S("ada_done"), 2)
                modulation(0, bank(7)[:, 16:24], 16, 24)
                dve.sem_inc(S("mod_ready"), 1)
                gd.skip(4)
                lru()

                def ada_steps(ks):
                    for k in ks:
                        if k % 2 == 0:
                            ada_in[k // 2 % 2].take(16)
                        ada_add(ADRS[:, :], ADR[(k // 2) % 2][:, k % 2, :], k)

                with rounds(dve, 3, (gd, 24), (mine, 16), (rga, 3), (cch, 10), (af, 8), (ada_in[0], 32), (ada_in[1], 32),
                            (ada_step, 8)) as it:
                    gd.skip(4)
                    conv_and_gates(it + 1)
                    ada_steps(range(4))
                    add_x(0)
                    ada_steps(range(4, 8))
                    gd.skip(4)
                    lru()
                add_x(0)

                exps, gmh = Tally(dve, S("exps")), Tally(dve, S("gmh"))
                gst = Tally(dve, S("gla_std"))
                chain.done(dve.memset(CHM[:, :], 1.0))
                chain.done(dve.memset(CHM[:, ::GLA_CHUNK], 0.0))
                for p in range(2):
                    if p == 0:
                        gd.skip(2)
                        af.skip(2)
                    gd.skip(14)
                    af.skip(2)
                    dve.wait_ge(S("z_ready"), p + 1)
                    chain.done(dve.scalar_tensor_tensor(out=B[0][:, :], in0=B[0][:, :], scalar=0.0, in1=B[3][:, :],
                                                        op0=ALU.min, op1=ALU.subtract))
                    for h in range(2):
                        chain.done(dve.tensor_tensor_scan(B[1][:, half(h)], CHM[:, :], B[0][:, half(h)], 0.0,
                                                          ALU.mult, ALU.add))
                    v16 = lambda t: t[:, :].rearrange("p (n s) -> p n s", s=GLA_CHUNK)
                    last = v16(B[1])[:, :, 63:64].broadcast_to([P, 16, GLA_CHUNK])
                    dve.tensor_tensor(v16(B[4]), last, v16(B[1]), ALU.subtract).then_inc(S("gl"), 1)
                    exps.take()
                    af.take(4)
                    dve.tensor_tensor(B[5][:, :], B[5][:, :], B[2][:, :], ALU.mult).then_inc(S("qk_ready"), 1)
                    dve.tensor_tensor(B[3][:, :], B[6][:, :], B[3][:, :], ALU.mult).then_inc(S("qk_ready"), 1)
                    dve.tensor_tensor(B[4][:, :], B[6][:, :], B[4][:, :], ALU.mult).then_inc(S("qk_ready"), 1)
                    for g in range(2):
                        free(dve.tensor_copy(B[6][:, half(g)], d_bank()))
                    for hh in range(2):
                        for g in range(2):
                            b = d_bank()
                            free(dve.tensor_tensor(ATT[:, hh, 4 * g:4 * g + 4, :],
                                                   b.rearrange("p (t c) -> p t c", t=4),
                                                   MASKG[:, :].unsqueeze(1).broadcast_to([P, 4, P]), ALU.mult))
                    chain.done(dve.memset(STT_[:, 0, :], 0.0))
                    for q in range(4):
                        banks = (d_bank(), d_bank())
                        for i in range(4):
                            n = 4 * q + i
                            if n == 15:
                                dve.sem_inc(S("d_free"), 1)
                                mine.skip()
                                break
                            for hh in range(2):
                                r = slice(64 * hh, 64 * hh + 64)
                                ins = dve.scalar_tensor_tensor(
                                    out=STT_[r, n + 1, :], in0=STT_[r, n, :], scalar=DEC[r, n:n + 1],
                                    in1=banks[i % 2][r, (i // 2) * 256 + hh * P:(i // 2) * 256 + (hh + 1) * P],
                                    op0=ALU.mult, op1=ALU.add)
                            if i < 2:
                                chain.done(ins)
                            else:
                                free(ins)
                                mine.wait_at(0)
                    af.skip(8)
                    gd.skip(4)
                    af.take(4)
                    gd.skip(4)
                    for hh in range(2):
                        for h in range(2):
                            af.take()
                            gst.take()
                            chain.done(dve.reciprocal(GRS[:, :], GRS[:, :]))
                            chain.done(dve.scalar_tensor_tensor(out=OO[h][:, :], in0=OO[h][:, :],
                                                                scalar=pv("ev_gla_norm_g", 2 * p + hh),
                                                                in1=B[2 + hh][:, half(h)], op0=ALU.mult, op1=ALU.mult))
                            dve.tensor_tensor(OO[h][:, :], OO[h][:, :], GRS[:, :], ALU.mult).then_inc(S("gla_o"), 1)
                            gmh.take()
                            dve.tensor_tensor(GML[hh][:, half(h)], OO[h][:, :], GMH[hh][:, half(h)].bitcast(F32),
                                              ALU.subtract).then_inc(S("m_ready"), 1)
                    add_x(0)
                    add_x(0)

            hh_ready = Tally(dve, S("hh_ready"))

            def mlp(l, gate):
                def ada_between(i):
                    if l == 0 and i % 2 and i < 8:
                        k = 4 * turn_q[0] + i // 2
                        ada_in[k % 2].take(16)
                        ada_add(ADMS[:, :, :], ADM[k % 2][:, :, :], k)

                turn_q = [0]
                ada = [(ada_in[0], 64), (ada_in[1], 64), (ada_step, 8)] if l == 0 else []
                with rounds(dve, 8, (gd, 40), (mine, 32), (hh_ready, 8), *ada) as it:
                    for q in range(2):
                        gd.skip(4)
                        for h in range(2):
                            for m in range(2):
                                hh_ready.take()
                                dve.tensor_tensor(HL[:, m, half(h)], SQ[(2 * h + m) % 2][:, :],
                                                  HH[:, m, half(h)].bitcast(F32), ALU.subtract)\
                                    .then_inc(S("h_ready"), 1)
                        turn_q[0] = q
                        add_x(gate, between=ada_between)
                af.skip(64)

            def odd():
                dve.wait_ge(S("fe_ready"), 1)
                chain.done(dve.scalar_tensor_tensor(out=FE[:, :], in0=FC[:, :], scalar=0.0, in1=FE[:, :],
                                                    op0=ALU.min, op1=ALU.subtract))
                dve.tensor_tensor_scan(FC[:, :], ONES[0:16, 0:1].broadcast_to([16, SEQ]), FE[:, :], 0.0,
                                       ALU.mult, ALU.subtract).then_inc(S("fc_ready"), 1)
                gd.skip(2)
                qst, qkh = Tally(dve, S("q_std")), Tally(dve, S("qkh"))
                nf = Tally(dve, S("nf_in"))
                sd, sf = Tally(dve, S("s_done")), Tally(dve, S("s_free"))
                pt4, pt5 = Tally(dve, S("pt4_done")), Tally(dve, S("pt5_done"))
                od = Tally(dve, S("o_done"), 2)
                oth = Tally(dve, S("oth"))
                och = Chain(dve, S("odd_chain"))
                with rounds(dve, 8, (gd, 28), (mine, 16), (qst, 4), (qkh, 4), (nf, 32), (sd, 16), (sf, 16), (pt4, 16),
                            (pt5, 8), (od, 16), (oth, 2), (och, 20)) as it:
                    for h in range(2):
                        for m, (th, tl) in enumerate(((QH, QL), (KH, KL))):
                            t = QT[2 * h + m]
                            rs = QRS[m][:, :]
                            qst.take()
                            och.done(dve.reciprocal(rs, rs))
                            dve.scalar_tensor_tensor(out=t[:, :], in0=t[:, :], scalar=QKG[:, m:m + 1],
                                                     in1=rs, op0=ALU.mult, op1=ALU.mult)\
                                .then_inc(S("qn_done"), 1)
                            qkh.take()
                            dve.tensor_tensor(tl[:, half(h)], t[:, :], th[:, half(h)].bitcast(F32),
                                              ALU.subtract).then_inc(S("qkn_ready"), 1)
                    nf.take(32)
                    gd.skip(12)

                    def scores(n):
                        hh, tb = n // NT, n % NT
                        w = (tb + 1) * P
                        b = 2 * (n % 2)
                        sd.take()
                        dve.sem_inc(S("ttr_turn"), 1)
                        dve.tensor_tensor_reduce(out=PR[n % 2][:, 0:w], in0=PS[:, b * HALF:b * HALF + w],
                                                 in1=NF[:, hh, 0:w], scale=1.0, scalar=-3.0e38, op0=ALU.add,
                                                 op1=ALU.max, accum_out=MXT[:, n:n + 1]).then_inc(S("s_free"), 1)
                        sf.take()
                        dve.tensor_scalar(NMX[:, n:n + 1], MXT[:, n:n + 1], -1.0, None, ALU.mult)\
                            .then_inc(S("p_ready"), 1)

                    def output(n):
                        hh, tb = n // NT, n % NT
                        od.take()
                        och.done(dve.reciprocal(RINV[:, n:n + 1], RSUM[:, n:n + 1]))
                        g = G[:, tb, 64 * hh:64 * hh + 64]
                        dve.scalar_tensor_tensor(out=g, in0=bank(6 + n % 2, 64), scalar=RINV[:, n:n + 1],
                                                 in1=g, op0=ALU.mult, op1=ALU.mult).then_inc(S("o_free"), 1)

                    scores(0)
                    scores(1)
                    for n in range(2 * NT):
                        hh, tb = n // NT, n % NT
                        w = (tb + 1) * P
                        pt4.take()
                        if tb >= 4:
                            pt5.take()
                            dve.tensor_copy(PT[n % 2][:, HALF:w], PS[:, 5 * HALF:5 * HALF + w - HALF])\
                                .then_inc(S("pt_d"), 1)
                        if n + 2 < 2 * NT:
                            scores(n + 2)
                        if n:
                            output(n - 1)
                    output(2 * NT - 1)
                    for g in range(2):
                        oth.take()
                        dve.tensor_tensor(QL[:, half(g)], PR[0][:, half(g)], QH[:, half(g)].bitcast(F32),
                                          ALU.subtract).then_inc(S("ot_ready"), 1)
                    add_x(2)
                af.skip(2 + 8 * 12)

            def spatial():
                dve.wait_ge(S("wst_done"), 1)
                dve.wait_ge(S("sp_in"), 16 * 4)
                chain.done(dve.tensor_tensor(WST[:, :, :], bank(6).rearrange("p (h t) -> p h t", h=4),
                                             MASKC[:, :].unsqueeze(1).broadcast_to([P, 4, P]), ALU.mult))
                gd.skip(16)
                for p in range(2):
                    for t in range(NT):
                        af.take()
                        for e in range(2):
                            hh = 2 * p + e
                            ins = dve.bn_stats(BST[:, 4 * t + hh, :], VS[:, t, hh * P:(hh + 1) * P])
                chain.done(ins)
                for j in range(32):
                    ins = dve.bn_aggr(MV[:, j, :], BST[:, j, :])
                ins.then_inc(S("va_var"), 1)
                dve.wait_ge(S("va_std"), 1)
                chain.done(dve.reciprocal(VR[:, :], VR[:, :]))
                for j in range(32):
                    v = VS[:, j // 4, (j % 4) * P:(j % 4 + 1) * P]
                    ins = dve.tensor_scalar(v, v, MV[:, j, 0:1], VR[:, j:j + 1], ALU.subtract, ALU.mult)
                chain.done(ins)
                g = lambda t: t[:, :].unsqueeze(1).broadcast_to([P, NT, 512])
                chain.done(dve.tensor_tensor(VS[:, :, :], VS[:, :, :], g(LAG), ALU.mult))
                chain.done(dve.tensor_tensor(VS[:, :, :], VS[:, :, :], g(LAB), ALU.add))
                dve.sem_inc(S("ab_used"), 1)
                dve.memset(YB[:, 0:CONV_PAD], 0.0)
                dve.wait_ge(S("bs_in"), 16)
                smh = Tally(dve, S("smh"))
                sch = Chain(dve, S("sp_chain"))
                cp = Tally(dve, S("cp_ready"), 1)
                with rounds(dve, 4, (gd, 24), (mine, 16), (af, 8), (smh, 2), (cp, 1),
                            (sch, 3 + CONV_PAD - POOL_TAPS)) as it:
                    for h in range(2):
                        af.take(2)
                        dve.tensor_tensor(YB[:, CONV_PAD + h * HALF:CONV_PAD + (h + 1) * HALF], AB[h][:, :], GB[h][:, :],
                                          ALU.mult).then_inc(S("ab_used"), 1)
                    gd.skip(8)
                    for h in range(2):
                        af.take()
                        t4 = TY[h][:, :].rearrange("p (c t) -> p c t", c=4)
                        sch.done(dve.tensor_tensor(t4, t4, BS[:, bass.ds(it, 1), :].broadcast_to([P, 4, P]), ALU.add))
                    for h in range(2):
                        af.take()
                        dve.tensor_tensor(TY[h][:, :], TY[h][:, :], UU[:, half(h)], ALU.mult)\
                            .then_inc(S("ty_ready"), 1)
                    for h in range(2):
                        smh.take()
                        dve.tensor_tensor(SML[:, half(h)], TY[h][:, :], SMH[:, half(h)].bitcast(F32),
                                          ALU.subtract).then_inc(S("sm_ready"), 1)
                    add_x(None)
                    cx = CX[:, bass.ds(it, 1), :].rearrange("p a n -> p (a n)")
                    pc = lambda n, j=0: PV[:, bass.ds(it + (pcol[n] + j), 1)]
                    sch.done(dve.tensor_scalar(cx, YB[:, CONV_PAD:CONV_PAD + SEQ], pc("conv_b_w_2", 4 * CONV_PAD),
                                               pc("conv_b_b_2"), ALU.mult, ALU.add))
                    for k in range(POOL_TAPS, CONV_PAD):
                        ins = dve.scalar_tensor_tensor(out=cx, in0=YB[:, k:k + SEQ], scalar=pc("conv_b_w_2", 4 * k),
                                                       in1=cx, op0=ALU.mult, op1=ALU.add)
                        sch.done(ins)
                    cp.take()
                    dve.tensor_tensor(cx, cx, CP[:, :], ALU.add).then_inc(S("cx_ready"), 1)
                dve.wait_ge(S("cx_ready"), 4)
                centre_both(4, lambda k, h: CX[:, k, half(h)])
                for h in range(2):
                    inverse(h)
                    for k in range(4):
                        c = CX[:, k, half(h)]
                        dve.tensor_tensor(c, c, RST[h][:, :], ALU.mult).then_inc(S("cx_norm"), 1)
                with rounds(dve, 4, (gd, 16), (mine, 16), (smh, 2)) as it:
                    for h in range(2):
                        smh.take()
                        dve.tensor_tensor(SML[:, half(h)], TY[h][:, :], SMH[:, half(h)].bitcast(F32),
                                          ALU.subtract).then_inc(S("sm_ready"), 1)
                    add_x(None)

            def ffn():
                for m in range(4):
                    ins = dve.memset(FZ[:, m, 0:2], 0.0)
                chain.done(ins)
                silu, fh = Tally(dve, S("silu")), Tally(dve, S("fh"))
                fch = Chain(dve, S("ffn_chain"))
                conv = Tally(dve, S("conv_ready"))
                with rounds(dve, D_FF2 // 256, (gd, 24), (conv, 8), (mine, 16), (af, 8), (silu, 4), (fh, 4), (fch, 16)) as it:
                    for h in range(2):
                        for m in range(4):
                            af.take()
                            w = lambda r: PV[:, bass.ds(it * 2 + (pcol["conv_f_w_2"] + 44 * r + (m if m < 2 else 20 + m)), 1)]
                            y = FY[:, m, :]
                            fch.done(dve.scalar_tensor_tensor(out=y, in0=FZ[:, m, 1:1 + HALF], scalar=w(1), in1=y,
                                                              op0=ALU.mult, op1=ALU.add))
                            dve.scalar_tensor_tensor(out=y, in0=FZ[:, m, 0:HALF], scalar=w(0), in1=y,
                                                     op0=ALU.mult, op1=ALU.add).then_inc(S("conv_ready"), 1)
                            conv.take()
                            if h == 0:
                                fch.done(dve.tensor_copy(FZ[:, m, 0:2], FZ[:, m, HALF:HALF + 2]))
                            else:
                                fch.done(dve.memset(FZ[:, m, 0:2], 0.0))
                        for m in range(2):
                            silu.take()
                            dve.tensor_tensor(FY[:, m, :], FY[:, m, :], FY[:, 2 + m, :], ALU.mult)\
                                .then_inc(S("prod_ready"), 1)
                        for m in range(2):
                            fh.take()
                            dve.tensor_tensor(FL[:, m, half(h)], FY[:, m, :], FH[:, m, half(h)].bitcast(F32),
                                              ALU.subtract).then_inc(S("h_ready"), 1)
                    gd.skip(8)
                    add_x(None)

            even()
            dve.wait_ge(S("ada_done"), 2 + 3)
            modulation(1, bank(7)[:, 0:24])
            dve.sem_inc(S("mod_ready"), 1)
            norm(*ln_vectors(1, 1, ALPHA_1, pv("mlp_b2", 0, NK), 1))
            mlp(0, 1)
            dve.wait_ge(S("ada_done"), 2 + 3 + 8)
            modulation(2, bank(7)[:, 0:24])
            modulation(3, bank(7)[:, 24:48])
            dve.sem_inc(S("mod_ready"), 1)
            norm(*ln_vectors(2, 2, ALPHA_1))
            odd()
            norm(*ln_vectors(3, 3, ALPHA_1, pv("mlp_b2", NK, NK), 3))
            mlp(1, 3)
            norm(*ln_vectors(4, None, ALPHA_2, pv("b_out_2", 0, NK)))
            spatial()
            norm(*ln_vectors(5, None, ALPHA_2))
            ffn()
            mine.wait_at(0)
            centre_both(NK, lambda k, h: X[:, k, half(h)])
            for h in range(2):
                inverse(h)
                for k in range(NK):
                    x = X[:, k, half(h)]
                    dve.tensor_tensor(x, x, RST[h][:, :], ALU.mult).then_inc(S("xn"), 1)

        @block.sync
        def _(sp):
            xin = A["x"].rearrange("a (t p) d -> p (a t) d", p=P)
            for h in range(2):
                sp.dma_start(XIN[:, 4 * h:4 * h + 4, :], xin[:, 4 * h:4 * h + 4, :]).then_inc(S(f"x_in{h}"), 16)
            sp.wait_ge(S("prow_zero"), 1)
            for n, ap in prow.items():
                done = 0
                while done < ap.shape[0]:
                    r = pcol[n] + done
                    k = min(ap.shape[0] - done, P - r % P)
                    sp.dma_start(PROW[r % P:r % P + k, r // P, :], ap[done:done + k, :]).then_inc(S("prow_in"), 16)
                    done += k
            ada = A["ada_w"][0, 0].rearrange("(k p) m -> p k m", p=P)
            for k in range(NK):
                sp.dma_start(ADS[:, k, :], ada[:, k, 0:2 * D]).then_inc(S(f"ada0_in{k}"), 16)
            ready = S("w_ready")
            for ph in plan.order:
                T = len(ph["tiles"])

                def load(it):
                    for j, (src, _, _) in enumerate(ph["tiles"]):
                        v = ph["W"] + ph["raws"][j]
                        if ph["count"] > 1:
                            assert v > 0
                            sp.wait_ge(ready, it * T + v)
                        elif v > 0:
                            sp.wait_ge(ready, v)
                        sp.sem_inc(S("load_turn"), 1)
                        for dst, ap in src(it, RAW[j % NRAW]):
                            sp.dma_start(dst, ap).then_inc(S(f"raw_in{j % NRAW}"), 16)

                if ph["count"] > 1:
                    with sp.Fori(0, ph["count"]) as it:
                        load(it)
                else:
                    load(0)
            orow = out.rearrange("a (t p) d -> (a t) p d", p=P)
            for t in range(NT):
                sp.wait_ge(S("yo_ready"), 2 * t + 2)
                sp.dma_start(orow[t], YO[t % 2][:, :]).then_inc(S(f"out_done{t % 2}"), 16)
            for i in range(2):
                sp.wait_ge(S(f"out_done{i}"), 16 * NT // 2)

        @block.gpsimd
        def _(pool):
            chain = Chain(pool, S("pool_chain"))
            pool.memset(PROW[:, n_ptile - 1, :], 0.0).then_inc(S("prow_zero"), 1)
            for t, v in ((IDENT, 0.0), (ONES, 1.0), (MASKC, 1.0), (MASKG, 1.0), (MASKA, 0.0),
                         (EPSL, LN_EPS), (EPSR, RMS_EPS), (WGA, 0.0), (WGX, 0.0)):
                ins = pool.memset(t[:, :], v)
            chain.done(ins)
            ins = pool.affine_select(out=IDENT[:, :], in_=IDENT[:, :], compare_op=ALU.not_equal, fill=1.0, base=0,
                                     pattern=[[-1, P]], channel_multiplier=1)
            ins = pool.affine_select(out=MASKC[:, :], in_=MASKC[:, :], compare_op=ALU.is_ge, fill=0.0, base=0,
                                     pattern=[[1, P]], channel_multiplier=-1)
            ins = pool.affine_select(out=MASKA[:, :], in_=MASKA[:, :], compare_op=ALU.is_ge, fill=NEG, base=0,
                                     pattern=[[-1, P]], channel_multiplier=1)
            pool.affine_select(out=MASKG[:, :], in_=MASKG[:, :], compare_op=ALU.is_ge, fill=0.0, base=0,
                               pattern=[[1, P]], channel_multiplier=-1).then_inc(S("consts"), 1)

            pool.sem_inc(S("cp_ready"), 1)

            yb, cx, cp = Tally(pool, S("ab_used"), 2), Tally(pool, S("cx_ready")), Chain(pool, S("pool_taps"))

            def long_conv(first):
                if not first:
                    cx.take()
                yb.take(2)
                pool.wait_ge(S("vh_ready"), 1) if first else vh.take()
                for k in range(POOL_TAPS):
                    for h in range(2):
                        y = YB[:, k + h * HALF:k + (h + 1) * HALF]
                        c = CP[:, h * HALF:(h + 1) * HALF]
                        pool.sem_inc(S("tap_turn"), 1)
                        cp.done(pool.tensor_scalar(TP[:, :] if k else c, y, TW[:, k:k + 1], None, ALU.mult))
                        if k:
                            cp.done(pool.tensor_tensor(c, c, TP[:, :], ALU.add))
                pool.sem_inc(S("cp_ready"), 1)

            vh = Tally(pool, S("vh_ready"), 1)
            norms = {"mlp0": 1, "odd": 2, "mlp1": 3, "sv": 4, "ffn": 5}
            uh = Tally(pool, S("uh"), 2 * NK)

            def scale_x(n):
                for h in range(2):
                    for k in range(NK):
                        uh.take()
                        x = X[:, k, h * HALF:(h + 1) * HALF]
                        pool.tensor_scalar(x, x, vec(f"xg{n}")[:, k:k + 1], vec(f"xb{n}")[:, k:k + 1],
                                           ALU.mult, ALU.add).then_inc(S("x_ready"), 1)

            raw = [Tally(pool, S(f"raw_in{i}")) for i in range(NRAW)]
            hi = Tally(pool, S("w_hi"))
            for ph in plan.order:
                T = len(ph["tiles"])

                def split(it, free):
                    for j, (src, _, slot) in enumerate(ph["tiles"]):
                        if it is None and j == 4 and ph["name"] in norms:
                            scale_x(norms[ph["name"]])
                        r = RAW[j % NRAW]
                        parts = src(0, r)
                        raw[j % NRAW].take(16 * len(parts))
                        v = ph["I"] + free[j]
                        if it is not None:
                            pool.wait_ge(S("gemm_done"), it * ph["items"] + (v + ph["items"]))
                        elif v > 0:
                            pool.wait_ge(S("gemm_done"), v)
                        pool.sem_inc(S("split_turn"), 1)
                        n = sum(int(np.prod(d.shape[1:])) for d, _ in parts)
                        pool.tensor_scalar(WH[slot][:, 0:n], r[:, 0:n], 1.0, None, ALU.mult).then_inc(S("w_hi"), 1)
                        hi.take()
                        pool.tensor_tensor(WL[slot][:, 0:n], r[:, 0:n], WH[slot][:, 0:n].bitcast(F32),
                                           ALU.subtract).then_inc(ready, 1)

                ready = S("w_ready")
                split(None, ph["first"])
                if T == 4 and ph["name"] in norms:
                    scale_x(norms[ph["name"]])
                conv = ph["name"] == "mix"
                if conv:
                    long_conv(True)
                if ph["count"] > 1:
                    per = [16 * sum(len(t[0](0, RAW[0])) for j, t in enumerate(ph["tiles"]) if j % NRAW == i)
                           for i in range(NRAW)]
                    pairs = [(raw[i], per[i]) for i in range(NRAW) if per[i]] + [(hi, T)]
                    if conv:
                        pairs += [(yb, 2), (cx, 1), (cp, 4 * POOL_TAPS - 2), (vh, 1)]
                    with rounds(pool, ph["count"] - 1, *pairs) as it:
                        split(it, ph["free"])
                        if conv:
                            long_conv(False)


_INS = ["x", "c", "ada_w", "ada_b", "ln_g", "ln_b", "ev_w_in", "ev_conv_w", "ev_conv_b", "ev_rg_wa", "ev_rg_ba",
        "ev_rg_wx", "ev_rg_bx", "ev_rg_lam", "ev_gla_w_up", "ev_gla_b_up", "ev_gla_norm_g", "ev_w_out", "od_w_in",
        "od_b_f", "od_q_norm_g", "od_k_norm_g", "od_w_out", "mlp_w1", "mlp_b1", "mlp_w2", "mlp_b2", "w_in_2", "b_in_2",
        "ln_a_g_2", "ln_a_b_2", "w_spatial_2", "b_spatial_2", "conv_b_w_2", "conv_b_b_2", "ln_b_g_2", "ln_b_b_2",
        "w_out_2", "b_out_2", "ln1_g_2", "ln1_b_2", "w_up_2", "conv_f_w_2", "conv_f_b_2", "w_down_2", "ln2_g_2",
        "ln2_b_2"]
_OUTS = [((1, 1024, 1024), "float32")]


def kernel(**inputs):
    import numpy as _np
    import concourse.bacc as _bacc
    from concourse import mybir as _mybir
    from concourse.bass_utils import run_bass_kernel_spmd as _run

    nc = _bacc.Bacc("TRN2", target_bir_lowering=False, num_devices=1)
    arrays, aps = {}, {}
    for name in _INS:
        a = _np.ascontiguousarray(inputs[name])
        arrays[f"in_{name}_dram"] = a
        aps[name] = nc.dram_tensor(f"in_{name}_dram", a.shape, _mybir.dt.from_np(a.dtype), kind="ExternalInput").ap()
    shape, dtype = _OUTS[0]
    out = nc.dram_tensor("out_0_dram", shape, _mybir.dt.from_np(_np.dtype(dtype)), kind="ExternalOutput").ap()
    build(nc, aps, out)
    r = _run(nc, [arrays], core_ids=[0])
    return _np.array(r.results[0]["out_0_dram"])
```
